# Optimizing a Trainium2 kernel written in Bass

```python
import math, functools
import jax, jax.numpy as jnp
from jax import lax
import numpy as np

D_MODEL = 1024
BATCH = 1
SEQ = 256
DEPTH = 4

N_MIXERS = 3
MEM_LEN = 256
BLOCK = 128
ROPE_THETA = 10000.0
NEG = -1e30
LN_EPS = 1e-5
RMS_EPS = 1e-6

A_HEADS = 16
A_KV_HEADS = 4
A_HEAD_DIM = 64
A_WINDOW = 128

LRU_WIDTH = D_MODEL
LRU_BLOCKS = 4
LRU_BLOCK_W = LRU_WIDTH // LRU_BLOCKS
LRU_CONV = 4
LRU_C = 8.0

C_HEADS = 8
C_NOPE = 128
C_ROPE = 64
C_V = 128
C_Q_RANK = 384
C_KV_RANK = 256

X_HEADS = 4
X_HEAD_DIM = D_MODEL // X_HEADS

D_FF = 2816
FFN_CONV = 3

ALPHA = (2.0 * DEPTH) ** 0.25
BETA = (8.0 * DEPTH) ** -0.25

N_A = (DEPTH + 2) // 3
N_B = (DEPTH + 1) // 3
N_C = DEPTH // 3


def layer_norm(x, g, b):
    xf = x.astype(jnp.float32)
    mu = jnp.mean(xf, axis=-1, keepdims=True)
    var = jnp.mean(jnp.square(xf - mu), axis=-1, keepdims=True)
    y = (xf - mu) * lax.rsqrt(var + LN_EPS) * g.astype(jnp.float32) + b.astype(jnp.float32)
    return y.astype(x.dtype)

def rms_norm(x, g):
    xf = x.astype(jnp.float32)
    y = xf * lax.rsqrt(jnp.mean(jnp.square(xf), axis=-1, keepdims=True) + RMS_EPS)
    return (y * g.astype(jnp.float32)).astype(x.dtype)

def rope_tables(seq, dim):
    inv = 1.0 / (ROPE_THETA ** (jnp.arange(0, dim, 2, dtype=jnp.float32) / dim))
    ang = jnp.arange(seq, dtype=jnp.float32)[:, None] * inv[None, :]
    return jnp.cos(ang), jnp.sin(ang)

def apply_rope(x, cos, sin):
    c = cos[None, :, None, :].astype(x.dtype)
    s = sin[None, :, None, :].astype(x.dtype)
    x1, x2 = jnp.split(x, 2, axis=-1)
    return jnp.concatenate([x1 * c - x2 * s, x2 * c + x1 * s], axis=-1)

def causal_depthwise_conv(x, w, b):
    k_width = w.shape[0]
    s = x.shape[1]
    xp = jnp.pad(x, ((0, 0), (k_width - 1, 0), (0, 0)))
    y = xp[:, 0:s] * w[0]
    for k in range(1, k_width):
        y = y + xp[:, k:k + s] * w[k]
    return y + b

def swa_sink_attention(x, w_qkv, sinks, w_o, cos, sin):
    bsz, s, _ = x.shape
    grp = A_HEADS // A_KV_HEADS
    nb = s // BLOCK
    qkv = x @ w_qkv
    q, k, v = jnp.split(qkv, [A_HEADS * A_HEAD_DIM, (A_HEADS + A_KV_HEADS) * A_HEAD_DIM], axis=-1)
    q = apply_rope(q.reshape(bsz, s, A_HEADS, A_HEAD_DIM), cos, sin)
    k = apply_rope(k.reshape(bsz, s, A_KV_HEADS, A_HEAD_DIM), cos, sin)
    v = v.reshape(bsz, s, A_KV_HEADS, A_HEAD_DIM)
    qb = q.reshape(bsz, nb, BLOCK, A_KV_HEADS, grp, A_HEAD_DIM)

    def with_prev(t):
        tb = t.reshape(bsz, nb, BLOCK, A_KV_HEADS, A_HEAD_DIM)
        prev = jnp.pad(tb[:, :-1], ((0, 0), (1, 0), (0, 0), (0, 0), (0, 0)))
        return jnp.concatenate([prev, tb], axis=2)

    kb, vb = with_prev(k), with_prev(v)
    scores = jnp.einsum('bnqhgd,bnkhd->bnhgqk', qb, kb).astype(jnp.float32) * (A_HEAD_DIM ** -0.5)
    qi = jnp.arange(BLOCK)[:, None]
    kj = jnp.arange(2 * BLOCK)[None, :]
    dist = qi + BLOCK - kj
    band = (dist >= 0) & (dist < A_WINDOW)
    real_key = (jnp.arange(nb)[:, None, None] > 0) | (kj >= BLOCK)[None]
    valid = band[None] & real_key
    scores = jnp.where(valid[None, :, None, None], scores, NEG)
    sink = sinks.astype(jnp.float32).reshape(A_KV_HEADS, grp)[None, None, :, :, None, None]
    sink = jnp.broadcast_to(sink, scores.shape[:-1] + (1,))
    probs = jax.nn.softmax(jnp.concatenate([scores, sink], axis=-1), axis=-1)[..., :-1]
    out = jnp.einsum('bnhgqk,bnkhd->bnqhgd', probs.astype(v.dtype), vb)
    return out.reshape(bsz, s, A_HEADS * A_HEAD_DIM) @ w_o

def rglru_block(x, w_in, conv_w, conv_b, w_rgate, b_rgate, w_igate, b_igate, lam, w_o):
    bsz, s, _ = x.shape
    gate, u = jnp.split(x @ w_in, 2, axis=-1)
    u = causal_depthwise_conv(u, conv_w, conv_b)
    ub = u.reshape(bsz, s, LRU_BLOCKS, LRU_BLOCK_W)
    r = jax.nn.sigmoid(jnp.einsum('bshi,hij->bshj', ub, w_rgate).reshape(bsz, s, LRU_WIDTH) + b_rgate)
    i = jax.nn.sigmoid(jnp.einsum('bshi,hij->bshj', ub, w_igate).reshape(bsz, s, LRU_WIDTH) + b_igate)
    log_a = -LRU_C * r.astype(jnp.float32) * jax.nn.softplus(-lam.astype(jnp.float32))
    a = jnp.exp(log_a)
    b_in = jnp.sqrt(-jnp.expm1(2.0 * log_a)) * (i * u).astype(jnp.float32)

    def combine(c1, c2):
        a1, b1 = c1
        a2, b2 = c2
        return a1 * a2, a2 * b1 + b2

    _, h = lax.associative_scan(combine, (a, b_in), axis=1)
    y = h.astype(x.dtype) * jax.nn.gelu(gate)
    return y @ w_o

def mla_attention(x, w_down, q_norm, kv_norm, w_uq, w_ukv, w_o, cos_r, sin_r):
    bsz, s, _ = x.shape
    nb = s // BLOCK
    c = x @ w_down
    cq, ckv, k_rope = jnp.split(c, [C_Q_RANK, C_Q_RANK + C_KV_RANK], axis=-1)
    cq = rms_norm(cq, q_norm)
    ckv = rms_norm(ckv, kv_norm)
    q = (cq @ w_uq).reshape(bsz, s, C_HEADS, C_NOPE + C_ROPE)
    q_nope, q_rope = jnp.split(q, [C_NOPE], axis=-1)
    q_rope = apply_rope(q_rope, cos_r, sin_r)
    k_rope = apply_rope(k_rope[:, :, None, :], cos_r, sin_r)[:, :, 0]
    kv = (ckv @ w_ukv).reshape(bsz, s, C_HEADS, C_NOPE + C_V)
    k_nope, v = jnp.split(kv, [C_NOPE], axis=-1)
    scale = (C_NOPE + C_ROPE) ** -0.5
    qn = q_nope.reshape(bsz, nb, BLOCK, C_HEADS, C_NOPE).transpose(1, 0, 2, 3, 4)
    qr = q_rope.reshape(bsz, nb, BLOCK, C_HEADS, C_ROPE).transpose(1, 0, 2, 3, 4)
    key_pos = jnp.arange(s)

    def attend(args):
        n, qn_b, qr_b = args
        sc = (jnp.einsum('bqhd,bkhd->bhqk', qn_b, k_nope)
              + jnp.einsum('bqhd,bkd->bhqk', qr_b, k_rope)).astype(jnp.float32) * scale
        q_pos = n * BLOCK + jnp.arange(BLOCK)
        sc = jnp.where(key_pos[None, :] <= q_pos[:, None], sc, NEG)
        p = jax.nn.softmax(sc, axis=-1)
        return jnp.einsum('bhqk,bkhd->bqhd', p.astype(v.dtype), v)

    out = lax.map(attend, (jnp.arange(nb), qn, qr))
    out = out.transpose(1, 0, 2, 3, 4).reshape(bsz, s, C_HEADS * C_V)
    return out @ w_o

def memory_cross_attention(x, mem_k, mem_v, w_q, w_o):
    bsz, s, _ = x.shape
    q = (x @ w_q).reshape(bsz, s, X_HEADS, X_HEAD_DIM)
    sc = jnp.einsum('bshd,bmhd->bhsm', q, mem_k).astype(jnp.float32) * (X_HEAD_DIM ** -0.5)
    p = jax.nn.softmax(sc, axis=-1)
    o = jnp.einsum('bhsm,bmhd->bshd', p.astype(mem_v.dtype), mem_v).reshape(bsz, s, D_MODEL)
    return o @ w_o

def conv_glu_ffn(x, w_up, conv_w, conv_b, w_down):
    h = causal_depthwise_conv(x @ w_up, conv_w, conv_b)
    g, u = jnp.split(h, 2, axis=-1)
    return (jax.nn.silu(g) * u) @ w_down

def first_inputs(seed: int = 0) -> dict:
    key = jax.random.key(seed)
    ks = iter(jax.random.split(key, 40))

    def dense(shape, fan_in, scale=1.0):
        return jax.random.normal(next(ks), shape, jnp.float32) * (scale * fan_in ** -0.5)

    def small(shape, scale=0.01):
        return jax.random.normal(next(ks), shape, jnp.float32) * scale

    def gain(shape):
        return 1.0 + small(shape)

    qkv_w = (A_HEADS + 2 * A_KV_HEADS) * A_HEAD_DIM
    a0 = jax.random.uniform(next(ks), (N_B, LRU_WIDTH), jnp.float32, 0.9, 0.999) ** (1.0 / LRU_C)
    return {
        "x": jax.random.normal(next(ks), (BATCH, SEQ, D_MODEL), jnp.float32),
        "mem": jax.random.normal(next(ks), (BATCH, MEM_LEN, D_MODEL), jnp.float32),
        "a_w_qkv": dense((N_A, D_MODEL, qkv_w), D_MODEL),
        "a_sinks": small((N_A, A_HEADS), 1.0),
        "a_w_o": dense((N_A, A_HEADS * A_HEAD_DIM, D_MODEL), A_HEADS * A_HEAD_DIM, BETA),
        "b_w_in": dense((N_B, D_MODEL, 2 * LRU_WIDTH), D_MODEL),
        "b_conv_w": dense((N_B, LRU_CONV, LRU_WIDTH), LRU_CONV),
        "b_conv_b": small((N_B, LRU_WIDTH)),
        "b_w_rgate": dense((N_B, LRU_BLOCKS, LRU_BLOCK_W, LRU_BLOCK_W), LRU_BLOCK_W),
        "b_b_rgate": small((N_B, LRU_WIDTH)),
        "b_w_igate": dense((N_B, LRU_BLOCKS, LRU_BLOCK_W, LRU_BLOCK_W), LRU_BLOCK_W),
        "b_b_igate": small((N_B, LRU_WIDTH)),
        "b_lambda": jnp.log(a0) - jnp.log1p(-a0),
        "b_w_o": dense((N_B, LRU_WIDTH, D_MODEL), LRU_WIDTH, BETA),
        "c_w_down": dense((N_C, D_MODEL, C_Q_RANK + C_KV_RANK + C_ROPE), D_MODEL),
        "c_q_norm": gain((N_C, C_Q_RANK)),
        "c_kv_norm": gain((N_C, C_KV_RANK)),
        "c_w_uq": dense((N_C, C_Q_RANK, C_HEADS * (C_NOPE + C_ROPE)), C_Q_RANK),
        "c_w_ukv": dense((N_C, C_KV_RANK, C_HEADS * (C_NOPE + C_V)), C_KV_RANK),
        "c_w_o": dense((N_C, C_HEADS * C_V, D_MODEL), C_HEADS * C_V, BETA),
        "mem_w_kv": dense((D_MODEL, 2 * D_MODEL), D_MODEL),
        "x_w_q": dense((DEPTH, D_MODEL, D_MODEL), D_MODEL),
        "x_w_o": dense((DEPTH, D_MODEL, D_MODEL), D_MODEL, BETA),
        "f_w_up": dense((DEPTH, D_MODEL, 2 * D_FF), D_MODEL),
        "f_conv_w": dense((DEPTH, FFN_CONV, 2 * D_FF), FFN_CONV),
        "f_conv_b": small((DEPTH, 2 * D_FF)),
        "f_w_down": dense((DEPTH, D_FF, D_MODEL), D_FF, BETA),
        "ln_g": gain((DEPTH, 3, D_MODEL)),
        "ln_b": small((DEPTH, 3, D_MODEL)),
    }

def first_block(x, mem, a_w_qkv, a_sinks, a_w_o, b_w_in, b_conv_w, b_conv_b, b_w_rgate, b_b_rgate,
              b_w_igate, b_b_igate, b_lambda, b_w_o, c_w_down, c_q_norm, c_kv_norm, c_w_uq, c_w_ukv,
              c_w_o, mem_w_kv, x_w_q, x_w_o, f_w_up, f_conv_w, f_conv_b, f_w_down, ln_g, ln_b):
    bsz, s, _ = x.shape
    cos_a, sin_a = rope_tables(s, A_HEAD_DIM)
    cos_c, sin_c = rope_tables(s, C_ROPE)
    mem_k, mem_v = jnp.split(mem @ mem_w_kv, 2, axis=-1)
    mem_k = mem_k.reshape(bsz, MEM_LEN, X_HEADS, X_HEAD_DIM)
    mem_v = mem_v.reshape(bsz, MEM_LEN, X_HEADS, X_HEAD_DIM)
    for i in range(DEPTH):
        kind, j = i % N_MIXERS, i // N_MIXERS
        if kind == 0:
            y = swa_sink_attention(x, a_w_qkv[j], a_sinks[j], a_w_o[j], cos_a, sin_a)
        elif kind == 1:
            y = rglru_block(x, b_w_in[j], b_conv_w[j], b_conv_b[j], b_w_rgate[j], b_b_rgate[j],
                            b_w_igate[j], b_b_igate[j], b_lambda[j], b_w_o[j])
        else:
            y = mla_attention(x, c_w_down[j], c_q_norm[j], c_kv_norm[j], c_w_uq[j], c_w_ukv[j],
                              c_w_o[j], cos_c, sin_c)
        x = layer_norm(ALPHA * x + y, ln_g[i, 0], ln_b[i, 0])
        x = layer_norm(ALPHA * x + memory_cross_attention(x, mem_k, mem_v, x_w_q[i], x_w_o[i]),
                       ln_g[i, 1], ln_b[i, 1])
        x = layer_norm(ALPHA * x + conv_glu_ffn(x, f_w_up[i], f_conv_w[i], f_conv_b[i], f_w_down[i]),
                       ln_g[i, 2], ln_b[i, 2])
    return x


DEPTH_2 = 1

PLE_DIM = 256
EPS = 1e-6
RET_HEADS = 4
RET_QK_DIM = 256
RET_V_DIM = 512
RET_CHUNK = 128
RET_ROPE_BASE = 10000.0
DIL_GROUPS = ((128, 1), (512, 4), (2048, 16))
DIL_SLOTS = 8
DIL_HEAD_DIM = 64
DIL_BLOCK = 128
ROPE_THETA_2 = 500000.0
ROPE_DIM = DIL_HEAD_DIM // 4
D_FF_2 = 4 * D_MODEL

RET_QK_W = RET_HEADS * RET_QK_DIM
RET_V_W = RET_HEADS * RET_V_DIM
DIL_HEADS = len(DIL_GROUPS) * DIL_SLOTS
DIL_W = DIL_HEADS * DIL_HEAD_DIM
DIL_OUT_W = DIL_SLOTS * DIL_HEAD_DIM
SPLITS = (RET_QK_W, RET_QK_W, RET_V_W, RET_V_W, DIL_W, DIL_W, DIL_W, D_MODEL, D_MODEL)
IN_W = RET_QK_W * 2 + RET_V_W * 2 + DIL_W * 3 + D_MODEL * 2


def rmsnorm(x, g=None):
    xf = x.astype(jnp.float32)
    y = xf * lax.rsqrt(jnp.mean(xf * xf, axis=-1, keepdims=True) + EPS)
    if g is not None:
        y = y * g.astype(jnp.float32)
    return y.astype(x.dtype)

def rope(x, cos, sin, rot_dim):
    half = rot_dim // 2
    x1 = x[..., :half]
    x2 = x[..., half:rot_dim]
    return jnp.concatenate([x1 * cos - x2 * sin, x2 * cos + x1 * sin, x[..., rot_dim:]], axis=-1)

def retention(q, k, v, pos):
    B, S, H, dk = q.shape
    dv = v.shape[-1]
    f32 = jnp.float32
    half = dk // 2
    inv_freq = 1.0 / (RET_ROPE_BASE ** jnp.linspace(0.0, 1.0, half, dtype=f32))
    ang = pos.astype(f32)[:, :, None, None] * inv_freq
    cos, sin = jnp.cos(ang), jnp.sin(ang)
    q = rope(q.astype(f32), cos, sin, dk)
    k = rope(k.astype(f32), cos, sin, dk) * (dk ** -0.5)
    v = v.astype(f32)
    C = RET_CHUNK
    Sp = -(-S // C) * C
    padw = ((0, 0), (0, Sp - S), (0, 0), (0, 0))
    nc = Sp // C
    qc = jnp.pad(q, padw).reshape(B, nc, C, H, dk)
    kc = jnp.pad(k, padw).reshape(B, nc, C, H, dk)
    vc = jnp.pad(v, padw).reshape(B, nc, C, H, dv)
    log_gamma = jnp.log1p(-(2.0 ** (-5.0 - jnp.arange(H, dtype=f32))))
    idx = jnp.arange(C, dtype=f32)
    diff = idx[:, None] - idx[None, :]
    decay = jnp.where(diff[None] >= 0, jnp.exp(jnp.maximum(diff, 0.0)[None] * log_gamma[:, None, None]), 0.0)
    scores = jnp.einsum('bnihd,bnjhd->bnhij', qc, kc) * decay[None, None]
    inner = jnp.einsum('bnhij,bnjhe->bnihe', scores, vc)
    q_dec = jnp.exp((idx + 1.0)[:, None] * log_gamma[None, :])
    k_dec = jnp.exp((C - 1.0 - idx)[:, None] * log_gamma[None, :])
    chunk_dec = jnp.exp(C * log_gamma)

    def step(R, inp):
        qn, kn, vn = inp
        cross = jnp.einsum('bihd,bhde->bihe', qn * q_dec[None, :, :, None], R)
        R = R * chunk_dec[None, :, None, None] + jnp.einsum('bjhd,bjhe->bhde', kn * k_dec[None, :, :, None], vn)
        return R, cross

    R0 = jnp.zeros((B, H, dk, dv), f32)
    _, cross = lax.scan(step, R0, (jnp.moveaxis(qc, 1, 0), jnp.moveaxis(kc, 1, 0), jnp.moveaxis(vc, 1, 0)))
    y = inner + jnp.moveaxis(cross, 0, 1)
    return y.reshape(B, Sp, H, dv)[:, :S]

def dilated_group(q, k, v, window, dilation):
    B, S, Hg, hd = q.shape
    f32 = jnp.float32
    band = window // dilation
    QB = DIL_BLOCK
    seg = dilation * QB
    Sp = -(-S // seg) * seg
    L = Sp // dilation
    nb = L // QB
    padw = ((0, 0), (0, Sp - S), (0, 0), (0, 0))

    def to_streams(t):
        t = jnp.pad(t.astype(f32), padw).reshape(B, L, dilation, Hg, hd)
        return t.transpose(0, 2, 1, 3, 4).reshape(B, dilation, nb, QB, Hg, hd)

    def with_prev(t):
        prev = jnp.pad(t[:, :, :-1], ((0, 0), (0, 0), (1, 0), (0, 0), (0, 0), (0, 0)))
        return jnp.concatenate([prev, t], axis=3)

    qs = to_streams(q)
    kk = with_prev(to_streams(k))
    vv = with_prev(to_streams(v))
    s = jnp.einsum('bcnqhe,bcnkhe->bcnhqk', qs, kk) * (hd ** -0.5)
    qi = jnp.arange(QB)[:, None]
    kj = jnp.arange(2 * QB)[None, :] - QB
    dist = qi - kj
    in_band = (dist >= 0) & (dist <= band)
    key_exists = (jnp.arange(nb)[:, None, None] * QB + kj[None]) >= 0
    mask = in_band[None] & key_exists
    s = jnp.where(mask[None, None, :, None], s, -1e30)
    lse = jax.nn.logsumexp(s, axis=-1)
    pr = jnp.exp(s - lse[..., None])
    o = jnp.einsum('bcnhqk,bcnkhe->bcnqhe', pr, vv)
    o = o.reshape(B, dilation, L, Hg, hd).transpose(0, 2, 1, 3, 4).reshape(B, Sp, Hg, hd)[:, :S]
    lse = lse.transpose(0, 1, 2, 4, 3).reshape(B, dilation, L, Hg).transpose(0, 2, 1, 3).reshape(B, Sp, Hg)[:, :S]
    return o, lse

def dilated_attention(q, k, v, pos):
    f32 = jnp.float32
    freqs = ROPE_THETA_2 ** (-jnp.arange(0, ROPE_DIM, 2, dtype=f32) / ROPE_DIM)
    ang = pos.astype(f32)[:, :, None, None] * freqs
    cos, sin = jnp.cos(ang), jnp.sin(ang)
    q = rope(q.astype(f32), cos, sin, ROPE_DIM)
    k = rope(k.astype(f32), cos, sin, ROPE_DIM)
    outs, lses = [], []
    for g, (window, dilation) in enumerate(DIL_GROUPS):
        sl = slice(g * DIL_SLOTS, (g + 1) * DIL_SLOTS)
        o, l = dilated_group(q[:, :, sl], k[:, :, sl], v[:, :, sl], window, dilation)
        outs.append(o)
        lses.append(l)
    w = jax.nn.softmax(jnp.stack(lses, axis=0), axis=0)
    return jnp.sum(w[..., None] * jnp.stack(outs, axis=0), axis=0)

def second_inputs(seed: int = 0) -> dict:
    key = jax.random.key(seed)
    ks = jax.random.split(key, 24)
    f32 = jnp.float32
    nrm = lambda k, shape, fan_in: jax.random.normal(k, shape, f32) * (fan_in ** -0.5)
    gain = lambda k: 1.0 + 0.02 * jax.random.normal(k, (DEPTH_2, D_MODEL), f32)
    x = jax.random.normal(ks[0], (BATCH, SEQ, D_MODEL), f32)
    p = jax.random.normal(ks[1], (DEPTH_2, BATCH, SEQ, PLE_DIM), f32)
    positions = jnp.broadcast_to(jnp.arange(SEQ, dtype=jnp.int32)[None, :], (BATCH, SEQ))
    return {
        "x": x,
        "p": p,
        "positions": positions,
        "w_in": nrm(ks[2], (DEPTH_2, D_MODEL, IN_W), D_MODEL),
        "b_gate": 0.01 * jax.random.normal(ks[3], (DEPTH_2, 2, D_MODEL), f32),
        "w_ret_out": nrm(ks[4], (DEPTH_2, RET_V_W, D_MODEL), RET_V_W),
        "w_dil_out": nrm(ks[5], (DEPTH_2, DIL_OUT_W, D_MODEL), DIL_OUT_W),
        "w_o": nrm(ks[6], (DEPTH_2, D_MODEL, D_MODEL), D_MODEL),
        "g_pre_mix": gain(ks[7]),
        "g_post_mix": gain(ks[8]),
        "g_pre_mlp": gain(ks[9]),
        "g_post_mlp": gain(ks[10]),
        "w_up": nrm(ks[11], (DEPTH_2, D_MODEL, D_FF_2), D_MODEL),
        "w_down": nrm(ks[12], (DEPTH_2, D_FF_2, D_MODEL), D_FF_2),
        "g_pre_ple": gain(ks[13]),
        "w_ple_gate": nrm(ks[14], (DEPTH_2, D_MODEL, D_MODEL), D_MODEL),
        "b_ple_gate": 0.01 * jax.random.normal(ks[15], (DEPTH_2, D_MODEL), f32),
        "w_ple_in": nrm(ks[16], (DEPTH_2, PLE_DIM, D_MODEL), PLE_DIM),
        "g_post_ple": gain(ks[17]),
    }

def second_block(x, p, positions, w_in, b_gate, w_ret_out, w_dil_out, w_o, g_pre_mix, g_post_mix,
              g_pre_mlp, g_post_mlp, w_up, w_down, g_pre_ple, w_ple_gate, b_ple_gate, w_ple_in,
              g_post_ple):
    B, S, _ = x.shape
    split_points = [int(s) for s in np.cumsum(SPLITS)[:-1]]
    h = x
    for i in range(DEPTH_2):
        u = rmsnorm(h, g_pre_mix[i])
        proj = u @ w_in[i]
        rq, rk, rv, rg, aq, ak, av, gr, ga = jnp.split(proj, split_points, axis=-1)
        yr = retention(rq.reshape(B, S, RET_HEADS, RET_QK_DIM), rk.reshape(B, S, RET_HEADS, RET_QK_DIM),
                       rv.reshape(B, S, RET_HEADS, RET_V_DIM), positions)
        yr = rmsnorm(yr) * jax.nn.silu(rg.reshape(B, S, RET_HEADS, RET_V_DIM).astype(jnp.float32))
        ya_branch = yr.reshape(B, S, RET_V_W).astype(h.dtype) @ w_ret_out[i]
        ya = dilated_attention(aq.reshape(B, S, DIL_HEADS, DIL_HEAD_DIM), ak.reshape(B, S, DIL_HEADS, DIL_HEAD_DIM),
                               av.reshape(B, S, DIL_HEADS, DIL_HEAD_DIM), positions)
        yb_branch = ya.reshape(B, S, DIL_OUT_W).astype(h.dtype) @ w_dil_out[i]
        mixed = jax.nn.sigmoid(gr + b_gate[i, 0]) * ya_branch + jax.nn.sigmoid(ga + b_gate[i, 1]) * yb_branch
        h = h + rmsnorm(mixed @ w_o[i], g_post_mix[i])
        v2 = rmsnorm(h, g_pre_mlp[i])
        f = jnp.square(jax.nn.relu(v2 @ w_up[i])) @ w_down[i]
        h = h + rmsnorm(f, g_post_mlp[i])
        gate = jax.nn.sigmoid(rmsnorm(h, g_pre_ple[i]) @ w_ple_gate[i] + b_ple_gate[i])
        e = p[i].astype(h.dtype) @ w_ple_in[i]
        h = h + rmsnorm(gate * e, g_post_ple[i])
    return h


def setup_inputs(seed=0):
    out = dict(first_inputs(seed))
    for name, value in second_inputs(seed + 1).items():
        if name != "x":
            out[name + "_2"] = value
    return out


def reference(
    x, mem, a_w_qkv, a_sinks, a_w_o, b_w_in, b_conv_w, b_conv_b, b_w_rgate, b_b_rgate,
    b_w_igate, b_b_igate, b_lambda, b_w_o, c_w_down, c_q_norm, c_kv_norm, c_w_uq, c_w_ukv,
    c_w_o, mem_w_kv, x_w_q, x_w_o, f_w_up, f_conv_w, f_conv_b, f_w_down, ln_g, ln_b, p_2,
    positions_2, w_in_2, b_gate_2, w_ret_out_2, w_dil_out_2, w_o_2, g_pre_mix_2, g_post_mix_2,
    g_pre_mlp_2, g_post_mlp_2, w_up_2, w_down_2, g_pre_ple_2, w_ple_gate_2, b_ple_gate_2,
    w_ple_in_2, g_post_ple_2,
):
    x = first_block(
        x, mem, a_w_qkv, a_sinks, a_w_o, b_w_in, b_conv_w, b_conv_b, b_w_rgate, b_b_rgate,
        b_w_igate, b_b_igate, b_lambda, b_w_o, c_w_down, c_q_norm, c_kv_norm, c_w_uq, c_w_ukv,
        c_w_o, mem_w_kv, x_w_q, x_w_o, f_w_up, f_conv_w, f_conv_b, f_w_down, ln_g, ln_b,
    )
    return second_block(
        x, p_2, positions_2, w_in_2, b_gate_2, w_ret_out_2, w_dil_out_2, w_o_2, g_pre_mix_2,
        g_post_mix_2, g_pre_mlp_2, g_post_mlp_2, w_up_2, w_down_2, g_pre_ple_2, w_ple_gate_2,
        b_ple_gate_2, w_ple_in_2, g_post_ple_2,
    )


_drawn_inputs = setup_inputs


def setup_inputs(seed=0):
    import zlib

    import numpy as np

    out = dict(_drawn_inputs(seed))
    spreads = {}
    factors = {'a_sinks': 4.031,
     'b_conv_b': 6.298,
     'b_b_rgate': 8.0,
     'b_b_igate': 8.0,
     'c_q_norm': 8.0,
     'c_kv_norm': 8.0,
     'f_conv_b': 8.0,
     'b_gate_2': 8.0,
     'g_post_mix_2': 4.082,
     'g_pre_mlp_2': 13.184,
     'g_post_mlp_2': 19.523,
     'g_pre_ple_2': 33.207,
     'b_ple_gate_2': 64.0,
     'g_post_ple_2': 25.633}
    for name, (base, spread) in spreads.items():
        noise = np.random.default_rng([zlib.crc32(name.encode()), seed]).standard_normal(out[name].shape)
        drawn = base * np.exp(spread * noise) if base else spread * noise
        out[name] = __import__('jax').numpy.asarray(drawn.astype(out[name].dtype))
    for name, factor in factors.items():
        out[name] = (out[name] * factor).astype(out[name].dtype)
    return out
```

```python
from contextlib import ExitStack

import numpy as np

import concourse.bass as bass
from concourse import mybir

F32 = mybir.dt.float32
I32 = mybir.dt.int32
ALU = mybir.AluOpType
ACT = mybir.ActivationFunctionType
AX = mybir.AxisListType

P = 128
S = 256
D = 1024
DEPTH = 4
TT = S // P
DC = D // P
SLOTS = 4
UW = 256
NEG = -1e30
LN_EPS = 1e-5
RMS_EPS = 1e-6
ALPHA = (2.0 * DEPTH) ** 0.25

A_HEADS, A_KV, A_HD = 16, 4, 64
LRU_BLOCKS, LRU_TAPS, LRU_C = 4, 4, 8.0
C_HEADS, C_NOPE, C_ROPE, C_QR, C_KVR = 8, 128, 64, 384, 256
C_DOWN = C_QR + C_KVR + C_ROPE
X_HEADS, X_HD = 4, 256
FF, FFC, F_TAPS = 2816, 22, 3
FF2 = 4096
R_HEADS, R_QK, R_V = 4, 256, 512
D_SLOTS, D_GROUPS, D_HD, D_ROT = 8, ((128, 1), (512, 4), (2048, 16)), 64, 16
D_W = D_SLOTS * len(D_GROUPS) * D_HD
R_COLS = 2 * R_HEADS * R_QK + 2 * R_HEADS * R_V
D_COLS = 3 * D_W + 2 * D
NF = R_QK // 2 + D_ROT // 2
TWO_PI = 2 * np.pi
PI_1 = 6.28125
PI_2 = 2029 / 2.0**20
PI_3 = TWO_PI - PI_1 - PI_2
ROUND = 12582912.0
LRU_SP = 2

PARAM_ROWS = [
    ("ln_g", 96), ("ln_b", 96), ("f_conv_w", 528), ("f_conv_b", 176), ("b_conv_w", 32), ("b_conv_b", 8),
    ("b_b_rgate", 8), ("b_b_igate", 8), ("b_lambda", 8), ("c_q_norm", 3), ("c_kv_norm", 2),
    ("g_pre_mix_2", 8), ("g_pre_mlp_2", 8), ("g_pre_ple_2", 8),
]
COL = {}
_at = 0
for _name, _rows in PARAM_ROWS:
    COL[_name] = _at
    _at += _rows
PARAMS = _at

ACC, STEP, TURN = 0, 4, 6


def shape_constants():
    f = np.float32
    inv = f(1.0) / (f(10000.0) ** (np.arange(0, A_HD, 2, dtype=f) / f(A_HD)))
    ang = np.arange(S, dtype=f)[:, None] * inv[None, :]
    rope = np.stack([np.cos(ang), np.sin(ang)], 1).astype(f)
    q = np.arange(P)[:, None]
    k = np.arange(P)[None, :]
    causal = np.where(q >= k, 0.0, NEG)
    window = np.where(k > q, 0.0, NEG)
    mask_a = np.concatenate([causal, window, causal], 1)
    mask_c = np.concatenate([causal, np.zeros((P, P)), causal], 1)
    parts = []
    for tt in range(TT):
        for span, dil in D_GROUPS:
            dist = q + tt * P - np.arange((tt + 1) * P)[None, :]
            parts.append(np.where((dist >= 0) & (dist % dil == 0) & (dist <= span), 0.0, NEG))
    mask_d = np.concatenate(parts, 1)
    log_gamma = np.log1p(-(2.0 ** (-5.0 - np.arange(R_HEADS))))
    diff = np.arange(S)[None, :] - np.arange(P)[:, None]
    dec = np.where(diff[None] >= 0, np.exp(np.maximum(diff, 0)[None] * log_gamma[:, None, None]), 0.0) * R_QK**-0.5
    dec = np.concatenate([dec, dec[:, :, :P]], 2).transpose(1, 0, 2)
    fr = f(1.0) / (f(10000.0) ** np.linspace(0.0, 1.0, R_QK // 2, dtype=f))
    fd = f(500000.0) ** (-np.arange(0, D_ROT, 2, dtype=f) / f(D_ROT))
    return {
        "k_ident": np.eye(P, dtype=f), "k_rope": rope, "k_mask_a": mask_a.astype(f), "k_mask_c": mask_c.astype(f),
        "k_mask_d": mask_d.astype(f), "k_decay": np.ascontiguousarray(dec.astype(f)),
        "k_freq": np.concatenate([fr, fd]).astype(f)[None, :],
    }


LAYOUT = {
    "x": (S, D), "mem": (S, D), "p_2": (S, 256), "positions_2": (S,), "w_in_2": (D, R_COLS + D_COLS), "b_gate_2": (2, D),
    "w_ret_out_2": (R_HEADS * R_V, D), "w_dil_out_2": (D_SLOTS * D_HD, D), "w_o_2": (D, D), "g_pre_mix_2": (D,),
    "g_post_mix_2": (D,), "g_pre_mlp_2": (D,), "g_post_mlp_2": (D,), "w_up_2": (D, FF2), "w_down_2": (FF2, D),
    "g_pre_ple_2": (D,), "w_ple_gate_2": (D, D), "b_ple_gate_2": (D,), "w_ple_in_2": (256, D), "g_post_ple_2": (D,),
}


def build(nc, w, out):
    param_views = {}
    for name, rows in PARAM_ROWS:
        v = w[name]
        axes = "abcd"[:len(v.shape) - 1]
        names = " ".join(axes)
        param_views[name] = v.rearrange(f"{names} (c f) -> ({names} c) f", f=P)
    n_row_loads = 0
    _r = 0
    for name, rows in PARAM_ROWS:
        n_row_loads += (_r + rows - 1) // P - _r // P + 1
        _r += rows
    with ExitStack() as ctx:
        sb = lambda name, shape, dt=F32: ctx.enter_context(nc.sbuf_tensor(name, shape, dt))
        sem = lambda name: ctx.enter_context(nc.semaphore(name))

        ring = [sb(f"ring{i}", [P, 2048]) for i in range(SLOTS)]
        resid = sb("resid", [P, TT, D])
        normed = sb("normed", [P, TT, D])
        xt = sb("xt", [P, DC, S])
        ht = sb("ht", [P, FF2 // P, S])
        work = sb("work", [P, TT * D_COLS])
        qt = sb("qt", [P, DC, S])
        kt = sb("kt", [P, DC, S])
        mem_kt = sb("mem_kt", [P, DC, S])
        mem_v = sb("mem_v", [P, TT, D])
        heads = sb("heads", [P, TT, D])
        gains = sb("gains", [P, 2, D])
        params = sb("params", [P, PARAMS])
        ident = sb("ident", [P, P])
        rope_t = sb("rope_t", [P, TT, 2, A_HD // 2])
        mask_a = sb("mask_a", [P, 3 * P])
        mask_c = sb("mask_c", [P, 3 * P])
        sinks = sb("sinks", [P, 2 * A_HEADS])
        masked = [sb(f"masked{i}", [P, 512]) for i in range(2)]
        probs = [sb(f"probs{i}", [P, 512]) for i in range(2)]
        probs_t = [sb(f"probs_t{i}", [P, 512]) for i in range(2)]
        stat = [sb(f"stat{i}", [P, 12]) for i in range(2)]
        var = sb("var", [P, 96])
        rstd = sb("rstd", [P, 96])
        ssq = sb("ssq", [P, 96])
        bn = sb("bn", [P, TT, 2, 6])
        bn_mv = sb("bn_mv", [P, TT, 2])
        minus_half = sb("minus_half", [P, 4])
        q_rope_t = ht[0:C_ROPE, DC:DC + C_HEADS, :]
        k_rope_t = ht[0:C_ROPE, DC + C_HEADS, :]
        softplus = sb("softplus", [P, 6, DC])
        bank = ctx.enter_context(nc.psum_tensor("bank", [P, 8, 512], F32))

        tok = lambda cols: work[:, 0:TT * cols].rearrange("p (t c) -> p t c", t=TT)
        part = lambda i: work[:, i * 2048:(i + 1) * 2048].rearrange("p (c s) -> p c s", s=S)
        stage_rows = work[:, 0:1024].rearrange("p (a f) -> p a f", f=P)
        k_dup = work[:, 4096:4096 + TT * A_KV * P].rearrange("p (t h e d) -> p t h e d", t=TT, h=A_KV, e=2)
        mla_qr = lambda: work[:, 8192:8192 + TT * C_HEADS * C_ROPE].rearrange("p (t h d) -> p t h d", t=TT, h=C_HEADS)
        mla_v = lambda: work[:, 10240:10240 + TT * D].rearrange("p (t f) -> p t f", t=TT)

        def in_rows(flat, n, half):
            return flat[:, 0:n * 2 * half].rearrange("p (h e d) -> p h e d", e=2, d=half)

        rot_c_view = lambda k, n, half: in_rows(heads[:, k % 2, :], n, half)
        rot_s_view = lambda k, n, half: in_rows(ht[:, 24 + k % 2 * 4:28 + k % 2 * 4, :].rearrange("p c s -> p (c s)"), n, half)

        def bcast(table, n, half):
            return table.unsqueeze(1).unsqueeze(1).to_broadcast([P, n, 2, half])

        def flat2(x):
            return x[:, :, :].rearrange("p c s -> p (c s)")

        wide_bufs = [[flat2(x)[:, i * 768:(i + 1) * 768] for i in range(2)] for x in (qt, kt, xt)]
        cwork = [[work[:, (2 * i + j) * 512:(2 * i + j + 1) * 512].rearrange("p (c s) -> p c s", s=S)
                  for j in range(2)] for i in range(2)]
        swork = [work[:, 2048 + i * 512:2560 + i * 512].rearrange("p (c s) -> p c s", s=S) for i in range(2)]
        m2 = mem_kt[:, :, :].rearrange("p c s -> p (c s)")
        mask_d = m2[:, 0:9 * P]
        v2 = mem_v[:, :, :].rearrange("p c s -> p (c s)")
        decay = v2[:, 0:R_HEADS * 3 * P].rearrange("p (h c) -> p h c", h=R_HEADS)
        angles = sb("angles", [P, 3, TT, NF])
        pos_i = sb("pos_i", [P, TT], I32)
        pos_f = sb("pos_f", [P, TT])
        freq = sb("freq", [P, NF])

        w_full = [sem(f"w_full{i}") for i in range(SLOTS)]
        unit_done = sem("unit_done")
        acc_first = sem("acc_first")
        gate_step = sem("gate_step")
        step_out = [sem("step_out0"), sem("step_out1")]
        turn_done = sem("turn_done")
        turn_out = [sem("turn_out0"), sem("turn_out1")]
        ident_in, x_in, mem_in, rows_in, tables_in = (sem(n) for n in ("ident_in", "x_in", "mem_in", "rows_in", "tables_in"))
        tables2_in, p_in, out_written = sem("tables2_in"), sem("p_in"), sem("out_written")
        gains_in = sem("gains_in")
        gains_used = sem("gains_used")
        half_set = sem("half_set")
        var_ready, rstd_ready, ssq_ready = sem("var_ready"), sem("rstd_ready"), sem("ssq_ready")
        normed_ready, resid_ready = sem("normed_ready"), sem("resid_ready")
        dve_link, act_link, pool_link = sem("dve_link"), sem("act_link"), sem("pool_link")
        scores_done, soft_done, exp_done, pt_done, pt_out, pv_done, head_out = (
            sem(n) for n in ("scores_done", "soft_done", "exp_done", "pt_done", "pt_out", "pv_done", "head_out"))
        conv_start, conv_tap, glu_gate, glu_out = (sem(n) for n in ("conv_start", "conv_tap", "glu_gate", "glu_out"))
        rot_cos, rot_sin, rot_out = sem("rot_cos"), sem("rot_sin"), sem("rot_out")
        lru_act, lru_dve, lru_pool, lru_pool_exp = (sem(n) for n in ("lru_act", "lru_dve", "lru_pool", "lru_pool_exp"))
        mla_sq, mla_scaled = sem("mla_sq"), sem("mla_scaled")
        ret_scores, ret_decayed, ret_pv, ret_norm = (sem(n) for n in ("ret_scores", "ret_decayed", "ret_pv", "ret_norm"))
        relu_out, relu_sq = sem("relu_out"), sem("relu_sq")
        angle_ready, trig_ready = sem("angle_ready"), sem("trig_ready")
        branch_out, gate_in, gate_sig, mix_ready = (sem(n) for n in ("branch_out", "gate_in", "gate_sig", "mix_ready"))
        ple_in, ple_sig, ple_prod = sem("ple_in"), sem("ple_sig"), sem("ple_prod")
        block = ctx.enter_context(nc.Block())

        class At:

            def __init__(self):
                self.u = self.v = self.r = self.n = self.rot = self.msq = self.col = self.sq = self.nrm = self.acc = 0

        def unit_groups(eng, u0, n, peel=0):
            full = n // SLOTS
            start = full if (u0 < SLOTS or full - peel < 3) else peel
            for i in range(start):
                for j in range(SLOTS):
                    yield i, j
            if start < full:
                with eng.Fori(start, full) as i:
                    for j in range(SLOTS):
                        yield i, j
            for j in range(n - SLOTS * full):
                yield full, j

        def slot_of(u0, j):
            return (u0 + j) % SLOTS

        def fills(u0, i, j):
            return i * 16 + 16 * ((u0 + j) // SLOTS + 1)

        def pairs_before(v0, i, j):
            return i * 2 + (v0 + j) // 2

        def wait_step(eng, v):
            eng.wait_ge(step_out[v % 2], v // 2 + 1)

        def wait_turn(eng, r):
            eng.wait_ge(turn_out[r % 2], r // 2 + 1)

        def wait_turns(eng, r_end):
            wait_turn(eng, r_end - 1)
            wait_turn(eng, r_end - 2)

        def wait_steps(eng, v_end):
            wait_step(eng, v_end - 1)
            wait_step(eng, v_end - 2)

        def step_bank(v):
            return bank[:, STEP + v % 2, :]

        def turn_bank(r):
            return bank[:, TURN + r % 2, :]

        def acc_bank(tt, half):
            return bank[:, ACC + 2 * tt + half, :]

        def acc_tile(tt):
            return bank[:, ACC + 2 * tt:ACC + 2 * tt + 2, :].rearrange("p a b -> p (a b)")

        def for_turns(at, copy):

            def wide(dst, chunks, tts=range(TT), base=0):
                for tt in tts:
                    for c in range(0, chunks, 4):
                        m = min(4, chunks - c)
                        copy([(dst[:, base + c:base + c + m, tt * P:(tt + 1) * P], (0, m * P), None, None)])

            def setup():
                wide(ht, DC)
                copy([(params[:, 0:4 * P], (0, 4 * P), None, None)])
                copy([(params[:, 4 * P:PARAMS], (0, PARAMS - 4 * P), None, None)])
                wide(xt, DC)

            def swa_turns():
                for tt in range(TT):
                    wide(qt, DC, [tt])
                    wide(kt, A_KV, [tt])

            def norm(gain):
                for tt in range(TT):
                    for c in range(0, DC, 4):
                        copy([(xt[:, c + k, tt * P:(tt + 1) * P], (k * P, (k + 1) * P), *gain(c + k)) for k in range(4)])

            def mla_low():
                for tt in range(TT):
                    t = slice(tt * P, (tt + 1) * P)
                    copy([(ht[:, c, t], (c * P, (c + 1) * P), col("c_q_norm", c) if c < 3 else col("c_kv_norm", 0), None)
                          for c in range(4)])
                    copy([(ht[:, 4, t], (0, P), col("c_kv_norm", 1), None), (k_rope_t[:, t], (P, 2 * P), None, None)])

            def mla_q():
                for tt in range(TT):
                    for h in range(0, C_HEADS, 4):
                        copy([(q_rope_t[:, h:h + 4, tt * P:(tt + 1) * P], (0, 4 * P), None, None)])

            def ret_qk():
                for dst in (qt, kt):
                    wide(dst, DC)

            def dil_qk():
                for pq in range(2):
                    wide(ht, D_W // P, base=pq * (D_W // P))

            def p_turn():
                copy([(ht[:, c, tt * P:(tt + 1) * P], ((2 * tt + c) * P, (2 * tt + c + 1) * P), None, None)
                      for tt in range(TT) for c in range(2)])

            return {"setup": setup, "swa": swa_turns, "heads": lambda: wide(ht, DC), "norm": norm, "mla_low": mla_low,
                    "mla_q": mla_q, "ret_qk": ret_qk, "ret_out": lambda: wide(ht, 2 * DC), "dil_qk": dil_qk,
                    "dil_out": lambda: wide(ht, 4, base=24), "p": p_turn}

        col = lambda name, i: params[:, COL[name] + i:COL[name] + i + 1]

        class Attention:
            def __init__(self, count, segs, scale, mask, sink, scores, pv, dest, wide=False):
                self.count, self.segs, self.scale, self.mask, self.sink = count, segs, scale, mask, sink
                self.scores, self.pv, self.dest, self.wide = scores, pv, dest, wide

            def bufs(self, n):
                return [x[n % 2] for x in (wide_bufs if self.wide else (masked, probs, probs_t))]

            def s_bank(self, i):
                n = self.segs(i)[-1][1]
                if self.wide:
                    return bank[:, ACC + 2 * (i % 2):ACC + 2 * (i % 2) + 2, :].rearrange("p a b -> p (a b)")[:, 0:n]
                return bank[:, ACC + i % 2, 0:n]

            def t_bank(self, i):
                n = self.segs(i)[-1][1]
                if self.wide:
                    return bank[:, STEP:STEP + 2, :].rearrange("p a b -> p (a b)")[:, 0:n]
                return bank[:, ACC + 2 + i % 2, 0:n]

            def o_bank(self, i):
                return bank[:, (TURN if self.wide else STEP) + i % 2, :]

        causal_segs = lambda i: [(0, P), (P, 3 * P)]

        def swa(layer):
            qkv = tok(1536)

            def scores(h):
                o, kv = h % 2 * A_HD, h // (A_HEADS // A_KV)
                return [(c0, c1, [(qt[o:o + A_HD, h // 2, tt * P:(tt + 1) * P], kt[o:o + A_HD, kv, 0:c1 - c0])])
                        for tt, (c0, c1) in enumerate(causal_segs(h))]

            def pv(h):
                at = (A_HEADS + A_KV + h // (A_HEADS // A_KV)) * A_HD
                v = [qkv[:, kb, at:at + A_HD] for kb in range(TT)]
                return [(0, A_HD, [(0, v[0])]), (A_HD, 2 * A_HD, [(1, v[0]), (2, v[1])])]

            return Attention(A_HEADS, causal_segs, A_HD**-0.5, lambda i: mask_a[:, :],
                             lambda i: sinks[:, layer * A_HEADS + i:layer * A_HEADS + i + 1], scores, pv,
                             lambda i: heads[:, :, i * A_HD:(i + 1) * A_HD])

        def mla():
            v_tok = mla_v()

            def scores(h):
                return [(c0, c1, [(qt[:, h, tt * P:(tt + 1) * P], kt[:, h, 0:c1 - c0]),
                                  (q_rope_t[:, h, tt * P:(tt + 1) * P], k_rope_t[:, 0:c1 - c0])])
                        for tt, (c0, c1) in enumerate(causal_segs(h))]

            def pv(h):
                v = [v_tok[:, kb, h * P:(h + 1) * P] for kb in range(TT)]
                return [(0, P, [(0, v[0])]), (P, 2 * P, [(1, v[0]), (2, v[1])])]

            return Attention(C_HEADS, causal_segs, (C_NOPE + C_ROPE) ** -0.5, lambda i: mask_c[:, :], None, scores, pv,
                             lambda i: heads[:, :, i * P:(i + 1) * P])

        def cross():
            segs = lambda i: [(0, S), (S, 2 * S)]

            def scores(h):
                return [(c0, c1, [(qt[:, 2 * h + c, tt * P:(tt + 1) * P], mem_kt[:, 2 * h + c, :]) for c in range(2)])
                        for tt, (c0, c1) in enumerate(segs(h))]

            def pv(h):
                v = [mem_v[:, kb, h * X_HD:(h + 1) * X_HD] for kb in range(TT)]
                return [(0, X_HD, [(0, v[0]), (1, v[1])]), (X_HD, 2 * X_HD, [(2, v[0]), (3, v[1])])]

            return Attention(X_HEADS, segs, X_HD**-0.5, None, None, scores, pv,
                             lambda i: heads[:, :, i * X_HD:(i + 1) * X_HD])

        def dilated():
            qkv = tok(D_COLS)
            n_g = len(D_GROUPS)
            width = lambda i: (i % TT + 1) * P

            def scores(i):
                s, tt, kw = i // TT, i % TT, width(i)
                mms = []
                for g in range(n_g):
                    head = g * D_SLOTS + s
                    o = head % 2 * D_HD
                    mms.append((g * kw, (g + 1) * kw, [(ht[o:o + D_HD, head // 2, tt * P:(tt + 1) * P],
                                                        ht[o:o + D_HD, D_W // P + head // 2, 0:kw])]))
                return mms

            def pv(i):
                s, tt = i // TT, i % TT
                terms = []
                for g in range(n_g):
                    at = 2 * D_W + (g * D_SLOTS + s) * D_HD
                    terms += [(g * (tt + 1) + kb, qkv[:, kb, at:at + D_HD]) for kb in range(tt + 1)]
                return [(0, D_HD, terms)]

            return Attention(D_SLOTS * TT, lambda i: [(0, n_g * width(i))], D_HD**-0.5,
                             lambda i: mask_d[:, 0:n_g * P] if i % TT == 0 else mask_d[:, n_g * P:9 * P], None, scores, pv,
                             lambda i: heads[:, i % TT:i % TT + 1, i // TT * D_HD:(i // TT + 1) * D_HD], wide=True)

        @block.sync
        def _(sp):
            at = At()

            def load(n, src, dst=lambda slot: ring[slot][:, :].rearrange("p (k c) -> p k c", k=DC)):
                u0 = at.u
                for i, j in unit_groups(sp, u0, n):
                    if isinstance(i, int) and u0 + 4 * i + j < SLOTS:
                        pass
                    else:
                        sp.wait_ge(unit_done, i * SLOTS + (u0 + j - SLOTS + 1))
                    slot = slot_of(u0, j)
                    sp.dma_start(dst(slot), src(i * SLOTS + j)).then_inc(w_full[slot], 16)
                at.u += n

            def cols(mat, first=0, width=UW, kc=DC):
                view = mat.rearrange("(k p) n -> p k n", p=P)
                return lambda q: view[:, :, bass.ds(q * width + first, width)]

            def packed(kc, width):
                return lambda slot: ring[slot][:, 0:kc * width].rearrange("p (k c) -> p k c", k=kc)

            def rows(mat):
                view = mat.rearrange("(u k p) n -> p u k n", p=P, k=2)
                return lambda q: view[:, bass.ds(q, 1), :, :].rearrange("p a k n -> p (a k) n")

            def load_gains(first, second):
                g = at.nrm
                if g >= 1:
                    sp.wait_ge(gains_used, g)
                for h, row in enumerate((first, second)):
                    sp.dma_start(gains[:, h, :], row.rearrange("(a n) -> a n", a=1).to_broadcast([P, D])).then_inc(gains_in, 16)
                at.nrm += 1

            def square(mat, n_units):
                load(n_units, rows(mat), packed(2, D))

            def load_ln(n):
                load_gains(w["ln_g"][n // 3, n % 3, :], w["ln_b"][n // 3, n % 3, :])

            load(8, cols(w["mem_w_kv"]))
            for layer in range(DEPTH):
                kind, j = layer % 3, layer // 3
                if kind == 0:
                    load(6, cols(w["a_w_qkv"][j]))
                    load_ln(3 * layer)
                    square(w["a_w_o"][j], 4)
                elif kind == 1:
                    load(8, cols(w["b_w_in"][j]))
                    for name in ("b_w_rgate", "b_w_igate"):
                        v = w[name][j].rearrange("h (k p) n -> p (h k) n", p=P)
                        load(1, lambda q, v=v: v)
                    load_ln(3 * layer)
                    square(w["b_w_o"][j], 4)
                else:
                    load(2, cols(w["c_w_down"][j]))
                    load(1, cols(w["c_w_down"][j], 2 * UW, C_DOWN - 2 * UW), packed(DC, C_DOWN - 2 * UW))
                    load(8, cols(w["c_w_uq"][j], 0, C_NOPE + C_ROPE), packed(3, C_NOPE + C_ROPE))
                    load(8, cols(w["c_w_ukv"][j]), packed(2, UW))
                    load_ln(3 * layer)
                    square(w["c_w_o"][j], 4)
                load(4, cols(w["x_w_q"][layer]))
                load_ln(3 * layer + 1)
                square(w["x_w_o"][layer], 4)
                up = w["f_w_up"][layer].rearrange("(k p) (h q n) -> p k h q n", p=P, h=2, n=UW)
                u0 = at.u
                for i, j in unit_groups(sp, u0, FFC, peel=1):
                    sp.wait_ge(unit_done, i * SLOTS + (u0 + j - SLOTS + 1))
                    slot = slot_of(u0, j)
                    src = up[:, :, j % 2, bass.ds(i * 2 + j // 2, 1), :].rearrange("p k a n -> p k (a n)")
                    sp.dma_start(ring[slot][:, :].rearrange("p (k c) -> p k c", k=DC), src).then_inc(w_full[slot], 16)
                at.u += FFC
                load_ln(3 * layer + 2)
                square(w["f_w_down"][layer], FFC // 2)
            load(24, cols(w["w_in_2"]))
            square(w["w_ret_out_2"], 8)
            load_gains(w["b_gate_2"][0, :], w["b_gate_2"][1, :])
            load(26, cols(w["w_in_2"], R_COLS))
            square(w["w_dil_out_2"], 2)
            square(w["w_o_2"], 4)
            load_gains(w["g_post_mix_2"], w["g_post_mlp_2"])
            load(16, cols(w["w_up_2"]))
            square(w["w_down_2"], 16)
            load_gains(w["b_ple_gate_2"], w["g_post_ple_2"])
            load(4, cols(w["w_ple_gate_2"]))
            square(w["w_ple_in_2"], 1)
            sp.wait_ge(resid_ready, TT * (3 * DEPTH + 3))
            sp.dma_start(out.rearrange("(t p) n -> p t n", p=P), resid[:, :, :]).then_inc(out_written, 16)
            sp.wait_ge(out_written, 16)

        @block.tensor
        def _(pe):
            at = At()

            def turn(blocks):
                r = at.r
                if r >= 2:
                    pe.wait_ge(turn_out[r % 2], r // 2)
                for j, x in enumerate(blocks):
                    n, m = x.shape[0], x.shape[1]
                    mm = nc.tensor.transpose(turn_bank(r)[0:m, j * P:j * P + n], x, ident[0:n, 0:n])
                mm.then_inc(turn_done, 1)
                at.r += 1

            def turn_wide(src, tt, chunks):
                for c in range(0, chunks, 4):
                    turn([src[:, tt, k * P:(k + 1) * P] for k in range(c, min(c + 4, chunks))])

            def turn_all(src, chunks):
                for tt in range(TT):
                    turn_wide(src, tt, chunks)

            def w_of(slot, kc, width):
                return ring[slot][:, 0:kc * width].rearrange("p (k c) -> p k c", k=kc)

            def mm_tok(v, x, wt, kc, c0, c1, b0):
                n = c1 - c0
                for tt in range(TT):
                    for k in range(kc):
                        mm = nc.tensor.matmul(step_bank(v)[:, b0 + tt * n:b0 + (tt + 1) * n], x[:, k, tt * P:(tt + 1) * P],
                                              wt[:, k, c0:c1], start=k == 0, stop=k == kc - 1)
                return mm

            def mm_feat(v, x, wt, kc, c0, c1, b0):
                for c in range(c0, c1, P):
                    b = b0 + (c - c0) // P * S
                    for k in range(kc):
                        mm = nc.tensor.matmul(step_bank(v)[:, b:b + S], wt[:, k, c:c + P], x[:, k, :],
                                              start=k == 0, stop=k == kc - 1)
                return mm

            def project(n, x, kind, kc=DC, width=UW, peel=0):
                u0, v0 = at.u, at.v
                for i, j in unit_groups(pe, u0, n, peel):
                    pe.wait_ge(w_full[slot_of(u0, j)], fills(u0, i, j))
                    if not (isinstance(i, int) and v0 + 4 * i + j < 2):
                        pe.wait_ge(step_out[(v0 + j) % 2], pairs_before(v0, i, j))
                    wt = w_of(slot_of(u0, j), kc, width)
                    if kind == "tok":
                        mm = mm_tok(v0 + j, x, wt, kc, 0, width, 0)
                    elif kind == "feat":
                        mm = mm_feat(v0 + j, x, wt, kc, 0, width, 0)
                    else:
                        mm_feat(v0 + j, x, wt, kc, 0, P, 0)
                        mm = mm_tok(v0 + j, x, wt, kc, P, width, S)
                    mm.then_inc(unit_done, 1)
                at.u += n
                at.v += n

            def gather(n, x, first=0, ready=None):
                for q in range(n):
                    slot = at.u % SLOTS
                    if ready:
                        ready(q)
                    pe.wait_ge(w_full[slot], fills(at.u, 0, 0))
                    wt = w_of(slot, 2, D)
                    for tt in range(TT):
                        for k in range(2):
                            for half in range(2):
                                mm = nc.tensor.matmul(acc_bank(tt, half), x[:, first + 2 * q + k, tt * P:(tt + 1) * P],
                                                      wt[:, k, half * 512:(half + 1) * 512],
                                                      start=q == 0 and k == 0, stop=q == n - 1 and k == 1)
                        if q == n - 1 and tt == 0:
                            mm.then_inc(acc_first, 1)
                    mm.then_inc(unit_done, 1)
                    at.u += 1

            def attend(a):
                n0 = at.n

                def scores(i):
                    n = n0 + i
                    if n >= 2:
                        pe.wait_ge(soft_done if a.mask else exp_done, n - 1)
                    for c0, c1, terms in a.scores(i):
                        for t, (l, r) in enumerate(terms):
                            mm = nc.tensor.matmul(a.s_bank(i)[:, c0:c1], l, r, start=t == 0, stop=t == len(terms) - 1)
                    mm.then_inc(scores_done, 1)

                def turn_probs(i):
                    n = n0 + i
                    pe.wait_ge(exp_done, n + 1)
                    if n >= 1 and a.wide:
                        pe.wait_ge(pt_out, n)
                    elif n >= 2:
                        pe.wait_ge(pt_out, n - 1)
                    for c in range(0, a.segs(i)[-1][1], P):
                        mm = nc.tensor.transpose(a.t_bank(i)[:, c:c + P], a.bufs(n)[1][:, c:c + P], ident[:, :])
                    mm.then_inc(pt_done, 1)

                def values(i):
                    n = n0 + i
                    pe.wait_ge(pt_out, n + 1)
                    if n >= 2:
                        pe.wait_ge(head_out, n - 1)
                    for c0, c1, terms in a.pv(i):
                        for t, (b, r) in enumerate(terms):
                            mm = nc.tensor.matmul(a.o_bank(i)[:, c0:c1], a.bufs(n)[2][:, b * P:(b + 1) * P], r,
                                                  start=t == 0, stop=t == len(terms) - 1)
                    mm.then_inc(pv_done, 1)

                scores(0)
                for i in range(a.count):
                    if i + 1 < a.count:
                        scores(i + 1)
                    turn_probs(i)
                    if i >= 1:
                        values(i - 1)
                values(a.count - 1)
                at.n += a.count

            def norm_turns():
                for tt in range(TT):
                    pe.wait_ge(normed_ready, at.nrm + tt + 1)
                    turn_wide(normed, tt, DC)
                at.nrm += TT
                wait_turns(pe, at.r)

            def output(n_units, source_ready=True):
                pe.wait_ge(head_out, at.n)
                turn_all(heads, DC)
                wait_turns(pe, at.r)
                gather(n_units, ht)

            pe.wait_ge(ident_in, 16)
            pe.wait_ge(mem_in, 16)
            turn_all(heads, DC)
            pe.wait_ge(rows_in, 16 * n_row_loads)
            turn([stage_rows[:, c, :] for c in range(4)])
            turn([stage_rows[0:min(P, PARAMS - c * P), c, :] for c in range(4, 8)])
            pe.wait_ge(x_in, 16)
            turn_all(resid, DC)
            wait_turn(pe, 3)
            wait_turn(pe, 2)
            project(4, ht, "feat")
            project(4, ht, "tok")

            for layer in range(DEPTH):
                kind = layer % 3
                if kind == 0:
                    if layer == 0:
                        wait_turns(pe, at.r)
                    project(6, xt, "tok")
                    for tt in range(TT):
                        pe.wait_ge(rot_out, at.rot + 2 * tt + 2)
                        turn_wide(tok(1536), tt, DC)
                        turn([k_dup[:, tt, h, :, :].rearrange("p e d -> p (e d)") for h in range(A_KV)])
                    at.rot += 2 * TT
                    wait_turns(pe, at.r)
                    wait_steps(pe, at.v)
                    attend(swa(layer // 3))
                    output(4)
                elif kind == 1:
                    project(8, xt, "feat")
                    wait_steps(pe, at.v)
                    u = part(1)
                    for gate in range(2):
                        slot = at.u % SLOTS
                        pe.wait_ge(w_full[slot], fills(at.u, 0, 0))
                        wt = w_of(slot, DC, UW)
                        for h in range(LRU_BLOCKS):
                            v = at.v
                            pe.wait_ge(step_out[v % 2], v // 2)
                            for c in range(2):
                                for k in range(2):
                                    mm = nc.tensor.matmul(step_bank(v)[:, c * S:(c + 1) * S], wt[:, 2 * h + k, c * P:(c + 1) * P],
                                                          u[:, 2 * h + k, :], start=k == 0, stop=k == 1)
                            mm.then_inc(gate_step if h < LRU_BLOCKS - 1 else unit_done, 1)
                            at.v += 1
                        at.u += 1
                    gather(4, ht, ready=lambda q: pe.wait_ge(lru_pool, 2 * q + 2))
                else:
                    project(2, xt, "tok")
                    project(1, xt, "tok", width=C_DOWN - 2 * UW)
                    pe.wait_ge(rot_out, at.rot + TT)
                    at.rot += TT
                    pe.wait_ge(mla_scaled, 1)
                    low = tok(C_DOWN)
                    for tt in range(TT):
                        turn([low[:, tt, c * P:(c + 1) * P] for c in range(4)])
                        turn([low[:, tt, 4 * P:5 * P], low[:, tt, 5 * P:5 * P + C_ROPE]])
                    wait_turns(pe, at.r)
                    project(8, ht, "both", kc=3, width=C_NOPE + C_ROPE)
                    project(8, ht[:, 3:5, :], "both", kc=2)
                    for tt in range(TT):
                        pe.wait_ge(rot_out, at.rot + tt + 1)
                        q_rope = mla_qr()
                        for h in range(0, C_HEADS, 4):
                            turn([q_rope[:, tt, h + m, :] for m in range(4)])
                    at.rot += TT
                    wait_turns(pe, at.r)
                    wait_steps(pe, at.v)
                    attend(mla())
                    output(4)
                norm_turns()
                project(4, xt, "feat")
                wait_steps(pe, at.v)
                attend(cross())
                output(4)
                norm_turns()
                project(FFC, xt, "feat", peel=1)
                gather(FFC // 2, ht, ready=lambda q: pe.wait_ge(glu_out, layer * (FFC // 2) + q + 1))
                if layer < DEPTH - 1:
                    norm_turns()
                else:
                    at.nrm += TT

            norm_turns()
            project(24, xt, "tok")
            ret = tok(R_COLS)
            for part_q in range(2):
                for tt in range(TT):
                    pe.wait_ge(rot_out, at.rot + 2)
                    at.rot += 2
                    turn_wide(ret[:, :, part_q * 1024:(part_q + 1) * 1024], tt, DC)
            wait_turns(pe, at.r)

            def ret_score(h):
                if h >= 2:
                    pe.wait_ge(ret_decayed, h - 1)
                for c0, c1, kb, q0 in ((0, S, 0, 0), (S, S + P, 1, P)):
                    for k in range(2):
                        mm = nc.tensor.matmul(bank[:, STEP + h % 2, c0:c1], kt[:, 2 * h + k, kb * P:(kb + 1) * P],
                                              qt[:, 2 * h + k, q0:S], start=k == 0, stop=k == 1)
                mm.then_inc(ret_scores, 1)

            wait_steps(pe, at.v)
            ret_score(0)
            for h in range(R_HEADS):
                if h + 1 < R_HEADS:
                    ret_score(h + 1)
                pe.wait_ge(ret_decayed, h + 1)
                if h >= 2:
                    pe.wait_ge(ret_norm, TT * (h - 1))
                for tt in range(TT):
                    for kb in range(tt + 1):
                        b = tt + kb
                        mm = nc.tensor.matmul(bank[:, ACC + 2 * (h % 2) + tt, :], probs_t[h % 2][:, b * P:(b + 1) * P],
                                              ret[:, kb, 2048 + h * R_V:2048 + (h + 1) * R_V], start=kb == 0, stop=kb == tt)
                    mm.then_inc(ret_pv, 1)
            pe.wait_ge(ret_norm, TT * R_HEADS)
            for tt in range(TT):
                turn_wide(ret[:, :, 4096:6144], tt, 16)
            wait_turns(pe, at.r)
            gather(8, ht)
            project(26, xt, "tok")
            dil = tok(D_COLS)
            for part_q in range(2):
                for tt in range(TT):
                    pe.wait_ge(rot_out, at.rot + 1)
                    at.rot += 1
                    turn_wide(dil[:, :, part_q * D_W:(part_q + 1) * D_W], tt, D_W // P)
            wait_turns(pe, at.r)
            wait_steps(pe, at.v)
            pe.wait_ge(branch_out, TT)
            attend(dilated())
            pe.wait_ge(head_out, at.n)
            turn_all(heads, 4)
            wait_turns(pe, at.r)
            gather(2, ht, first=24)
            for tt in range(TT):
                pe.wait_ge(mix_ready, tt + 1)
                turn_wide(heads, tt, DC)
            wait_turns(pe, at.r)
            gather(4, ht)
            norm_turns()
            project(16, xt, "feat")
            gather(16, ht, ready=lambda q: pe.wait_ge(relu_sq, q + 1))
            norm_turns()
            project(4, xt, "tok")
            pe.wait_ge(p_in, 16)
            turn([heads[:, tt, c * P:(c + 1) * P] for tt in range(TT) for c in range(2)])
            wait_turn(pe, at.r - 1)
            gather(1, ht)

        @block.scalar
        def _(act):
            at = At()
            links = [0]

            def link(ins):
                links[0] += 1
                ins.then_inc(act_link, 1)
                act.wait_ge(act_link, links[0])

            act.dma_start(ident[:, :], w["k_ident"]).then_inc(ident_in, 16)
            act.dma_start(heads[:, :, :], w["mem"].rearrange("(t p) n -> p t n", p=P)).then_inc(mem_in, 16)
            r = 0
            for name, rows in PARAM_ROWS:
                v = param_views[name]
                done = 0
                while done < rows:
                    k = min(rows - done, P - r % P)
                    act.dma_start(stage_rows[r % P:r % P + k, r // P, :], v[done:done + k, :]).then_inc(rows_in, 16)
                    r += k
                    done += k
            act.dma_start(resid[:, :, :], w["x"].rearrange("(t p) n -> p t n", p=P)).then_inc(x_in, 16)
            act.dma_start(rope_t[:, :, :, :], w["k_rope"].rearrange("(t p) e d -> p t e d", p=P)).then_inc(tables_in, 16)
            act.dma_start(mask_a[:, :], w["k_mask_a"]).then_inc(tables_in, 16)
            act.dma_start(mask_c[:, :], w["k_mask_c"]).then_inc(tables_in, 16)
            act.dma_start(sinks[:, :], w["a_sinks"].rearrange("a h -> (a h)").rearrange("(o n) -> o n", o=1).to_broadcast([P, 2 * A_HEADS])).then_inc(tables_in, 16)
            act.dma_start(freq[:, :], w["k_freq"].to_broadcast([P, NF])).then_inc(tables_in, 16)
            with nc.allow_non_contiguous_dma(reason="256 positions"):
                act.dma_start(pos_i[:, :], w["positions_2"].rearrange("(t p) -> p t", p=P)).then_inc(tables_in, 16)

            def turn_copy(dests):
                r = at.r
                if r % 2 == 0:
                    act.wait_ge(turn_done, r + 1)
                    for k, (dst, src, scale, bias) in enumerate(dests):
                        ins = nc.scalar.activation(dst, turn_bank(r)[0:dst.shape[0], src[0]:src[1]] if len(dst.shape) == 2 else
                                                   turn_bank(r)[0:dst.shape[0], src[0]:src[1]].rearrange("p (c s) -> p c s", s=P),
                                                   ACT.Identity if bias is not None else ACT.Copy,
                                                   **({"scale": scale} if scale is not None else {}), **({"bias": bias} if bias is not None else {}))
                    ins.then_inc(turn_out[0], 1)
                at.r += 1

            def step_copy(dest_of, n, peel=0):
                u0, v0 = at.u, at.v
                for i, j in unit_groups(act, u0, n, peel):
                    if (v0 + j) % 2 == 0:
                        act.wait_ge(unit_done, i * SLOTS + (u0 + j + 1))
                        for dst, c0, c1 in dest_of(i * SLOTS + j):
                            src = step_bank(v0 + j)[:, c0:c1]
                            if len(dst.shape) == 3:
                                src = src.rearrange("p (a b) -> p a b", a=dst.shape[1])
                            ins = nc.scalar.copy(dst, src)
                        ins.then_inc(step_out[0], 1)
                at.u += n
                at.v += n

            def attend(a):
                n0 = at.n

                def exps(i):
                    n = n0 + i
                    act.wait_ge(soft_done, n + 1)
                    if n >= 2:
                        act.wait_ge(pt_done, n - 1)
                    st = stat[n % 2]
                    segs = a.segs(i)
                    if a.sink:
                        nc.scalar.activation(st[:, 6:8], st[:, 2:4], ACT.Exp, bias=a.sink(i))
                    for t, (c0, c1) in enumerate(segs):
                        src = a.bufs(n)[0][:, c0:c1] if a.mask else a.s_bank(i)[:, c0:c1]
                        ins = nc.scalar.activation(a.bufs(n)[1][:, c0:c1], src, ACT.Exp, bias=st[:, 2 + t:3 + t],
                                                   scale=1.0 if a.mask else a.scale, accum_out=st[:, 4 + t:5 + t])
                    ins.then_inc(exp_done, 1)

                def copy_t(i):
                    n = n0 + i
                    act.wait_ge(pt_done, n + 1)
                    if n >= 2:
                        act.wait_ge(pv_done, n - 1)
                    nc.scalar.copy(a.bufs(n)[2][:, 0:a.segs(i)[-1][1]], a.t_bank(i)).then_inc(pt_out, 1)

                for i in range(a.count):
                    exps(i)
                    if a.wide:
                        if i >= 1:
                            copy_t(i - 1)
                    elif i >= 1:
                        copy_t(i - 1)
                copy_t(a.count - 1)
                at.n += a.count

            turns = for_turns(at, turn_copy)
            turns["setup"]()
            step_copy(lambda q: [(mem_kt[:, 2 * q:2 * q + 2, :], 0, 512)], 4)
            step_copy(lambda q: [(mem_v[:, :, q * UW:(q + 1) * UW], 0, 512)], 4)

            for layer in range(DEPTH):
                kind = layer % 3
                if kind == 0:
                    step_copy(lambda q: [(tok(1536)[:, :, q * UW:(q + 1) * UW], 0, 512)], 6)
                    turns["swa"]()
                    attend(swa(layer // 3))
                    turns["heads"]()
                    at.u += 4
                elif kind == 1:
                    gel, u, rg, ig, a_, b_ = (part(i) for i in range(6))
                    for q in range(8):
                        act.wait_ge(unit_done, at.u + 1)
                        bk = step_bank(at.v)
                        if q < 4:
                            nc.scalar.activation(gel[:, 2 * q:2 * q + 2, :], bk.rearrange("p (c s) -> p c s", s=S),
                                                 ACT.Gelu_apprx_tanh).then_inc(step_out[at.v % 2], 1)
                        else:
                            for c in range(2):
                                ch = 2 * (q - 4) + c
                                ins = nc.scalar.activation(u[:, ch, :], bk[:, c * S:(c + 1) * S], ACT.Identity,
                                                           bias=col("b_conv_b", ch), scale=col("b_conv_w", 3 * DC + ch))
                            ins.then_inc(lru_act, 1)
                        at.u += 1
                        at.v += 1
                    for gate, (dst, bias) in enumerate(((rg, "b_b_rgate"), (ig, "b_b_igate"))):
                        for h in range(LRU_BLOCKS):
                            if h < LRU_BLOCKS - 1:
                                act.wait_ge(gate_step, gate * (LRU_BLOCKS - 1) + h + 1)
                            else:
                                act.wait_ge(unit_done, at.u + 1)
                            for c in range(2):
                                ins = nc.scalar.activation(dst[:, 2 * h + c, :], step_bank(at.v)[:, c * S:(c + 1) * S],
                                                           ACT.Sigmoid, bias=col(bias, 2 * h + c))
                            ins.then_inc(step_out[at.v % 2], 1)
                            at.v += 1
                        at.u += 1
                    wait_steps(act, at.v)
                    act.wait_ge(lru_dve, LRU_SP)
                    for ch in range(DC):
                        nc.scalar.activation(a_[:, ch, :], rg[:, ch, :], ACT.Exp, scale=softplus[:, 5, ch:ch + 1])
                    for ch in range(DC):
                        ins = nc.scalar.activation(b_[:, ch, :], rg[:, ch, :], ACT.Tanh, scale=softplus[:, 5, ch:ch + 1])
                    ins.then_inc(lru_act, 1)
                    act.wait_ge(lru_dve, LRU_SP + 1)
                    nc.scalar.activation(rg[:, :, :], b_[:, :, :], ACT.Sqrt).then_inc(lru_act, 1)
                    at.u += 4
                else:
                    low = tok(C_DOWN)
                    step_copy(lambda q: [(low[:, :, q * UW:(q + 1) * UW], 0, 512)], 2)
                    step_copy(lambda q: [(low[:, :, 2 * UW:C_DOWN], 0, 2 * (C_DOWN - 2 * UW))], 1)
                    wait_steps(act, at.v)
                    for tt in range(TT):
                        for t, (c0, c1) in enumerate(((0, C_QR), (C_QR, C_QR + C_KVR))):
                            k = at.col + 2 * tt + t
                            ins = nc.scalar.activation((masked, probs)[tt][t][:, 0:c1 - c0], low[:, tt, c0:c1], ACT.Square,
                                                       accum_out=ssq[:, k:k + 1])
                    ins.then_inc(ssq_ready, 1)
                    at.col += 4
                    at.sq += 1
                    turns["mla_low"]()
                    step_copy(lambda q: [(qt[:, q, :], 0, S), (mla_qr()[:, :, q, :], S, S + 2 * C_ROPE)], 8)
                    step_copy(lambda q: [(kt[:, q, :], 0, S), (mla_v()[:, :, q * P:(q + 1) * P], S, 2 * S)], 8)
                    turns["mla_q"]()
                    attend(mla())
                    turns["heads"]()
                    at.u += 4
                at.col += TT
                turns["norm"](lambda c, n=3 * layer: (col("ln_g", n * DC + c), col("ln_b", n * DC + c)))
                step_copy(lambda q: [(qt[:, 2 * q:2 * q + 2, :], 0, 512)], 4)
                attend(cross())
                turns["heads"]()
                at.u += 4
                at.col += TT
                turns["norm"](lambda c, n=3 * layer + 1: (col("ln_g", n * DC + c), col("ln_b", n * DC + c)))
                u0, v0 = at.u, at.v
                for i, j in unit_groups(act, u0, FFC, peel=1):
                    par, role = j // 2, j % 2
                    act.wait_ge(unit_done, i * SLOTS + (u0 + j + 1))
                    if not (isinstance(i, int) and layer == 0 and 2 * i + par < 2):
                        act.wait_ge(glu_out, i * 2 + (layer * (FFC // 2) + par - 1))
                    for c in range(2):
                        ch = i * 4 + (2 * par + c + role * FFC)
                        ins = nc.scalar.activation(cwork[par][role][:, c, :], step_bank(v0 + j)[:, c * S:(c + 1) * S], ACT.Identity,
                                                   bias=params[:, bass.ds(ch + (COL["f_conv_b"] + layer * 2 * FFC), 1)],
                                                   scale=params[:, bass.ds(ch + (COL["f_conv_w"] + (layer * 3 + 2) * 2 * FFC), 1)])
                    ins.then_inc(conv_start, 1)
                    if role == 1:
                        act.wait_ge(step_out[(v0 + j - 1) % 2], pairs_before(v0, i, j - 1) + 1)
                        nc.scalar.activation(swork[par][:, :, :], cwork[par][0][:, :, :], ACT.Silu).then_inc(glu_gate, 1)
                at.u += FFC
                at.v += FFC
                at.u += FFC // 2
                at.col += TT
                if layer < DEPTH - 1:
                    turns["norm"](lambda c, n=3 * layer + 2: (col("ln_g", n * DC + c), col("ln_b", n * DC + c)))

            def squares(src_of, wait_of, n=TT):
                for tt in range(n):
                    wait_of(tt)
                    nc.scalar.activation(normed[:, tt, :], src_of(tt), ACT.Square,
                                         accum_out=ssq[:, at.col:at.col + 1]).then_inc(ssq_ready, 1)
                    at.col += 1
                    at.sq += 1

            act.wait_ge(head_out, at.n)
            act.dma_start(mask_d, w["k_mask_d"]).then_inc(tables2_in, 16)
            act.dma_start(decay, w["k_decay"]).then_inc(tables2_in, 16)
            act.wait_ge(resid_ready, TT * 3 * DEPTH)
            squares(lambda tt: resid[:, tt, :], lambda tt: None)
            turns["norm"](lambda c: (col("g_pre_mix_2", c), None))
            act.wait_ge(angle_ready, 1)
            nc.scalar.activation(angles[:, 1, :, :], angles[:, 0, :, :], ACT.Sin)
            nc.scalar.activation(angles[:, 2, :, :], angles[:, 0, :, :], ACT.Sin, scale=0.5).then_inc(trig_ready, 1)
            ret = tok(R_COLS)
            step_copy(lambda q: [(ret[:, :, bass.ds(q * UW, UW)], 0, 512)], 24)
            turns["ret_qk"]()
            wait_steps(act, at.v)
            for tt in range(TT):
                ins = nc.scalar.activation(ret[:, tt, 4096:6144], ret[:, tt, 4096:6144], ACT.Silu)
            ins.then_inc(gate_sig, 1)
            for h in range(R_HEADS):
                for tt in range(TT):
                    if h:
                        act.wait_ge(ssq_ready, at.sq - 1)
                    act.wait_ge(ret_pv, TT * h + tt + 1)
                    nc.scalar.activation(masked[tt][:, 0:512], bank[:, ACC + 2 * (h % 2) + tt, :], ACT.Square,
                                         accum_out=ssq[:, at.col:at.col + 1]).then_inc(ssq_ready, 1)
                    at.col += 1
                    at.sq += 1
            turns["ret_out"]()
            at.u += 8
            dil = tok(D_COLS)
            step_copy(lambda q: [(dil[:, :, bass.ds(q * UW, UW)], 0, 512)], 26)
            turns["dil_qk"]()
            attend(dilated())
            turns["dil_out"]()
            act.wait_ge(gate_in, 1)
            for tt in range(TT):
                ins = nc.scalar.activation(dil[:, tt, 3 * D_W:D_COLS], dil[:, tt, 3 * D_W:D_COLS], ACT.Sigmoid)
            ins.then_inc(gate_sig, 1)
            at.u += 2
            turns["heads"]()
            at.u += 4

            def post_squares():
                squares(acc_tile, lambda tt: act.wait_ge(acc_first, at.acc) if tt == 0 else act.wait_ge(unit_done, at.u))

            def pre_squares(k):
                squares(lambda tt: resid[:, tt, :], lambda tt: act.wait_ge(resid_ready, TT * (3 * DEPTH + k) + tt + 1))

            at.acc = 3 * DEPTH + 3
            post_squares()
            pre_squares(0)
            turns["norm"](lambda c: (col("g_pre_mlp_2", c), None))
            u0, v0 = at.u, at.v
            for i, j in unit_groups(act, u0, 16, peel=1):
                act.wait_ge(unit_done, i * SLOTS + (u0 + j + 1))
                if not (isinstance(i, int) and 4 * i + j < 2):
                    act.wait_ge(relu_sq, i * SLOTS + (j - 1))
                nc.scalar.activation(cwork[0][j % 2][:, :, :], step_bank(v0 + j).rearrange("p (c s) -> p c s", s=S),
                                     ACT.Relu).then_inc(step_out[(v0 + j) % 2], 1)
            at.u += 16
            at.v += 16
            at.u += 16
            at.acc += 1
            post_squares()
            pre_squares(1)
            act.wait_ge(pv_done, at.n)
            act.wait_ge(turn_done, at.r)
            act.dma_start(heads[:, :, 0:2 * P], w["p_2"].rearrange("(t p) n -> p t n", p=P)).then_inc(p_in, 16)
            turns["norm"](lambda c: (col("g_pre_ple_2", c), None))
            step_copy(lambda q: [(tok(D)[:, :, q * UW:(q + 1) * UW], 0, 512)], 4)
            turns["p"]()
            at.u += 1
            act.wait_ge(ple_in, 1)
            nc.scalar.activation(tok(D), tok(D), ACT.Sigmoid).then_inc(ple_sig, 1)
            for tt in range(TT):
                act.wait_ge(ple_prod, tt + 1)
                nc.scalar.activation(normed[:, tt, :], heads[:, tt, :], ACT.Square,
                                     accum_out=ssq[:, at.col:at.col + 1]).then_inc(ssq_ready, 1)
                at.col += 1

        @block.vector
        def _(dve):
            at = At()
            links = [0]
            v_ = nc.vector

            def mark(ins):
                links[0] += 1
                ins.then_inc(dve_link, 1)
                return links[0]

            def link(ins):
                dve.wait_ge(dve_link, mark(ins))

            def turn_copy(dests):
                r = at.r
                if r % 2 == 1:
                    dve.wait_ge(turn_done, r + 1)
                    for dst, src, scale, bias in dests:
                        s = turn_bank(r)[0:dst.shape[0], src[0]:src[1]]
                        if len(dst.shape) == 3:
                            s = s.rearrange("p (c s) -> p c s", s=P)
                        if scale is None:
                            ins = v_.tensor_copy(dst, s)
                        elif bias is None:
                            ins = v_.tensor_scalar(dst, s, scale, None, ALU.mult)
                        else:
                            ins = v_.tensor_scalar(dst, s, scale, bias, ALU.mult, ALU.add)
                    ins.then_inc(turn_out[1], 1)
                at.r += 1

            def step_copy(dest_of, n, peel=0):
                u0, v0 = at.u, at.v
                for i, j in unit_groups(dve, u0, n, peel):
                    if (v0 + j) % 2 == 1:
                        dve.wait_ge(unit_done, i * SLOTS + (u0 + j + 1))
                        for dst, c0, c1 in dest_of(i * SLOTS + j):
                            src = step_bank(v0 + j)[:, c0:c1]
                            if len(dst.shape) == 3:
                                src = src.rearrange("p (a b) -> p a b", a=dst.shape[1])
                            ins = v_.tensor_copy(dst, src)
                        ins.then_inc(step_out[1], 1)
                at.u += n
                at.v += n

            def rotate(rows, cos, sin, dests):
                k = at.rot
                n, half = rows.shape[1], rows.shape[3]
                c = rot_c_view(k, n, half)
                s = rot_s_view(k, n, half)
                if k >= 2:
                    dve.wait_ge(rot_out, k - 1)
                link(v_.tensor_tensor(c, rows, bcast(cos, n, half), ALU.mult))
                dve.wait_ge(rot_sin, k + 1)
                ins = None
                for (a, b), outs in dests:
                    for e, op in ((0, ALU.subtract), (1, ALU.add)):
                        x, y = c[:, a:b, e, :], s[:, a:b, 1 - e, :]
                        o = outs[e]
                        if len(o.shape) == 4:
                            x = x.unsqueeze(2).to_broadcast([P, b - a, o.shape[2], half])
                            y = y.unsqueeze(2).to_broadcast([P, b - a, o.shape[2], half])
                        ins = v_.tensor_tensor(o, x, y, op)
                ins.then_inc(rot_out, 1)
                at.rot += 1

            def attend(a):
                n0 = at.n

                def soft(i):
                    n = n0 + i
                    st = stat[n % 2]
                    segs = a.segs(i)
                    ns = len(segs)
                    dve.wait_ge(scores_done, n + 1)
                    if n >= 2:
                        dve.wait_ge(exp_done, n - 1)
                    if a.mask:
                        src = a.bufs(n)[0][:, 0:segs[-1][1]]
                        link(v_.scalar_tensor_tensor(out=src, in0=a.s_bank(i), scalar=a.scale, in1=a.mask(i),
                                                     op0=ALU.mult, op1=ALU.add))
                    else:
                        src = a.s_bank(i)
                    for t, (c0, c1) in enumerate(segs):
                        ins = v_.reduce_max(st[:, t:t + 1], src[:, c0:c1], AX.X)
                        if t < ns - 1:
                            pass
                    link(ins)
                    if a.sink:
                        ins = v_.tensor_scalar(st[:, 2:2 + ns], st[:, 0:ns], a.sink(i), -1.0, ALU.max, ALU.mult)
                    else:
                        ins = v_.tensor_scalar(st[:, 2:2 + ns], st[:, 0:ns], -1.0 if a.mask else -a.scale, None, ALU.mult)
                    ins.then_inc(soft_done, 1)

                def denominators(i):
                    n = n0 + i
                    st = stat[n % 2]
                    ns = len(a.segs(i))
                    dve.wait_ge(exp_done, n + 1)
                    den = st[:, 4:4 + ns]
                    if a.sink:
                        den = st[:, 8:8 + ns]
                        link(v_.tensor_tensor(den, st[:, 4:4 + ns], st[:, 6:6 + ns], ALU.add))
                    link(v_.reciprocal(st[:, 10:10 + ns], den))

                def heads_out(i):
                    n = n0 + i
                    st = stat[n % 2]
                    dst = a.dest(i)
                    t, wd = dst.shape[1], dst.shape[2]
                    dve.wait_ge(pv_done, n + 1)
                    v_.tensor_tensor(dst, a.o_bank(i)[:, 0:t * wd].rearrange("p (t c) -> p t c", t=t),
                                     st[:, 10:10 + t].unsqueeze(2).to_broadcast([P, t, wd]), ALU.mult).then_inc(head_out, 1)

                for i in range(a.count):
                    soft(i)
                    if i >= 2:
                        heads_out(i - 2)
                    if i >= 1:
                        denominators(i - 1)
                if a.count >= 2:
                    heads_out(a.count - 2)
                denominators(a.count - 1)
                heads_out(a.count - 1)
                at.n += a.count

            def wait_acc(tt):
                if tt == 0:
                    at.acc += 1
                    dve.wait_ge(acc_first, at.acc)
                else:
                    dve.wait_ge(unit_done, at.u)

            def layer_norm():
                n = at.nrm
                for tt in range(TT):
                    wait_acc(tt)
                    if n == 0:
                        dve.wait_ge(x_in, 16)
                        dve.wait_ge(turn_done, 10)
                    else:
                        dve.wait_ge(resid_ready, TT * (n - 1) + tt + 1)
                    ks = []
                    for half in range(2):
                        h = slice(half * 512, (half + 1) * 512)
                        ks.append(mark(v_.scalar_tensor_tensor(out=resid[:, tt, h], in0=resid[:, tt, h], scalar=ALPHA,
                                                               in1=acc_bank(tt, half), op0=ALU.mult, op1=ALU.add)))
                    for half in range(2):
                        dve.wait_ge(dve_link, ks[half])
                        k = mark(v_.bn_stats(bn[:, tt, half, :], resid[:, tt, half * 512:(half + 1) * 512]))
                    dve.wait_ge(dve_link, k)
                    link(v_.bn_aggr(bn_mv[:, tt, :], bn[:, tt, :, :].rearrange("p a b -> p (a b)")))
                    v_.tensor_scalar(var[:, at.col + tt:at.col + tt + 1], bn_mv[:, tt, 1:2], LN_EPS, None, ALU.add).then_inc(var_ready, 1)
                for tt in range(TT):
                    at.msq += 1
                    dve.wait_ge(rstd_ready, at.msq)
                    k = at.col + tt
                    v_.tensor_scalar(normed[:, tt, :], resid[:, tt, :], bn_mv[:, tt, 0:1], rstd[:, k:k + 1],
                                     ALU.subtract, ALU.mult).then_inc(normed_ready, 1)
                at.col += TT
                at.nrm += 1

            def mean_square(width, n=1):
                at.sq += 1
                dve.wait_ge(ssq_ready, at.sq)
                v_.tensor_scalar(var[:, at.col:at.col + n], ssq[:, at.col:at.col + n], 1.0 / width, RMS_EPS,
                                 ALU.mult, ALU.add).then_inc(var_ready, 1)
                at.msq += 1
                at.col += n

            turns = for_turns(at, turn_copy)
            turns["setup"]()
            step_copy(lambda q: [(mem_kt[:, 2 * q:2 * q + 2, :], 0, 512)], 4)
            step_copy(lambda q: [(mem_v[:, :, q * UW:(q + 1) * UW], 0, 512)], 4)
            dve.wait_ge(tables_in, 16 * 6)
            link(v_.tensor_copy(pos_f[:, :], pos_i[:, :]))
            for tt in range(TT):
                k = mark(v_.tensor_scalar(angles[:, 0, tt, :], freq[:, :], pos_f[:, tt:tt + 1], None, ALU.mult))
            dve.wait_ge(dve_link, k)
            link(v_.tensor_scalar(angles[:, 1, :, :], angles[:, 0, :, :], 1.0 / TWO_PI, ROUND, ALU.mult, ALU.add))
            link(v_.tensor_scalar(angles[:, 1, :, :], angles[:, 1, :, :], -ROUND, None, ALU.add))
            for c in (PI_1, PI_2, PI_3):
                link(v_.scalar_tensor_tensor(out=angles[:, 0, :, :], in0=angles[:, 1, :, :], scalar=-c, in1=angles[:, 0, :, :],
                                             op0=ALU.mult, op1=ALU.add))
            v_.tensor_scalar(angles[:, 0, :, :], angles[:, 0, :, :], 3.1415925, -3.1415925, ALU.min, ALU.max).then_inc(angle_ready, 1)

            for layer in range(DEPTH):
                kind = layer % 3
                if kind == 0:
                    qkv = tok(1536)
                    step_copy(lambda q: [(qkv[:, :, q * UW:(q + 1) * UW], 0, 512)], 6)
                    wait_steps(dve, at.v)
                    for tt in range(TT):
                        rows = in_rows(qkv[:, tt, 0:A_HEADS * A_HD], A_HEADS, A_HD // 2)
                        rotate(rows, rope_t[:, tt, 0, :], rope_t[:, tt, 1, :], [((0, A_HEADS), [rows[:, :, e, :] for e in range(2)])])
                        rows = in_rows(qkv[:, tt, A_HEADS * A_HD:], A_KV, A_HD // 2)
                        rotate(rows, rope_t[:, tt, 0, :], rope_t[:, tt, 1, :],
                               [((0, A_KV), [k_dup[:, tt, :, :, e * 32:(e + 1) * 32] for e in range(2)])])
                    turns["swa"]()
                    attend(swa(layer // 3))
                    turns["heads"]()
                    at.u += 4
                elif kind == 1:
                    gel, u, rg, ig, a_, b_ = (part(i) for i in range(6))
                    lam = params[:, COL["b_lambda"]:COL["b_lambda"] + DC]
                    sp0, sp1, sp2, sp3, sp4, sp5 = (softplus[:, i, :] for i in range(6))
                    link(v_.tensor_scalar(sp0, lam, -1.0, None, ALU.mult))
                    link(v_.tensor_tensor(sp1, sp0, lam, ALU.min))
                    v_.tensor_scalar(sp5, sp0, 0.0, None, ALU.max).then_inc(lru_dve, 1)
                    for q in range(8):
                        if q >= 4:
                            dve.wait_ge(lru_act, q - 3)
                            bk = step_bank(at.v)
                            for sh in range(1, LRU_TAPS):
                                for c in range(2):
                                    ch = 2 * (q - 4) + c
                                    ins = v_.scalar_tensor_tensor(out=u[:, ch, sh:S], in0=bk[:, c * S:(c + 1) * S - sh],
                                                                  scalar=col("b_conv_w", (3 - sh) * DC + ch), in1=u[:, ch, sh:S],
                                                                  op0=ALU.mult, op1=ALU.add)
                                    if sh < LRU_TAPS - 1:
                                        k = mark(ins)
                                if sh < LRU_TAPS - 1:
                                    dve.wait_ge(dve_link, k)
                            ins.then_inc(step_out[at.v % 2], 1)
                        at.u += 1
                        at.v += 1
                    dve.wait_ge(lru_pool_exp, 1)
                    link(v_.tensor_scalar(sp0, sp2, 2.0, None, ALU.add))
                    link(v_.reciprocal(sp3, sp0))
                    link(v_.tensor_tensor(sp0, sp2, sp3, ALU.mult))
                    link(v_.tensor_tensor(sp1, sp0, sp0, ALU.mult))
                    link(v_.tensor_scalar(sp3, sp1, 1.0 / 17, 1.0 / 15, ALU.mult, ALU.add))
                    for k in range(13, 0, -2):
                        link(v_.tensor_tensor(sp3, sp3, sp1, ALU.mult))
                        link(v_.tensor_scalar(sp3, sp3, 1.0 / k, None, ALU.add))
                    link(v_.tensor_tensor(sp3, sp3, sp0, ALU.mult))
                    link(v_.scalar_tensor_tensor(out=sp5, in0=sp3, scalar=2.0, in1=sp5, op0=ALU.mult, op1=ALU.add))
                    v_.tensor_scalar(sp5, sp5, -LRU_C, None, ALU.mult).then_inc(lru_dve, 1)
                    at.u += 2
                    at.v += 2 * LRU_BLOCKS
                    dve.wait_ge(lru_act, 5)
                    wait_steps(dve, at.v)
                    link(v_.tensor_tensor(ig[:, :, :], ig[:, :, :], u[:, :, :], ALU.mult))
                    link(v_.tensor_tensor(u[:, :, :], a_[:, :, :], a_[:, :, :], ALU.mult))
                    link(v_.tensor_scalar(u[:, :, :], u[:, :, :], -1.0, -1.0, ALU.mult, ALU.add))
                    v_.tensor_tensor(b_[:, :, :], b_[:, :, :], u[:, :, :], ALU.mult).then_inc(lru_dve, 1)
                    dve.wait_ge(lru_act, 6)
                    link(v_.tensor_tensor(b_[:, :, :], rg[:, :, :], ig[:, :, :], ALU.mult))
                    for ch in range(DC):
                        v_.tensor_tensor_scan(u[:, ch, :], a_[:, ch, :], b_[:, ch, :], 0.0, ALU.mult, ALU.add).then_inc(lru_dve, 1)
                    at.u += 4
                else:
                    low = tok(C_DOWN)
                    step_copy(lambda q: [(low[:, :, q * UW:(q + 1) * UW], 0, 512)], 2)
                    step_copy(lambda q: [(low[:, :, 2 * UW:C_DOWN], 0, 2 * (C_DOWN - 2 * UW))], 1)
                    wait_steps(dve, at.v)
                    for tt in range(TT):
                        rows = low[:, tt, C_QR + C_KVR:C_DOWN].rearrange("p (h e d) -> p h e d", e=2, d=C_ROPE // 2)
                        rotate(rows, rope_t[:, tt, 0, :], rope_t[:, tt, 1, :], [((0, 1), [rows[:, :, e, :] for e in range(2)])])
                    at.sq += 1
                    dve.wait_ge(ssq_ready, at.sq)
                    for t, width in enumerate((C_QR, C_KVR)):
                        ins = v_.tensor_scalar(var[:, at.col + t:at.col + 4:2], ssq[:, at.col + t:at.col + 4:2], 1.0 / width, RMS_EPS,
                                               ALU.mult, ALU.add)
                    ins.then_inc(var_ready, 1)
                    at.msq += 1
                    dve.wait_ge(rstd_ready, at.msq)
                    for tt in range(TT):
                        for t, (c0, c1) in enumerate(((0, C_QR), (C_QR, C_QR + C_KVR))):
                            k = at.col + 2 * tt + t
                            ins = v_.tensor_scalar(low[:, tt, c0:c1], low[:, tt, c0:c1], rstd[:, k:k + 1], None, ALU.mult)
                    ins.then_inc(mla_scaled, 1)
                    at.col += 4
                    turns["mla_low"]()
                    step_copy(lambda q: [(qt[:, q, :], 0, S), (mla_qr()[:, :, q, :], S, S + 2 * C_ROPE)], 8)
                    wait_steps(dve, at.v)
                    for tt in range(TT):
                        rows = mla_qr()[:, tt, :, :].rearrange("p h (e d) -> p h e d", e=2)
                        rotate(rows, rope_t[:, tt, 0, :], rope_t[:, tt, 1, :], [((0, C_HEADS), [rows[:, :, e, :] for e in range(2)])])
                    step_copy(lambda q: [(kt[:, q, :], 0, S), (mla_v()[:, :, q * P:(q + 1) * P], S, 2 * S)], 8)
                    turns["mla_q"]()
                    attend(mla())
                    turns["heads"]()
                    at.u += 4
                layer_norm()
                turns["norm"](lambda c, n=3 * layer: (col("ln_g", n * DC + c), col("ln_b", n * DC + c)))
                step_copy(lambda q: [(qt[:, 2 * q:2 * q + 2, :], 0, 512)], 4)
                attend(cross())
                turns["heads"]()
                at.u += 4
                layer_norm()
                turns["norm"](lambda c, n=3 * layer + 1: (col("ln_g", n * DC + c), col("ln_b", n * DC + c)))
                u0, v0 = at.u, at.v
                for i, j in unit_groups(dve, u0, FFC, peel=1):
                    par, role = j // 2, j % 2
                    dve.wait_ge(conv_start, i * SLOTS + (layer * FFC + j + 1))
                    bk = step_bank(v0 + j)
                    for sh in (1, 2):
                        for c in range(2):
                            ch = i * 4 + (2 * par + c + role * FFC)
                            dst = cwork[par][role][:, c, sh:S]
                            if sh == 2 and c == 0:
                                dve.wait_ge(conv_tap, i * SLOTS + (layer * FFC + j + 1))
                            ins = v_.scalar_tensor_tensor(out=dst, in0=bk[:, c * S:(c + 1) * S - sh],
                                                          scalar=params[:, bass.ds(ch + (COL["f_conv_w"] + (layer * 3 + 2 - sh) * 2 * FFC), 1)],
                                                          in1=dst, op0=ALU.mult, op1=ALU.add)
                        ins.then_inc(conv_tap if sh == 1 else step_out[(v0 + j) % 2], 1)
                at.u += FFC
                at.v += FFC
                at.u += FFC // 2
                layer_norm()
                if layer < DEPTH - 1:
                    turns["norm"](lambda c, n=3 * layer + 2: (col("ln_g", n * DC + c), col("ln_b", n * DC + c)))

            def pre_norm():
                for tt in range(TT):
                    mean_square(D)
                for tt in range(TT):
                    k = at.col - TT + tt
                    dve.wait_ge(rstd_ready, at.msq - TT + tt + 1)
                    v_.tensor_scalar(normed[:, tt, :], resid[:, tt, :], rstd[:, k:k + 1], None, ALU.mult).then_inc(normed_ready, 1)

            def post_norm(gain, src_of):
                for tt in range(TT):
                    mean_square(D)
                for tt in range(TT):
                    k = at.col - TT + tt
                    dve.wait_ge(rstd_ready, at.msq - TT + tt + 1)
                    link(v_.scalar_tensor_tensor(out=normed[:, tt, :], in0=src_of(tt), scalar=rstd[:, k:k + 1], in1=gain,
                                                 op0=ALU.mult, op1=ALU.mult))
                    v_.tensor_tensor(resid[:, tt, :], resid[:, tt, :], normed[:, tt, :], ALU.add).then_inc(resid_ready, 1)

            pre_norm()
            turns["norm"](lambda c: (col("g_pre_mix_2", c), None))
            dve.wait_ge(trig_ready, 1)
            link(v_.tensor_tensor(angles[:, 2, :, :], angles[:, 2, :, :], angles[:, 2, :, :], ALU.mult))
            v_.tensor_scalar(angles[:, 2, :, :], angles[:, 2, :, :], -2.0, 1.0, ALU.mult, ALU.add).then_inc(trig_ready, 1)
            dve.wait_ge(trig_ready, 2)
            ret = tok(R_COLS)
            step_copy(lambda q: [(ret[:, :, bass.ds(q * UW, UW)], 0, 512)], 24)
            wait_steps(dve, at.v)
            half = R_QK // 2
            for pq in range(2):
                for tt in range(TT):
                    for hh in range(0, R_HEADS, 2):
                        c = pq * 1024 + hh * R_QK
                        rows = ret[:, tt, c:c + 2 * R_QK].rearrange("p (h e d) -> p h e d", e=2, d=half)
                        rotate(rows, angles[:, 2, tt, 0:half], angles[:, 1, tt, 0:half], [((0, 2), [rows[:, :, e, :] for e in range(2)])])
            turns["ret_qk"]()
            dve.wait_ge(tables2_in, 32)
            for h in range(R_HEADS):
                def decayed(h):
                    dve.wait_ge(ret_scores, h + 1)
                    if h >= 2:
                        dve.wait_ge(ret_pv, TT * (h - 1))
                    v_.tensor_tensor(probs_t[h % 2][:, 0:3 * P], bank[:, STEP + h % 2, 0:3 * P], decay[:, h, :], ALU.mult).then_inc(ret_decayed, 1)
                if h == 0:
                    decayed(0)
                if h + 1 < R_HEADS:
                    decayed(h + 1)
                for tt in range(TT):
                    mean_square(R_V)
                if h == 0:
                    dve.wait_ge(gate_sig, 1)
                for tt in range(TT):
                    k = at.col - TT + tt
                    dve.wait_ge(rstd_ready, at.msq - TT + tt + 1)
                    g = ret[:, tt, 4096 + h * R_V:4096 + (h + 1) * R_V]
                    v_.scalar_tensor_tensor(out=g, in0=bank[:, ACC + 2 * (h % 2) + tt, :], scalar=rstd[:, k:k + 1], in1=g,
                                            op0=ALU.mult, op1=ALU.mult).then_inc(ret_norm, 1)
            turns["ret_out"]()
            at.u += 8
            for tt in range(TT):
                wait_acc(tt)
                v_.tensor_copy(normed[:, tt, :], acc_tile(tt)).then_inc(branch_out, 1)
            dil = tok(D_COLS)
            step_copy(lambda q: [(dil[:, :, bass.ds(q * UW, UW)], 0, 512)], 26)
            wait_steps(dve, at.v)
            rh = D_ROT // 2
            for pq in range(2):
                for tt in range(TT):
                    rows = dil[:, tt, pq * D_W:(pq + 1) * D_W].rearrange("p (h d) -> p h d", d=D_HD)[:, :, 0:D_ROT].rearrange("p h (e d) -> p h e d", e=2)
                    rotate(rows, angles[:, 2, tt, half:NF], angles[:, 1, tt, half:NF], [((0, D_W // D_HD), [rows[:, :, e, :] for e in range(2)])])
            turns["dil_qk"]()
            gb = 3 * DEPTH
            dve.wait_ge(gains_in, 32 * (gb + 1))
            for tt in range(TT):
                g = dil[:, tt, 3 * D_W:D_COLS]
                ins = v_.tensor_tensor(g, g, gains[:, :, :].rearrange("p a n -> p (a n)"), ALU.add)
            ins.then_inc(gate_in, 1)
            attend(dilated())
            turns["dil_out"]()
            at.u += 2
            dve.wait_ge(gate_sig, 2)
            for tt in range(TT):
                wait_acc(tt)
                link(v_.tensor_tensor(normed[:, tt, :], normed[:, tt, :], dil[:, tt, 3 * D_W:3 * D_W + D], ALU.mult))
                link(v_.tensor_tensor(heads[:, tt, :], acc_tile(tt), dil[:, tt, 3 * D_W + D:D_COLS], ALU.mult))
                v_.tensor_tensor(heads[:, tt, :], heads[:, tt, :], normed[:, tt, :], ALU.add).then_inc(mix_ready, 1)
            turns["heads"]()
            at.u += 4
            gp = gb + 1
            dve.wait_ge(gains_in, 32 * (gp + 1))
            at.acc += 1
            post_norm(gains[:, 0, :], acc_tile)
            pre_norm()
            turns["norm"](lambda c: (col("g_pre_mlp_2", c), None))
            u0, v0 = at.u, at.v
            for i, j in unit_groups(dve, u0, 16, peel=1):
                src = cwork[0][j % 2][:, :, :]
                dve.wait_ge(step_out[(v0 + j) % 2], pairs_before(v0, i, j) + 1)
                v_.tensor_tensor(ht[:, bass.ds(i * 8 + 2 * j, 2), :], src, src, ALU.mult).then_inc(relu_sq, 1)
            at.u += 16
            at.v += 16
            at.u += 16
            at.acc += 1
            post_norm(gains[:, 1, :], acc_tile)
            pre_norm()
            turns["norm"](lambda c: (col("g_pre_ple_2", c), None))
            step_copy(lambda q: [(tok(D)[:, :, q * UW:(q + 1) * UW], 0, 512)], 4)
            turns["p"]()
            wait_steps(dve, at.v)
            ge = gb + 2
            dve.wait_ge(gains_in, 32 * (ge + 1))
            for tt in range(TT):
                ins = v_.tensor_tensor(tok(D)[:, tt, :], tok(D)[:, tt, :], gains[:, 0, :], ALU.add)
            ins.then_inc(ple_in, 1)
            at.u += 1
            dve.wait_ge(ple_sig, 1)
            for tt in range(TT):
                wait_acc(tt)
                v_.tensor_tensor(heads[:, tt, :], acc_tile(tt), tok(D)[:, tt, :], ALU.mult).then_inc(ple_prod, 1)
            post_norm(gains[:, 1, :], lambda tt: heads[:, tt, :])

        @block.gpsimd
        def _(pool):
            at = At()
            links = [0]
            g_ = nc.gpsimd

            def link(ins):
                links[0] += 1
                ins.then_inc(pool_link, 1)
                pool.wait_ge(pool_link, links[0])

            def powers(n=1):
                pool.wait_ge(var_ready, at.msq + 1)
                g_.tensor_tensor(rstd[:, at.col:at.col + n], var[:, at.col:at.col + n], minus_half[:, 0:n], ALU.pow).then_inc(rstd_ready, 1)
                at.msq += 1
                at.col += n

            def layer_norm():
                n = at.nrm
                for tt in range(TT):
                    powers()
                pool.wait_ge(gains_in, 32 * (n + 1))
                ga = gains
                for tt in range(TT):
                    pool.wait_ge(normed_ready, TT * n + tt + 1)
                    link(g_.tensor_tensor(resid[:, tt, :], normed[:, tt, :], ga[:, 0, :], ALU.mult))
                    g_.tensor_tensor(resid[:, tt, :], resid[:, tt, :], ga[:, 1, :], ALU.add).then_inc(resid_ready, 1)
                pool.wait_ge(resid_ready, TT * (n + 1))
                pool.sem_inc(gains_used, 1)
                at.nrm += 1

            def rotate(rows, sin):
                k = at.rot
                n, half = rows.shape[1], rows.shape[3]
                if k >= 2:
                    pool.wait_ge(rot_out, k - 1)
                g_.tensor_tensor(rot_s_view(k, n, half), rows, bcast(sin, n, half), ALU.mult).then_inc(rot_sin, 1)
                at.rot += 1

            link(g_.memset(minus_half[:, :], -0.5))
            at.v += 8
            pool.wait_ge(tables_in, 16 * 6)
            for layer in range(DEPTH):
                kind = layer % 3
                if kind == 0:
                    at.v += 6
                    wait_steps(pool, at.v)
                    for tt in range(TT):
                        qkv = tok(1536)
                        rotate(in_rows(qkv[:, tt, 0:A_HEADS * A_HD], A_HEADS, A_HD // 2), rope_t[:, tt, 1, :])
                        rotate(in_rows(qkv[:, tt, A_HEADS * A_HD:], A_KV, A_HD // 2), rope_t[:, tt, 1, :])
                elif kind == 1:
                    pool.wait_ge(lru_dve, 1)
                    link(g_.memset(softplus[:, 4, :], float(np.e)))
                    g_.tensor_tensor(softplus[:, 2, :], softplus[:, 4, :], softplus[:, 1, :], ALU.pow).then_inc(lru_pool_exp, 1)
                    at.v += 8 + 2 * LRU_BLOCKS
                    gel, u = part(0), part(1)
                    for ch in range(DC):
                        pool.wait_ge(lru_dve, LRU_SP + 2 + ch)
                        g_.tensor_tensor(ht[:, ch, :], u[:, ch, :], gel[:, ch, :], ALU.mult).then_inc(lru_pool, 1)
                else:
                    at.v += 3
                    wait_steps(pool, at.v)
                    low = tok(C_DOWN)
                    for tt in range(TT):
                        rotate(low[:, tt, C_QR + C_KVR:C_DOWN].rearrange("p (h e d) -> p h e d", e=2, d=C_ROPE // 2), rope_t[:, tt, 1, :])
                    powers(4)
                    at.v += 8
                    wait_steps(pool, at.v)
                    for tt in range(TT):
                        rotate(mla_qr()[:, tt, :, :].rearrange("p h (e d) -> p h e d", e=2), rope_t[:, tt, 1, :])
                    at.v += 8
                layer_norm()
                at.v += 4
                layer_norm()
                u0, v0 = SLOTS, at.v
                for i, j in unit_groups(pool, u0, FFC, peel=1):
                    if j % 2 == 1:
                        par = j // 2
                        pool.wait_ge(glu_gate, i * 2 + (layer * (FFC // 2) + par + 1))
                        pool.wait_ge(step_out[(v0 + j) % 2], pairs_before(v0, i, j) + 1)
                        g_.tensor_tensor(ht[:, bass.ds(i * 4 + 2 * par, 2), :], swork[par][:, :, :], cwork[par][1][:, :, :],
                                         ALU.mult).then_inc(glu_out, 1)
                at.v += FFC
                layer_norm()
            for tt in range(TT):
                powers()
            pool.wait_ge(trig_ready, 2)
            at.v += 24
            wait_steps(pool, at.v)
            ret = tok(R_COLS)
            half = R_QK // 2
            for pq in range(2):
                for tt in range(TT):
                    for hh in range(0, R_HEADS, 2):
                        c = pq * 1024 + hh * R_QK
                        rotate(ret[:, tt, c:c + 2 * R_QK].rearrange("p (h e d) -> p h e d", e=2, d=half), angles[:, 1, tt, 0:half])
            for h in range(R_HEADS):
                for tt in range(TT):
                    powers()
            at.v += 26
            wait_steps(pool, at.v)
            dil = tok(D_COLS)
            for pq in range(2):
                for tt in range(TT):
                    rows = dil[:, tt, pq * D_W:(pq + 1) * D_W].rearrange("p (h d) -> p h d", d=D_HD)[:, :, 0:D_ROT].rearrange("p h (e d) -> p h e d", e=2)
                    rotate(rows, angles[:, 1, tt, half:NF])
            pool.wait_ge(gate_in, 1)
            pool.sem_inc(gains_used, 1)
            for _ in range(5):
                for tt in range(TT):
                    powers()
                if _ == 2:
                    pool.wait_ge(resid_ready, TT * (3 * DEPTH + 2))
                    pool.sem_inc(gains_used, 1)


def kernel(**inputs):
    import concourse.bacc as bacc
    from concourse.bass_utils import run_bass_kernel_spmd as run

    nc = bacc.Bacc("TRN2", target_bir_lowering=False, num_devices=1, dynamic_dma_scratch_size=1024)
    arrays, args = {}, {}
    for name, value in {**inputs, **shape_constants()}.items():
        a = np.ascontiguousarray(value)
        a = a.reshape(LAYOUT[name]) if name in LAYOUT else a
        arrays[f"in_{name}"] = a
        args[name] = nc.dram_tensor(f"in_{name}", a.shape, mybir.dt.from_np(a.dtype), kind="ExternalInput").ap()
    out = nc.dram_tensor("out", (S, D), F32, kind="ExternalOutput").ap()
    build(nc, args, out)
    r = run(nc, [arrays], core_ids=[0])
    return r.results[0]["out"].reshape(1, S, D)
```

```python
from contextlib import ExitStack

import numpy as np

import concourse.bass as bass
from concourse import mybir

F32 = mybir.dt.float32
F32R = mybir.dt.float32r
I32 = mybir.dt.int32
ALU = mybir.AluOpType
ACT = mybir.ActivationFunctionType
AX = mybir.AxisListType

P = 128
S = 256
D = 1024
DEPTH = 4
TT = S // P
DC = D // P
SLOTS = 4
AHEAD = 2
HC = 16
UW = 256
NEG = -1e30
LN_EPS = 1e-5
RMS_EPS = 1e-6
ALPHA = (2.0 * DEPTH) ** 0.25

A_HEADS, A_KV, A_HD = 16, 4, 64
LRU_BLOCKS, LRU_TAPS, LRU_C = 4, 4, 8.0
C_HEADS, C_NOPE, C_ROPE, C_QR, C_KVR = 8, 128, 64, 384, 256
C_DOWN = C_QR + C_KVR + C_ROPE
X_HEADS, X_HD = 4, 256
FF, FFC, F_TAPS = 2816, 22, 3
FF2 = 4096
R_HEADS, R_QK, R_V = 4, 256, 512
D_SLOTS, D_GROUPS, D_HD, D_ROT = 8, ((128, 1), (512, 4), (2048, 16)), 64, 16
D_W = D_SLOTS * len(D_GROUPS) * D_HD
R_COLS = 2 * R_HEADS * R_QK + 2 * R_HEADS * R_V
D_COLS = 3 * D_W + 2 * D
NF = R_QK // 2 + D_ROT // 2
TWO_PI = 2 * np.pi
PI_1 = 6.28125
PI_2 = 2029 / 2.0**20
PI_3 = TWO_PI - PI_1 - PI_2
ROUND = 12582912.0
LRU_SP = 2

PARAM_ROWS = [
    ("ln_g", 96), ("ln_b", 96), ("f_conv_w", 528), ("f_conv_b", 176), ("b_conv_w", 32), ("b_conv_b", 8),
    ("b_b_rgate", 8), ("b_b_igate", 8), ("b_lambda", 8), ("c_q_norm", 3), ("c_kv_norm", 2),
    ("g_pre_mix_2", 8), ("g_pre_mlp_2", 8), ("g_pre_ple_2", 8),
]
COL = {}
_at = 0
for _name, _rows in PARAM_ROWS:
    COL[_name] = _at
    _at += _rows
PARAMS = _at

ACC, STEP, TURN = 0, 4, 6


def shape_constants():
    f = np.float32
    inv = f(1.0) / (f(10000.0) ** (np.arange(0, A_HD, 2, dtype=f) / f(A_HD)))
    ang = np.arange(S, dtype=f)[:, None] * inv[None, :]
    rope = np.stack([np.cos(ang), np.sin(ang)], 1).astype(f)
    q = np.arange(P)[:, None]
    k = np.arange(P)[None, :]
    causal = np.where(q >= k, 0.0, NEG)
    window = np.where(k > q, 0.0, NEG)
    mask_a = np.concatenate([causal, window, causal], 1)
    mask_c = np.concatenate([causal, np.zeros((P, P)), causal], 1)
    parts = []
    for tt in range(TT):
        for span, dil in D_GROUPS:
            dist = q + tt * P - np.arange((tt + 1) * P)[None, :]
            parts.append(np.where((dist >= 0) & (dist % dil == 0) & (dist <= span), 0.0, NEG))
    mask_d = np.concatenate(parts, 1)
    log_gamma = np.log1p(-(2.0 ** (-5.0 - np.arange(R_HEADS))))
    diff = np.arange(S)[None, :] - np.arange(P)[:, None]
    dec = np.where(diff[None] >= 0, np.exp(np.maximum(diff, 0)[None] * log_gamma[:, None, None]), 0.0) * R_QK**-0.5
    dec = np.concatenate([dec, dec[:, :, :P]], 2).transpose(1, 0, 2)
    fr = f(1.0) / (f(10000.0) ** np.linspace(0.0, 1.0, R_QK // 2, dtype=f))
    fd = f(500000.0) ** (-np.arange(0, D_ROT, 2, dtype=f) / f(D_ROT))
    return {
        "k_ident": np.eye(P, dtype=f), "k_rope": rope, "k_mask_a": mask_a.astype(f), "k_mask_c": mask_c.astype(f),
        "k_mask_d": mask_d.astype(f), "k_decay": np.ascontiguousarray(dec.astype(f)),
        "k_freq": np.concatenate([fr, fd]).astype(f)[None, :],
    }


LAYOUT = {
    "x": (S, D), "mem": (S, D), "p_2": (S, 256), "positions_2": (S,), "w_in_2": (D, R_COLS + D_COLS), "b_gate_2": (2, D),
    "w_ret_out_2": (R_HEADS * R_V, D), "w_dil_out_2": (D_SLOTS * D_HD, D), "w_o_2": (D, D), "g_pre_mix_2": (D,),
    "g_post_mix_2": (D,), "g_pre_mlp_2": (D,), "g_post_mlp_2": (D,), "w_up_2": (D, FF2), "w_down_2": (FF2, D),
    "g_pre_ple_2": (D,), "w_ple_gate_2": (D, D), "b_ple_gate_2": (D,), "w_ple_in_2": (256, D), "g_post_ple_2": (D,),
}


def build(nc, w, out):
    param_views = {}
    for name, rows in PARAM_ROWS:
        v = w[name]
        axes = "abcd"[:len(v.shape) - 1]
        names = " ".join(axes)
        param_views[name] = v.rearrange(f"{names} (c f) -> ({names} c) f", f=P)
    n_row_loads = 0
    _r = 0
    for name, rows in PARAM_ROWS:
        n_row_loads += (_r + rows - 1) // P - _r // P + 1
        _r += rows
    with ExitStack() as ctx:
        sb = lambda name, shape, dt=F32: ctx.enter_context(nc.sbuf_tensor(name, shape, dt))
        sem = lambda name: ctx.enter_context(nc.semaphore(name))

        ring = [sb(f"ring{i}", [P, 2048]) for i in range(SLOTS)]
        w_hi = [sb(f"w_hi{i}", [P, 2, 1024], F32R) for i in range(2)]
        w_lo = [sb(f"w_lo{i}", [P, 2, 1024], F32R) for i in range(2)]
        resid = sb("resid", [P, TT, D])
        work = sb("work", [P, 9216])
        heads = sb("heads", [P, TT, D])
        qt = sb("qt", [P, DC, S])
        kt = sb("kt", [P, DC, S])
        mem_kt = sb("mem_kt", [P, DC, S])
        mem_v = sb("mem_v", [P, TT, D])
        gains = sb("gains", [P, 2, D])
        params = sb("params", [P, PARAMS])
        ident = sb("ident", [P, P])
        rope_t = sb("rope_t", [P, TT, 2, A_HD // 2])
        mask_a = sb("mask_a", [P, 3 * P])
        mask_c = sb("mask_c", [P, 3 * P])
        sinks = sb("sinks", [P, 2 * A_HEADS])
        stat = [sb(f"stat{i}", [P, 12]) for i in range(2)]
        var = sb("var", [P, 96])
        rstd = sb("rstd", [P, 96])
        ssq = sb("ssq", [P, 96])
        bn = sb("bn", [P, TT, 2, 6])
        bn_mv = sb("bn_mv", [P, TT, 2])
        minus_half = sb("minus_half", [P, 4])
        softplus = sb("softplus", [P, 6, DC])
        angles = sb("angles", [P, 3, TT, NF])
        pos_i = sb("pos_i", [P, TT], I32)
        pos_f = sb("pos_f", [P, TT])
        freq = sb("freq", [P, NF])
        align = 32
        x_at = (nc.sbuf_base + align - 1) // align * align
        h_at = x_at + 2 * DC * S * 4
        sb("parts_region", [P, 2 * (DC + HC) * S + align])
        at_byte = lambda name, shape, dt, byte: nc.alloc_sbuf_tensor_at(name, shape, dt, offset=byte)
        xt = [at_byte(f"xt_{n}", [P, DC, S], F32R, x_at + i * DC * S * 4) for i, n in enumerate(("hi", "lo"))]
        ht = [at_byte(f"ht_{n}", [P, HC, S], F32R, h_at + i * HC * S * 4) for i, n in enumerate(("hi", "lo"))]
        xt_plain = at_byte("xt_plain", [P, 2 * DC * S], F32, x_at)
        ht_plain = at_byte("ht_plain", [P, 2 * HC * S], F32, h_at)
        bank = ctx.enter_context(nc.psum_tensor("bank", [P, 8, 512], F32))

        tok_at = lambda first, cols: work[:, first:first + TT * cols].rearrange("p (t c) -> p t c", t=TT)
        tok = lambda cols: tok_at(0, cols)
        part = lambda i: work[:, i * 2048:(i + 1) * 2048].rearrange("p (c s) -> p c s", s=S)
        normed = tok_at(7168, D)
        heads_feat = heads[:, :, :].rearrange("p t f -> p (t f)").rearrange("p (c s) -> p c s", s=S)
        flat_heads = heads[:, :, :].rearrange("p t f -> p (t f)")
        stage_rows = work[:, 0:1024].rearrange("p (a f) -> p a f", f=P)
        k_dup = work[:, 4096:4096 + TT * A_KV * P].rearrange("p (t h e d) -> p t h e d", t=TT, h=A_KV, e=2)
        mla_qr = lambda: work[:, 2048:2048 + TT * C_HEADS * C_ROPE].rearrange("p (t h d) -> p t h d", t=TT, h=C_HEADS)
        mla_v = lambda: tok_at(4096, D)
        q_rope_t = ht_plain[0:C_ROPE, 2048:4096].rearrange("p (h s) -> p h s", s=S)
        k_rope_t = ht_plain[0:C_ROPE, 5632:5632 + S]
        dil_qk = ht_plain[:, 0:2 * D_W // P * S].rearrange("p (c s) -> p c s", s=S)
        masked = [xt_plain[:, i * 512:(i + 1) * 512] for i in range(2)]
        probs = [xt_plain[:, 1024 + i * 512:1536 + i * 512] for i in range(2)]
        probs_t = [xt_plain[:, 2048 + i * 512:2560 + i * 512] for i in range(2)]
        ret_pt = [flat_heads[:, i * 512:(i + 1) * 512] for i in range(2)]
        ret_junk = [flat_heads[:, 1024 + i * 512:1536 + i * 512] for i in range(2)]

        def in_rows(flat, n, half):
            return flat[:, 0:n * 2 * half].rearrange("p (h e d) -> p h e d", e=2, d=half)

        rot_c_view = lambda k, n, half: in_rows(heads[:, k % 2, :], n, half)
        rot_s_view = lambda k, n, half: in_rows(ht_plain[:, 6144 + k % 2 * 1024:7168 + k % 2 * 1024], n, half)

        def bcast(table, n, half):
            return table.unsqueeze(1).unsqueeze(1).to_broadcast([P, n, 2, half])

        def flat2(x):
            return x[:, :, :].rearrange("p c s -> p (c s)")

        wide_bufs = [[x[:, i * 768:(i + 1) * 768] for i in range(2)] for x in (flat2(qt), flat2(kt), xt_plain)]
        pair_view = lambda first: work[:, first:first + 512].rearrange("p (c s) -> p c s", s=S)
        cwork = [[pair_view((2 * i + j) * 512) for j in range(2)] for i in range(2)]
        swork = [pair_view(2048 + i * 512) for i in range(2)]
        pwork = [pair_view(3072 + i * 512) for i in range(2)]
        mask_d = flat2(mem_kt)[:, 0:9 * P]
        decay = flat2(mem_v)[:, 0:R_HEADS * 3 * P].rearrange("p (h c) -> p h c", h=R_HEADS)

        w_full = [sem(f"w_full{i}") for i in range(SLOTS)]
        halves_used = sem("halves_used")
        split_hi, split_lo = sem("split_hi"), sem("split_lo")
        turn_hi, scaled_out = sem("turn_hi"), sem("scaled_out")
        glu_hi, glu_prod = sem("glu_hi"), sem("glu_prod")
        relu_prod, relu_hi = sem("relu_prod"), sem("relu_hi")
        lru_uhi, lru_ulo, lru_hi, lru_lo = (sem(n) for n in ("lru_uhi", "lru_ulo", "lru_hi", "lru_lo"))
        acc_first = sem("acc_first")
        gate_step = sem("gate_step")
        step_out = [sem("step_out0"), sem("step_out1")]
        turn_done = sem("turn_done")
        turn_out = [sem("turn_out0"), sem("turn_out1")]
        ident_in, x_in, mem_in, rows_in, tables_in = (sem(n) for n in ("ident_in", "x_in", "mem_in", "rows_in", "tables_in"))
        tables2_in, p_in, out_written = sem("tables2_in"), sem("p_in"), sem("out_written")
        gains_in = sem("gains_in")
        gains_used = sem("gains_used")
        half_set = sem("half_set")
        var_ready, rstd_ready, ssq_ready = sem("var_ready"), sem("rstd_ready"), sem("ssq_ready")
        normed_ready, resid_ready = sem("normed_ready"), sem("resid_ready")
        dve_link, act_link, pool_link = sem("dve_link"), sem("act_link"), sem("pool_link")
        scores_done, soft_done, exp_done, pt_done, pt_out, pv_done, head_out = (
            sem(n) for n in ("scores_done", "soft_done", "exp_done", "pt_done", "pt_out", "pv_done", "head_out"))
        conv_start, conv_tap, glu_gate, glu_out = (sem(n) for n in ("conv_start", "conv_tap", "glu_gate", "glu_out"))
        rot_cos, rot_sin, rot_out = sem("rot_cos"), sem("rot_sin"), sem("rot_out")
        lru_act, lru_dve, lru_pool, lru_pool_exp = (sem(n) for n in ("lru_act", "lru_dve", "lru_pool", "lru_pool_exp"))
        mla_sq, mla_scaled = sem("mla_sq"), sem("mla_scaled")
        ret_scores, ret_decayed, ret_pv, ret_norm = (sem(n) for n in ("ret_scores", "ret_decayed", "ret_pv", "ret_norm"))
        relu_out, relu_sq = sem("relu_out"), sem("relu_sq")
        angle_ready, trig_ready = sem("angle_ready"), sem("trig_ready")
        branch_out, gate_in, gate_sig, mix_ready = (sem(n) for n in ("branch_out", "gate_in", "gate_sig", "mix_ready"))
        ple_in, ple_sig, ple_prod = sem("ple_in"), sem("ple_sig"), sem("ple_prod")
        block = ctx.enter_context(nc.Block())

        lru_parts = (qt[:, :, :], kt[:, :, :], part(0), part(1), part(2), heads_feat)
        p_tok = tok_at(4096, 256)

        class At:

            def __init__(self):
                self.u = self.v = self.r = self.n = self.rot = self.msq = self.col = self.sq = self.nrm = self.acc = self.th = self.sc = self.pair = self.relu = 0

        FULL = (1024, 1024)
        mixer_units = [[FULL] * 10, [FULL] * 14, [FULL] * 2 + [(4 * 192,) * 2] + [(192, 384)] * 8 + [(256, 256)] * 8 + [FULL] * 4]
        unit_sizes = [FULL] * 8
        for layer in range(DEPTH):
            unit_sizes += mixer_units[layer % 3] + [FULL] * (8 + FFC + FFC // 2)
        unit_sizes += [FULL] * (24 + 8 + 26 + 2 + 4 + 16 + 16 + 4 + 1)
        N_UNITS = len(unit_sizes)

        def unit_half(i, ub, h):
            sizes = unit_sizes[4 * i + ub] if isinstance(i, int) else FULL
            return sizes[h], h * sizes[0]

        def unit_groups(eng, u0, n, peel=0, loops=3):
            full = n // SLOTS
            start = full if (u0 < SLOTS or full - peel < loops) else peel
            for i in range(start):
                for j in range(SLOTS):
                    yield i, j
            if start < full:
                with eng.Fori(start, full) as i:
                    for j in range(SLOTS):
                        yield i, j
            for j in range(n - SLOTS * full):
                yield full, j

        GLU_LAG, RELU_LAG = HC // 2, HC // 2
        N_GLU, N_RELU = FFC // 2, FF2 // UW

        def interleave(n, lag):
            order = []
            for q in range(n):
                order.append(("down", q))
                if q + lag < n:
                    order.append(("up", q + lag))
            return order

        glu_order, relu_order = interleave(N_GLU, GLU_LAG), interleave(N_RELU, RELU_LAG)

        def slot_of(u0, j):
            return (u0 + j) % SLOTS

        def fills(u0, i, j):
            return i * 16 + 16 * ((u0 + j) // SLOTS + 1)

        def pairs_before(v0, i, j):
            return i * 2 + (v0 + j) // 2

        def wait_step(eng, v):
            eng.wait_ge(step_out[v % 2], v // 2 + 1)

        def wait_turn(eng, r):
            eng.wait_ge(turn_out[r % 2], r // 2 + 1)

        def wait_turns(eng, r_end):
            wait_turn(eng, r_end - 1)
            wait_turn(eng, r_end - 2)

        def wait_steps(eng, v_end):
            wait_step(eng, v_end - 1)
            wait_step(eng, v_end - 2)

        def step_bank(v):
            return bank[:, STEP + v % 2, :]

        def turn_bank(r):
            return bank[:, TURN + r % 2, :]

        def acc_bank(tt, half):
            return bank[:, ACC + 2 * tt + half, :]

        def acc_tile(tt):
            return bank[:, ACC + 2 * tt:ACC + 2 * tt + 2, :].rearrange("p a b -> p (a b)")

        def for_turns(at, copy, split, scaled):

            def wide(how, dst, chunks, tts=range(TT), base=0):
                for tt in tts:
                    for c in range(0, chunks, 4):
                        m = min(4, chunks - c)
                        at_c = (slice(None), slice(base + c, base + c + m), slice(tt * P, (tt + 1) * P))
                        if how is copy:
                            copy([(dst[at_c], (0, m * P))])
                        else:
                            split(dst[0][at_c], dst[1][at_c], m)

            def setup():
                wide(split, ht, DC)
                copy([(params[:, 0:4 * P], (0, 4 * P))])
                copy([(params[:, 4 * P:PARAMS], (0, PARAMS - 4 * P))])
                wide(split, xt, DC)

            def swa_turns():
                for tt in range(TT):
                    wide(copy, qt, DC, [tt])
                    wide(copy, kt, A_KV, [tt])

            def norm(gain):
                for tt in range(TT):
                    for c in range(0, DC, 4):
                        t = slice(tt * P, (tt + 1) * P)
                        scaled([(heads_feat[:, c + k, t], (k * P, (k + 1) * P), *gain(c + k)) for k in range(4)],
                               heads_feat[:, c:c + 4, t], xt[0][:, c:c + 4, t], xt[1][:, c:c + 4, t])

            def mla_low():
                for tt in range(TT):
                    t = slice(tt * P, (tt + 1) * P)
                    scaled([(heads_feat[:, c, t], (c * P, (c + 1) * P), col("c_q_norm", c) if c < 3 else col("c_kv_norm", 0), None)
                            for c in range(4)], heads_feat[:, 0:4, t], ht[0][:, 0:4, t], ht[1][:, 0:4, t])
                    scaled([(k_rope_t[:, t], (P, 2 * P), None, None), (heads_feat[:, 4, t], (0, P), col("c_kv_norm", 1), None)],
                           heads_feat[:, 4, t], ht[0][:, 4, t], ht[1][:, 4, t])

            def mla_q():
                for tt in range(TT):
                    for h in range(0, C_HEADS, 4):
                        copy([(q_rope_t[:, h:h + 4, tt * P:(tt + 1) * P], (0, 4 * P))])

            def ret_qk():
                for dst in (qt, kt):
                    wide(copy, dst, DC)

            def dil_turns():
                for pq in range(2):
                    wide(copy, dil_qk, D_W // P, base=pq * (D_W // P))

            def p_turn():
                for tt in range(TT):
                    split(ht[0][:, 0:2, tt * P:(tt + 1) * P], ht[1][:, 0:2, tt * P:(tt + 1) * P], 2)

            return {"setup": setup, "swa": swa_turns, "heads": lambda: wide(split, ht, DC), "norm": norm, "mla_low": mla_low,
                    "mla_q": mla_q, "ret_qk": ret_qk, "ret_out": lambda: wide(split, ht, 2 * DC), "dil_qk": dil_turns,
                    "dil_out": lambda: wide(split, ht, 4), "p": p_turn}

        col = lambda name, i: params[:, COL[name] + i:COL[name] + i + 1]

        class Attention:
            def __init__(self, count, segs, scale, mask, sink, scores, pv, dest, wide=False):
                self.count, self.segs, self.scale, self.mask, self.sink = count, segs, scale, mask, sink
                self.scores, self.pv, self.dest, self.wide = scores, pv, dest, wide

            def bufs(self, n):
                return [x[n % 2] for x in (wide_bufs if self.wide else (masked, probs, probs_t))]

            def s_bank(self, i):
                n = self.segs(i)[-1][1]
                if self.wide:
                    return bank[:, ACC + 2 * (i % 2):ACC + 2 * (i % 2) + 2, :].rearrange("p a b -> p (a b)")[:, 0:n]
                return bank[:, ACC + i % 2, 0:n]

            def t_bank(self, i):
                n = self.segs(i)[-1][1]
                if self.wide:
                    return bank[:, STEP:STEP + 2, :].rearrange("p a b -> p (a b)")[:, 0:n]
                return bank[:, ACC + 2 + i % 2, 0:n]

            def o_bank(self, i):
                return bank[:, (TURN if self.wide else STEP) + i % 2, :]

        causal_segs = lambda i: [(0, P), (P, 3 * P)]

        def swa(layer):
            qkv = tok(1536)

            def scores(h):
                o, kv = h % 2 * A_HD, h // (A_HEADS // A_KV)
                return [(c0, c1, [(qt[o:o + A_HD, h // 2, tt * P:(tt + 1) * P], kt[o:o + A_HD, kv, 0:c1 - c0])])
                        for tt, (c0, c1) in enumerate(causal_segs(h))]

            def pv(h):
                at = (A_HEADS + A_KV + h // (A_HEADS // A_KV)) * A_HD
                v = [qkv[:, kb, at:at + A_HD] for kb in range(TT)]
                return [(0, A_HD, [(0, v[0])]), (A_HD, 2 * A_HD, [(1, v[0]), (2, v[1])])]

            return Attention(A_HEADS, causal_segs, A_HD**-0.5, lambda i: mask_a[:, :],
                             lambda i: sinks[:, layer * A_HEADS + i:layer * A_HEADS + i + 1], scores, pv,
                             lambda i: heads[:, :, i * A_HD:(i + 1) * A_HD])

        def mla():
            v_tok = mla_v()

            def scores(h):
                return [(c0, c1, [(qt[:, h, tt * P:(tt + 1) * P], kt[:, h, 0:c1 - c0]),
                                  (q_rope_t[:, h, tt * P:(tt + 1) * P], k_rope_t[:, 0:c1 - c0])])
                        for tt, (c0, c1) in enumerate(causal_segs(h))]

            def pv(h):
                v = [v_tok[:, kb, h * P:(h + 1) * P] for kb in range(TT)]
                return [(0, P, [(0, v[0])]), (P, 2 * P, [(1, v[0]), (2, v[1])])]

            return Attention(C_HEADS, causal_segs, (C_NOPE + C_ROPE) ** -0.5, lambda i: mask_c[:, :], None, scores, pv,
                             lambda i: heads[:, :, i * P:(i + 1) * P])

        def cross():
            segs = lambda i: [(0, S), (S, 2 * S)]

            def scores(h):
                return [(c0, c1, [(qt[:, 2 * h + c, tt * P:(tt + 1) * P], mem_kt[:, 2 * h + c, :]) for c in range(2)])
                        for tt, (c0, c1) in enumerate(segs(h))]

            def pv(h):
                v = [mem_v[:, kb, h * X_HD:(h + 1) * X_HD] for kb in range(TT)]
                return [(0, X_HD, [(0, v[0]), (1, v[1])]), (X_HD, 2 * X_HD, [(2, v[0]), (3, v[1])])]

            return Attention(X_HEADS, segs, X_HD**-0.5, None, None, scores, pv,
                             lambda i: heads[:, :, i * X_HD:(i + 1) * X_HD])

        def dilated():
            v_tok = tok_at(2 * TT * D_W, D_W)
            n_g = len(D_GROUPS)
            width = lambda i: (i % TT + 1) * P

            def scores(i):
                s, tt, kw = i // TT, i % TT, width(i)
                mms = []
                for g in range(n_g):
                    head = g * D_SLOTS + s
                    o = head % 2 * D_HD
                    mms.append((g * kw, (g + 1) * kw, [(dil_qk[o:o + D_HD, head // 2, tt * P:(tt + 1) * P],
                                                        dil_qk[o:o + D_HD, D_W // P + head // 2, 0:kw])]))
                return mms

            def pv(i):
                s, tt = i // TT, i % TT
                terms = []
                for g in range(n_g):
                    at = (g * D_SLOTS + s) * D_HD
                    terms += [(g * (tt + 1) + kb, v_tok[:, kb, at:at + D_HD]) for kb in range(tt + 1)]
                return [(0, D_HD, terms)]

            return Attention(D_SLOTS * TT, lambda i: [(0, n_g * width(i))], D_HD**-0.5,
                             lambda i: mask_d[:, 0:n_g * P] if i % TT == 0 else mask_d[:, n_g * P:9 * P], None, scores, pv,
                             lambda i: heads[:, i % TT:i % TT + 1, i // TT * D_HD:(i // TT + 1) * D_HD], wide=True)

        @block.sync
        def _(sp):
            at = At()

            def load(n, src, dst=lambda slot: ring[slot][:, :].rearrange("p (k c) -> p k c", k=DC)):
                u0 = at.u
                for i, j in unit_groups(sp, u0, n):
                    if isinstance(i, int) and u0 + 4 * i + j < SLOTS:
                        pass
                    else:
                        sp.wait_ge(split_lo, i * (2 * SLOTS) + 2 * (u0 + j - SLOTS + 1))
                    slot = slot_of(u0, j)
                    sp.dma_start(dst(slot), src(i * SLOTS + j)).then_inc(w_full[slot], 16)
                at.u += n

            def cols(mat, first=0, width=UW, kc=DC):
                view = mat.rearrange("(k p) n -> p k n", p=P)
                return lambda q: view[:, :, bass.ds(q * width + first, width)]

            def packed(kc, width):
                return lambda slot: ring[slot][:, 0:kc * width].rearrange("p (k c) -> p k c", k=kc)

            def rows(mat):
                view = mat.rearrange("(u k p) n -> p u k n", p=P, k=2)
                return lambda q: view[:, bass.ds(q, 1), :, :].rearrange("p a k n -> p (a k) n")

            def load_gains(first, second):
                g = at.nrm
                if g >= 1:
                    sp.wait_ge(gains_used, g)
                for h, row in enumerate((first, second)):
                    sp.dma_start(gains[:, h, :], row.rearrange("(a n) -> a n", a=1).to_broadcast([P, D])).then_inc(gains_in, 16)
                at.nrm += 1

            def square(mat, n_units):
                load(n_units, rows(mat), packed(2, D))

            def load_ln(n):
                load_gains(w["ln_g"][n // 3, n % 3, :], w["ln_b"][n // 3, n % 3, :])

            load(8, cols(w["mem_w_kv"]))
            for layer in range(DEPTH):
                kind, j = layer % 3, layer // 3
                if kind == 0:
                    load(6, cols(w["a_w_qkv"][j]))
                    load_ln(3 * layer)
                    square(w["a_w_o"][j], 4)
                elif kind == 1:
                    load(8, cols(w["b_w_in"][j]))
                    for name in ("b_w_rgate", "b_w_igate"):
                        v = w[name][j].rearrange("h (k p) n -> p (h k) n", p=P)
                        load(1, lambda q, v=v: v)
                    load_ln(3 * layer)
                    square(w["b_w_o"][j], 4)
                else:
                    load(2, cols(w["c_w_down"][j]))
                    load(1, cols(w["c_w_down"][j], 2 * UW, C_DOWN - 2 * UW), packed(DC, C_DOWN - 2 * UW))
                    load(8, cols(w["c_w_uq"][j], 0, C_NOPE + C_ROPE), packed(3, C_NOPE + C_ROPE))
                    load(8, cols(w["c_w_ukv"][j]), packed(2, UW))
                    load_ln(3 * layer)
                    square(w["c_w_o"][j], 4)
                load(4, cols(w["x_w_q"][layer]))
                load_ln(3 * layer + 1)
                square(w["x_w_o"][layer], 4)
                up = w["f_w_up"][layer].rearrange("(k p) (h q n) -> p k h q n", p=P, h=2, n=UW)
                down = w["f_w_down"][layer].rearrange("(u k p) n -> p u k n", p=P, k=2)

                def load_up(i, ub, q, role):
                    slot = ub % SLOTS
                    sp.wait_ge(split_lo, i * (2 * SLOTS) + 2 * (ub - SLOTS + 1))
                    src = up[:, :, role, bass.ds(q, 1), :].rearrange("p k a n -> p k (a n)")
                    sp.dma_start(ring[slot][:, :].rearrange("p (k c) -> p k c", k=DC), src).then_inc(w_full[slot], 16)

                u0 = at.u
                for i, j in unit_groups(sp, u0, 2 * GLU_LAG):
                    load_up(i, u0 + j, i * 2 + j // 2, j % 2)
                at.u += 2 * GLU_LAG
                load_ln(3 * layer + 2)
                for what, q in glu_order:
                    if what == "up":
                        for role in range(2):
                            load_up(0, at.u, q, role)
                            at.u += 1
                    else:
                        slot = at.u % SLOTS
                        sp.wait_ge(split_lo, 2 * (at.u - SLOTS + 1))
                        sp.dma_start(packed(2, D)(slot), down[:, q, :, :]).then_inc(w_full[slot], 16)
                        at.u += 1
            load(24, cols(w["w_in_2"]))
            square(w["w_ret_out_2"], 8)
            load_gains(w["b_gate_2"][0, :], w["b_gate_2"][1, :])
            load(26, cols(w["w_in_2"], R_COLS))
            square(w["w_dil_out_2"], 2)
            square(w["w_o_2"], 4)
            load_gains(w["g_post_mix_2"], w["g_post_mlp_2"])
            load(RELU_LAG, cols(w["w_up_2"]))
            up, down = cols(w["w_up_2"]), rows(w["w_down_2"])
            for what, q in relu_order:
                slot = at.u % SLOTS
                sp.wait_ge(split_lo, 2 * (at.u - SLOTS + 1))
                if what == "up":
                    sp.dma_start(ring[slot][:, :].rearrange("p (k c) -> p k c", k=DC), up(q)).then_inc(w_full[slot], 16)
                else:
                    sp.dma_start(packed(2, D)(slot), down(q)).then_inc(w_full[slot], 16)
                at.u += 1
            load(4, cols(w["w_ple_gate_2"]))
            load_gains(w["b_ple_gate_2"], w["g_post_ple_2"])
            square(w["w_ple_in_2"], 1)
            sp.wait_ge(resid_ready, TT * (3 * DEPTH + 3))
            sp.dma_start(out.rearrange("(t p) n -> p t n", p=P), resid[:, :, :]).then_inc(out_written, 16)
            sp.wait_ge(out_written, 16)

        @block.tensor
        def _(pe):
            at = At()

            def turn(blocks):
                r = at.r
                if r >= 2:
                    pe.wait_ge(turn_out[r % 2], r // 2)
                for j, x in enumerate(blocks):
                    n, m = x.shape[0], x.shape[1]
                    mm = nc.tensor.transpose(turn_bank(r)[0:m, j * P:j * P + n], x, ident[0:n, 0:n])
                mm.then_inc(turn_done, 1)
                at.r += 1

            def turn_wide(src, tt, chunks):
                for c in range(0, chunks, 4):
                    turn([src[:, tt, k * P:(k + 1) * P] for k in range(c, min(c + 4, chunks))])

            def turn_all(src, chunks):
                for tt in range(TT):
                    turn_wide(src, tt, chunks)

            def half_k(kc):
                return [range(0, kc // 2), range(kc // 2, kc)]

            def parts_of(ub, h, kc, width):
                n = len(half_k(kc)[h])
                return [x[ub % 2][:, h, 0:n * width].rearrange("p (k c) -> p k c", k=n) for x in (w_hi, w_lo)]

            def three(out, x, w_, first, last, x_moves=False):
                for t, (a, b) in enumerate(((0, 0), (0, 1), (1, 0))):
                    l, r = (w_[b], x[a]) if x_moves else (x[a], w_[b])
                    mm = nc.tensor.matmul(out, l, r, start=first and t == 0, stop=last and t == 2, skip_group_check=True)
                return mm

            def unit(i, ub, vb, x, kind, kc, width):
                if not (isinstance(i, int) and 4 * i + vb < 2):
                    pe.wait_ge(step_out[vb % 2], i * 2 + vb // 2)
                bk = step_bank(vb)
                split_at = {"tok": 0, "feat": width, "both": P}[kind]
                tok_n = width - split_at
                first = True
                for h, ks in enumerate(half_k(kc)):
                    pe.wait_ge(split_lo, i * (2 * SLOTS) + 2 * ub + h + 1)
                    wt = parts_of(ub, h, kc, width)
                    for c in range(0, split_at, P):
                        for k in ks:
                            mm = three(bk[:, c * 2:c * 2 + S], [y[:, k, :] for y in x], [y[:, k - ks[0], c:c + P] for y in wt],
                                       first, k == kc - 1, x_moves=True)
                            first = False
                    if tok_n:
                        for tt in range(TT):
                            b0 = 2 * split_at + tt * tok_n
                            for k in ks:
                                mm = three(bk[:, b0:b0 + tok_n], [y[:, k, tt * P:(tt + 1) * P] for y in x],
                                           [y[:, k - ks[0], split_at:width] for y in wt], first, k == kc - 1)
                                first = False
                    mm.then_inc(halves_used, 1)

            def project(n, x, kind, kc=DC, width=UW, loops=3):
                u0, v0 = at.u, at.v
                for i, j in unit_groups(pe, u0, n, loops=loops):
                    unit(i, u0 + j, v0 + j, x, kind, kc, width)
                at.u += n
                at.v += n

            def gather_unit(x, chunk, first, last):
                ub = at.u
                for h in range(2):
                    pe.wait_ge(split_lo, 2 * ub + h + 1)
                    for tt in range(TT):
                        for half in range(2):
                            mm = three(acc_bank(tt, half), [y[:, chunk + h, tt * P:(tt + 1) * P] for y in x],
                                       [y[ub % 2][:, h, half * 512:(half + 1) * 512] for y in (w_hi, w_lo)],
                                       first and h == 0, last and h == 1)
                        if last and h == 1 and tt == 0:
                            mm.then_inc(acc_first, 1)
                    mm.then_inc(halves_used, 1)
                at.u += 1

            def gather(n, x, ready=None):
                for q in range(n):
                    if ready:
                        ready(q)
                    gather_unit(x, 2 * q, q == 0, q == n - 1)

            def attend(a):
                n0 = at.n

                def scores(i):
                    n = n0 + i
                    if n >= 2:
                        pe.wait_ge(soft_done if a.mask else exp_done, n - 1)
                    for c0, c1, terms in a.scores(i):
                        for t, (l, r) in enumerate(terms):
                            mm = nc.tensor.matmul(a.s_bank(i)[:, c0:c1], l, r, start=t == 0, stop=t == len(terms) - 1)
                    mm.then_inc(scores_done, 1)

                def turn_probs(i):
                    n = n0 + i
                    pe.wait_ge(exp_done, n + 1)
                    if n >= 1 and a.wide:
                        pe.wait_ge(pt_out, n)
                    elif n >= 2:
                        pe.wait_ge(pt_out, n - 1)
                    for c in range(0, a.segs(i)[-1][1], P):
                        mm = nc.tensor.transpose(a.t_bank(i)[:, c:c + P], a.bufs(n)[1][:, c:c + P], ident[:, :])
                    mm.then_inc(pt_done, 1)

                def values(i):
                    n = n0 + i
                    pe.wait_ge(pt_out, n + 1)
                    if n >= 2:
                        pe.wait_ge(head_out, n - 1)
                    for c0, c1, terms in a.pv(i):
                        for t, (b, r) in enumerate(terms):
                            mm = nc.tensor.matmul(a.o_bank(i)[:, c0:c1], a.bufs(n)[2][:, b * P:(b + 1) * P], r,
                                                  start=t == 0, stop=t == len(terms) - 1)
                    mm.then_inc(pv_done, 1)

                scores(0)
                for i in range(a.count):
                    if i + 1 < a.count:
                        scores(i + 1)
                    turn_probs(i)
                    if i >= 1:
                        values(i - 1)
                values(a.count - 1)
                at.n += a.count

            def norm_turns():
                for tt in range(TT):
                    pe.wait_ge(normed_ready, at.nrm + tt + 1)
                    turn_wide(normed, tt, DC)
                at.nrm += TT
                at.sc += 4
                pe.wait_ge(scaled_out, at.sc)

            def output(n_units, source_ready=True):
                pe.wait_ge(head_out, at.n)
                turn_all(heads, DC)
                wait_turns(pe, at.r)
                gather(n_units, ht)

            pe.wait_ge(ident_in, 16)
            pe.wait_ge(mem_in, 16)
            turn_all(heads, DC)
            pe.wait_ge(rows_in, 16 * n_row_loads)
            turn([stage_rows[:, c, :] for c in range(4)])
            turn([stage_rows[0:min(P, PARAMS - c * P), c, :] for c in range(4, 8)])
            pe.wait_ge(x_in, 16)
            turn_all(resid, DC)
            wait_turns(pe, 4)
            project(4, ht, "feat")
            project(4, ht, "tok")

            for layer in range(DEPTH):
                kind = layer % 3
                if kind == 0:
                    if layer == 0:
                        wait_turns(pe, at.r)
                    project(6, xt, "tok")
                    for tt in range(TT):
                        pe.wait_ge(rot_out, at.rot + 2 * tt + 2)
                        turn_wide(tok(1536), tt, DC)
                        turn([k_dup[:, tt, h, :, :].rearrange("p e d -> p (e d)") for h in range(A_KV)])
                    at.rot += 2 * TT
                    wait_turns(pe, at.r)
                    wait_steps(pe, at.v)
                    attend(swa(layer // 3))
                    output(4)
                elif kind == 1:
                    project(8, xt, "feat")
                    wait_steps(pe, at.v)
                    pe.wait_ge(lru_ulo, 1)
                    for gate in range(2):
                        for h in range(LRU_BLOCKS):
                            v, half = at.v, h // 2
                            pe.wait_ge(split_lo, 2 * at.u + half + 1)
                            pe.wait_ge(step_out[v % 2], v // 2)
                            wt = parts_of(at.u, half, DC, UW)
                            for c in range(2):
                                for k in range(2):
                                    mm = three(step_bank(v)[:, c * S:(c + 1) * S], [y[:, 2 * h + k, :] for y in xt],
                                               [y[:, 2 * (h % 2) + k, c * P:(c + 1) * P] for y in wt], k == 0 and c == 0, k == 1, x_moves=True)
                            mm.then_inc(halves_used if h % 2 else gate_step, 1)
                            at.v += 1
                        at.u += 1
                    gather(4, ht, ready=lambda q: pe.wait_ge(lru_lo, q + 1))
                else:
                    project(2, xt, "tok")
                    project(1, xt, "tok", width=C_DOWN - 2 * UW)
                    pe.wait_ge(rot_out, at.rot + TT)
                    at.rot += TT
                    pe.wait_ge(mla_scaled, 1)
                    low = tok(C_DOWN)
                    for tt in range(TT):
                        turn([low[:, tt, c * P:(c + 1) * P] for c in range(4)])
                        turn([low[:, tt, 4 * P:5 * P], low[:, tt, 5 * P:5 * P + C_ROPE]])
                    at.sc += 4
                    pe.wait_ge(scaled_out, at.sc)
                    project(8, ht, "both", kc=3, width=C_NOPE + C_ROPE)
                    project(8, [y[:, 3:5, :] for y in ht], "both", kc=2)
                    for tt in range(TT):
                        pe.wait_ge(rot_out, at.rot + tt + 1)
                        q_rope = mla_qr()
                        for h in range(0, C_HEADS, 4):
                            turn([q_rope[:, tt, h + m, :] for m in range(4)])
                    at.rot += TT
                    wait_turns(pe, at.r)
                    wait_steps(pe, at.v)
                    attend(mla())
                    output(4)
                norm_turns()
                project(4, xt, "feat")
                wait_steps(pe, at.v)
                attend(cross())
                output(4)
                norm_turns()
                project(2 * GLU_LAG, xt, "feat")
                for what, q in glu_order:
                    if what == "up":
                        project(2, xt, "feat")
                    else:
                        pe.wait_ge(glu_out, layer * N_GLU + q + 1)
                        gather_unit(ht, 2 * q % HC, q == 0, q == N_GLU - 1)
                if layer < DEPTH - 1:
                    norm_turns()
                else:
                    at.nrm += TT

            norm_turns()
            project(16, xt, "tok")
            ret = tok(2048)
            ret_v = tok_at(4096, 2048)
            for part_q in range(2):
                for tt in range(TT):
                    pe.wait_ge(rot_out, at.rot + 2)
                    at.rot += 2
                    turn_wide(ret[:, :, part_q * 1024:(part_q + 1) * 1024], tt, DC)
            wait_turns(pe, at.r)
            project(8, xt, "tok")

            def ret_score(h):
                if h >= 2:
                    pe.wait_ge(ret_decayed, h - 1)
                for c0, c1, kb, q0 in ((0, S, 0, 0), (S, S + P, 1, P)):
                    for k in range(2):
                        mm = nc.tensor.matmul(bank[:, STEP + h % 2, c0:c1], kt[:, 2 * h + k, kb * P:(kb + 1) * P],
                                              qt[:, 2 * h + k, q0:S], start=k == 0, stop=k == 1)
                mm.then_inc(ret_scores, 1)

            wait_steps(pe, at.v)
            ret_score(0)
            for h in range(R_HEADS):
                if h + 1 < R_HEADS:
                    ret_score(h + 1)
                pe.wait_ge(ret_decayed, h + 1)
                if h >= 2:
                    pe.wait_ge(ret_norm, TT * (h - 1))
                for tt in range(TT):
                    for kb in range(tt + 1):
                        b = tt + kb
                        mm = nc.tensor.matmul(bank[:, ACC + 2 * (h % 2) + tt, :], ret_pt[h % 2][:, b * P:(b + 1) * P],
                                              ret_v[:, kb, h * R_V:(h + 1) * R_V], start=kb == 0, stop=kb == tt)
                    mm.then_inc(ret_pv, 1)
            pe.wait_ge(ret_norm, TT * R_HEADS)
            for tt in range(TT):
                turn_wide(ret, tt, 16)
            wait_turns(pe, at.r)
            gather(8, ht)
            project(18, xt, "tok")
            dil = tok(2 * D_W)
            for part_q in range(2):
                for tt in range(TT):
                    pe.wait_ge(rot_out, at.rot + 1)
                    at.rot += 1
                    turn_wide(dil[:, :, part_q * D_W:(part_q + 1) * D_W], tt, D_W // P)
            wait_turns(pe, at.r)
            project(8, xt, "tok")
            wait_steps(pe, at.v)
            pe.wait_ge(branch_out, TT)
            attend(dilated())
            pe.wait_ge(head_out, at.n)
            turn_all(heads, 4)
            wait_turns(pe, at.r)
            gather(2, ht)
            for tt in range(TT):
                pe.wait_ge(mix_ready, tt + 1)
                turn_wide(heads, tt, DC)
            wait_turns(pe, at.r)
            gather(4, ht)
            norm_turns()
            project(RELU_LAG, xt, "feat")
            for what, q in relu_order:
                if what == "up":
                    project(1, xt, "feat")
                else:
                    pe.wait_ge(relu_sq, q + 1)
                    gather_unit(ht, 2 * q % HC, q == 0, q == N_RELU - 1)
            norm_turns()
            project(4, xt, "tok")
            pe.wait_ge(p_in, 16)
            for tt in range(TT):
                turn([p_tok[:, tt, c * P:(c + 1) * P] for c in range(2)])
            wait_turns(pe, at.r)
            gather(1, ht)

        @block.scalar
        def _(act):
            at = At()
            links = [0]

            def link(ins):
                links[0] += 1
                ins.then_inc(act_link, 1)
                act.wait_ge(act_link, links[0])

            act.dma_start(ident[:, :], w["k_ident"]).then_inc(ident_in, 16)
            act.dma_start(heads[:, :, :], w["mem"].rearrange("(t p) n -> p t n", p=P)).then_inc(mem_in, 16)
            r = 0
            for name, rows in PARAM_ROWS:
                v = param_views[name]
                done = 0
                while done < rows:
                    k = min(rows - done, P - r % P)
                    act.dma_start(stage_rows[r % P:r % P + k, r // P, :], v[done:done + k, :]).then_inc(rows_in, 16)
                    r += k
                    done += k
            act.dma_start(resid[:, :, :], w["x"].rearrange("(t p) n -> p t n", p=P)).then_inc(x_in, 16)
            act.dma_start(rope_t[:, :, :, :], w["k_rope"].rearrange("(t p) e d -> p t e d", p=P)).then_inc(tables_in, 16)
            act.dma_start(mask_a[:, :], w["k_mask_a"]).then_inc(tables_in, 16)
            act.dma_start(mask_c[:, :], w["k_mask_c"]).then_inc(tables_in, 16)
            act.dma_start(sinks[:, :], w["a_sinks"].rearrange("a h -> (a h)").rearrange("(o n) -> o n", o=1).to_broadcast([P, 2 * A_HEADS])).then_inc(tables_in, 16)
            act.dma_start(freq[:, :], w["k_freq"].to_broadcast([P, NF])).then_inc(tables_in, 16)
            with nc.allow_non_contiguous_dma(reason="256 positions"):
                act.dma_start(pos_i[:, :], w["positions_2"].rearrange("(t p) -> p t", p=P)).then_inc(tables_in, 16)

            def turn_copy(dests):
                r = at.r
                if r % 2 == 0:
                    act.wait_ge(turn_done, r + 1)
                    for dst, (c0, c1) in dests:
                        src = turn_bank(r)[0:dst.shape[0], c0:c1]
                        if len(dst.shape) == 3:
                            src = src.rearrange("p (c s) -> p c s", s=P)
                        ins = nc.scalar.copy(dst, src)
                    ins.then_inc(turn_out[0], 1)
                at.r += 1

            def turn_split(hi, lo, m):
                act.wait_ge(turn_done, at.r + 1)
                nc.scalar.copy(hi, turn_bank(at.r)[:, 0:m * P].rearrange("p (c s) -> p c s", s=P)).then_inc(turn_hi, 1)
                at.r += 1
                at.th += 1

            late = []

            def turn_scaled(dests, v, hi, lo):
                r = at.r
                if r % 2 == 0:
                    act.wait_ge(turn_done, r + 1)
                    for dst, (c0, c1), scale, bias in dests:
                        ins = nc.scalar.activation(dst, turn_bank(r)[0:dst.shape[0], c0:c1], ACT.Copy if bias is None else ACT.Identity,
                                                   **({} if scale is None else {"scale": scale}), **({} if bias is None else {"bias": bias}))
                    ins.then_inc(turn_out[0], 1)
                late.append((r, v, hi))
                at.r += 1
                if len(late) == 2:
                    for r_, v_, hi_ in late:
                        wait_turn(act, r_)
                        nc.scalar.copy(hi_, v_).then_inc(turn_hi, 1)
                        at.th += 1
                    late.clear()

            def split(i, ub, h):
                if isinstance(i, int) and 4 * i + ub >= N_UNITS:
                    return
                n, first = unit_half(i, ub, h)
                if h == 0:
                    act.wait_ge(w_full[ub % SLOTS], i * 16 + 16 * (ub // SLOTS + 1))
                if not (isinstance(i, int) and 4 * i + ub < AHEAD):
                    act.wait_ge(halves_used, i * (2 * SLOTS) + 2 * (ub - AHEAD) + h + 1)
                nc.scalar.copy(w_hi[ub % 2][:, h, 0:n], ring[ub % SLOTS][:, first:first + n]).then_inc(split_hi, 1)

            def splits(n):
                for _ in range(n):
                    for h in range(2):
                        split(0, at.u + AHEAD, h)
                    at.u += 1

            def step_copy(dest_of, n):
                u0, v0 = at.u, at.v
                for i, j in unit_groups(act, u0, n):
                    split(i, u0 + j + AHEAD, 0)
                    if (v0 + j) % 2 == 0:
                        act.wait_ge(halves_used, i * (2 * SLOTS) + 2 * (u0 + j + 1))
                        for dst, c0, c1 in dest_of(i * SLOTS + j):
                            src = step_bank(v0 + j)[:, c0:c1]
                            if len(dst.shape) == 3:
                                src = src.rearrange("p (a b) -> p a b", a=dst.shape[1])
                            ins = nc.scalar.copy(dst, src)
                        ins.then_inc(step_out[0], 1)
                    split(i, u0 + j + AHEAD, 1)
                at.u += n
                at.v += n

            def attend(a):
                n0 = at.n

                def exps(i):
                    n = n0 + i
                    act.wait_ge(soft_done, n + 1)
                    if n >= 2:
                        act.wait_ge(pt_done, n - 1)
                    st = stat[n % 2]
                    segs = a.segs(i)
                    if a.sink:
                        nc.scalar.activation(st[:, 6:8], st[:, 2:4], ACT.Exp, bias=a.sink(i))
                    for t, (c0, c1) in enumerate(segs):
                        src = a.bufs(n)[0][:, c0:c1] if a.mask else a.s_bank(i)[:, c0:c1]
                        ins = nc.scalar.activation(a.bufs(n)[1][:, c0:c1], src, ACT.Exp, bias=st[:, 2 + t:3 + t],
                                                   scale=1.0 if a.mask else a.scale, accum_out=st[:, 4 + t:5 + t])
                    ins.then_inc(exp_done, 1)

                def copy_t(i):
                    n = n0 + i
                    act.wait_ge(pt_done, n + 1)
                    if n >= 2:
                        act.wait_ge(pv_done, n - 1)
                    nc.scalar.copy(a.bufs(n)[2][:, 0:a.segs(i)[-1][1]], a.t_bank(i)).then_inc(pt_out, 1)

                for i in range(a.count):
                    exps(i)
                    if a.wide:
                        if i >= 1:
                            copy_t(i - 1)
                    elif i >= 1:
                        copy_t(i - 1)
                copy_t(a.count - 1)
                at.n += a.count

            turns = for_turns(at, turn_copy, turn_split, turn_scaled)
            for u in range(AHEAD):
                for h in range(2):
                    split(0, u, h)
            turns["setup"]()
            step_copy(lambda q: [(mem_kt[:, 2 * q:2 * q + 2, :], 0, 512)], 4)
            step_copy(lambda q: [(mem_v[:, :, q * UW:(q + 1) * UW], 0, 512)], 4)

            def glu_unit(i, ub, vb, qb, role, layer):
                par = qb % 2
                split(i, ub + AHEAD, 0)
                act.wait_ge(halves_used, i * (2 * SLOTS) + 2 * (ub + 1))
                first = isinstance(i, int) and layer == 0 and 2 * i + qb < 2
                if not first:
                    act.wait_ge(glu_prod, i * 2 + (layer * N_GLU + qb - 1))
                for c in range(2):
                    ch = i * 4 + (2 * qb + c + role * FFC)
                    ins = nc.scalar.activation(cwork[par][role][:, c, :], step_bank(vb)[:, c * S:(c + 1) * S], ACT.Identity,
                                               bias=params[:, bass.ds(ch + (COL["f_conv_b"] + layer * 2 * FFC), 1)],
                                               scale=params[:, bass.ds(ch + (COL["f_conv_w"] + (layer * 3 + 2) * 2 * FFC), 1)])
                ins.then_inc(conv_start, 1)
                split(i, ub + AHEAD, 1)
                if role == 1:
                    act.wait_ge(step_out[(vb - 1) % 2], i * 2 + (vb - 1) // 2 + 1)
                    nc.scalar.activation(swork[par][:, :, :], cwork[par][0][:, :, :], ACT.Silu).then_inc(glu_gate, 1)
                    if not (isinstance(i, int) and 2 * i + qb == 0):
                        glu_high(i, qb - 1, layer)

            def glu_high(i, qb, layer):
                act.wait_ge(glu_prod, i * 2 + (layer * N_GLU + qb + 1))
                if isinstance(i, int):
                    dst = ht[0][:, (4 * i + 2 * qb) % HC:(4 * i + 2 * qb) % HC + 2, :]
                else:
                    dst = ht[0][:, bass.ds(i * 4 + 2 * qb, 2), :]
                nc.scalar.copy(dst, pwork[qb % 2][:, :, :]).then_inc(glu_hi, 1)

            for layer in range(DEPTH):
                kind = layer % 3
                if kind == 0:
                    step_copy(lambda q: [(tok(1536)[:, :, q * UW:(q + 1) * UW], 0, 512)], 6)
                    turns["swa"]()
                    attend(swa(layer // 3))
                    turns["heads"]()
                    splits(4)
                elif kind == 1:
                    gel, u, rg, ig, a_, b_ = lru_parts
                    for q in range(8):
                        split(0, at.u + AHEAD, 0)
                        act.wait_ge(halves_used, 2 * (at.u + 1))
                        bk = step_bank(at.v)
                        if q < 4:
                            nc.scalar.activation(gel[:, 2 * q:2 * q + 2, :], bk.rearrange("p (c s) -> p c s", s=S),
                                                 ACT.Gelu_apprx_tanh).then_inc(step_out[at.v % 2], 1)
                        else:
                            for c in range(2):
                                ch = 2 * (q - 4) + c
                                ins = nc.scalar.activation(u[:, ch, :], bk[:, c * S:(c + 1) * S], ACT.Identity,
                                                           bias=col("b_conv_b", ch), scale=col("b_conv_w", 3 * DC + ch))
                            ins.then_inc(lru_act, 1)
                        split(0, at.u + AHEAD, 1)
                        at.u += 1
                        at.v += 1
                    wait_steps(act, at.v)
                    nc.scalar.copy(xt[0][:, :, :], u[:, :, :]).then_inc(lru_uhi, 1)
                    for gate, (dst, bias) in enumerate(((rg, "b_b_rgate"), (ig, "b_b_igate"))):
                        for h in range(LRU_BLOCKS):
                            if h % 2 == 0:
                                act.wait_ge(gate_step, gate * 2 + h // 2 + 1)
                            else:
                                act.wait_ge(halves_used, 2 * at.u + h // 2 + 1)
                            for c in range(2):
                                ins = nc.scalar.activation(dst[:, 2 * h + c, :], step_bank(at.v)[:, c * S:(c + 1) * S],
                                                           ACT.Sigmoid, bias=col(bias, 2 * h + c))
                            ins.then_inc(step_out[at.v % 2], 1)
                            at.v += 1
                            if h % 2:
                                split(0, at.u + AHEAD, h // 2)
                        at.u += 1
                    wait_steps(act, at.v)
                    act.wait_ge(lru_dve, LRU_SP)
                    for ch in range(DC):
                        nc.scalar.activation(a_[:, ch, :], rg[:, ch, :], ACT.Exp, scale=softplus[:, 5, ch:ch + 1])
                    for ch in range(DC):
                        ins = nc.scalar.activation(b_[:, ch, :], rg[:, ch, :], ACT.Tanh, scale=softplus[:, 5, ch:ch + 1])
                    ins.then_inc(lru_act, 1)
                    act.wait_ge(lru_dve, LRU_SP + 1)
                    nc.scalar.activation(rg[:, :, :], b_[:, :, :], ACT.Sqrt).then_inc(lru_act, 1)
                    for q in range(4):
                        act.wait_ge(lru_pool, 2 * q + 2)
                        nc.scalar.copy(ht[0][:, 2 * q:2 * q + 2, :], ig[:, 2 * q:2 * q + 2, :]).then_inc(lru_hi, 1)
                    splits(4)
                else:
                    low = tok(C_DOWN)
                    step_copy(lambda q: [(low[:, :, q * UW:(q + 1) * UW], 0, 512)], 2)
                    step_copy(lambda q: [(low[:, :, 2 * UW:C_DOWN], 0, 2 * (C_DOWN - 2 * UW))], 1)
                    wait_steps(act, at.v)
                    for tt in range(TT):
                        for t, (c0, c1) in enumerate(((0, C_QR), (C_QR, C_QR + C_KVR))):
                            k = at.col + 2 * tt + t
                            ins = nc.scalar.activation((masked, probs)[tt][t][:, 0:c1 - c0], low[:, tt, c0:c1], ACT.Square,
                                                       accum_out=ssq[:, k:k + 1])
                    ins.then_inc(ssq_ready, 1)
                    at.col += 4
                    at.sq += 1
                    turns["mla_low"]()
                    step_copy(lambda q: [(qt[:, q, :], 0, S), (mla_qr()[:, :, q, :], S, S + 2 * C_ROPE)], 8)
                    step_copy(lambda q: [(kt[:, q, :], 0, S), (mla_v()[:, :, q * P:(q + 1) * P], S, 2 * S)], 8)
                    turns["mla_q"]()
                    attend(mla())
                    turns["heads"]()
                    splits(4)
                at.col += TT
                turns["norm"](lambda c, n=3 * layer: (col("ln_g", n * DC + c), col("ln_b", n * DC + c)))
                step_copy(lambda q: [(qt[:, 2 * q:2 * q + 2, :], 0, 512)], 4)
                attend(cross())
                turns["heads"]()
                splits(4)
                at.col += TT
                turns["norm"](lambda c, n=3 * layer + 1: (col("ln_g", n * DC + c), col("ln_b", n * DC + c)))
                u0, v0 = at.u, at.v
                for i, j in unit_groups(act, u0, 2 * GLU_LAG, peel=1):
                    glu_unit(i, u0 + j, v0 + j, j // 2, j % 2, layer)
                at.u += 2 * GLU_LAG
                at.v += 2 * GLU_LAG
                for what, q in glu_order:
                    if what == "up":
                        for role in range(2):
                            glu_unit(0, at.u, at.v, q, role, layer)
                            at.u += 1
                            at.v += 1
                        if q == N_GLU - 1:
                            glu_high(0, q, layer)
                    else:
                        splits(1)
                at.col += TT
                if layer < DEPTH - 1:
                    turns["norm"](lambda c, n=3 * layer + 2: (col("ln_g", n * DC + c), col("ln_b", n * DC + c)))

            def squares(src_of, wait_of, n=TT):
                for tt in range(n):
                    wait_of(tt)
                    nc.scalar.activation(normed[:, tt, :], src_of(tt), ACT.Square,
                                         accum_out=ssq[:, at.col:at.col + 1]).then_inc(ssq_ready, 1)
                    at.col += 1
                    at.sq += 1

            act.wait_ge(head_out, at.n)
            act.dma_start(mask_d, w["k_mask_d"]).then_inc(tables2_in, 16)
            act.dma_start(decay, w["k_decay"]).then_inc(tables2_in, 16)
            act.wait_ge(resid_ready, TT * 3 * DEPTH)
            squares(lambda tt: resid[:, tt, :], lambda tt: None)
            turns["norm"](lambda c: (col("g_pre_mix_2", c), None))
            act.wait_ge(angle_ready, 1)
            nc.scalar.activation(angles[:, 1, :, :], angles[:, 0, :, :], ACT.Sin)
            nc.scalar.activation(angles[:, 2, :, :], angles[:, 0, :, :], ACT.Sin, scale=0.5).then_inc(trig_ready, 1)
            ret = tok(2048)
            ret_v = tok_at(4096, 2048)
            step_copy(lambda q: [(ret[:, :, q * UW:(q + 1) * UW], 0, 512)], 8)
            step_copy(lambda q: [(ret_v[:, :, q * UW:(q + 1) * UW], 0, 512)], 8)
            turns["ret_qk"]()
            step_copy(lambda q: [(ret[:, :, q * UW:(q + 1) * UW], 0, 512)], 8)
            wait_steps(act, at.v)
            for tt in range(TT):
                ins = nc.scalar.activation(ret[:, tt, :], ret[:, tt, :], ACT.Silu)
            ins.then_inc(gate_sig, 1)
            for h in range(R_HEADS):
                for tt in range(TT):
                    if h:
                        act.wait_ge(ssq_ready, at.sq - 1)
                    act.wait_ge(ret_pv, TT * h + tt + 1)
                    nc.scalar.activation(ret_junk[tt], bank[:, ACC + 2 * (h % 2) + tt, :], ACT.Square,
                                         accum_out=ssq[:, at.col:at.col + 1]).then_inc(ssq_ready, 1)
                    at.col += 1
                    at.sq += 1
            turns["ret_out"]()
            splits(8)
            dil = tok(2 * D_W)
            dil_v = tok_at(2 * TT * D_W, D_W)
            step_copy(lambda q: [(dil[:, :, bass.ds(q * UW, UW)], 0, 512)], 12)
            step_copy(lambda q: [(dil_v[:, :, q * UW:(q + 1) * UW], 0, 512)], 6)
            turns["dil_qk"]()
            gates = tok(2 * D)
            step_copy(lambda q: [(gates[:, :, q * UW:(q + 1) * UW], 0, 512)], 8)
            attend(dilated())
            turns["dil_out"]()
            act.wait_ge(gate_in, 1)
            for tt in range(TT):
                ins = nc.scalar.activation(gates[:, tt, :], gates[:, tt, :], ACT.Sigmoid)
            ins.then_inc(gate_sig, 1)
            splits(2)
            turns["heads"]()
            splits(4)

            def post_squares():
                squares(acc_tile, lambda tt: act.wait_ge(acc_first, at.acc) if tt == 0 else act.wait_ge(halves_used, 2 * at.u))

            def pre_squares(k):
                squares(lambda tt: resid[:, tt, :], lambda tt: act.wait_ge(resid_ready, TT * (3 * DEPTH + k) + tt + 1))

            at.acc = 3 * DEPTH + 3
            post_squares()
            pre_squares(0)
            turns["norm"](lambda c: (col("g_pre_mlp_2", c), None))

            def relu_high(q):
                act.wait_ge(relu_prod, q + 1)
                nc.scalar.copy(ht[0][:, 2 * q % HC:2 * q % HC + 2, :], pwork[q % 2][:, :, :]).then_inc(relu_hi, 1)

            def relu_unit(q):
                split(0, at.u + AHEAD, 0)
                act.wait_ge(halves_used, 2 * (at.u + 1))
                if q >= 2:
                    act.wait_ge(relu_prod, q - 1)
                nc.scalar.activation(cwork[0][q % 2][:, :, :], step_bank(at.v).rearrange("p (c s) -> p c s", s=S),
                                     ACT.Relu).then_inc(step_out[at.v % 2], 1)
                split(0, at.u + AHEAD, 1)
                if q:
                    relu_high(q - 1)
                at.u += 1
                at.v += 1

            for q in range(RELU_LAG):
                relu_unit(q)
            for what, q in relu_order:
                if what == "up":
                    relu_unit(q)
                    if q == N_RELU - 1:
                        relu_high(q)
                else:
                    splits(1)
            at.acc += 1
            post_squares()
            pre_squares(1)
            act.dma_start(p_tok, w["p_2"].rearrange("(t p) n -> p t n", p=P)).then_inc(p_in, 16)
            turns["norm"](lambda c: (col("g_pre_ple_2", c), None))
            step_copy(lambda q: [(tok(D)[:, :, q * UW:(q + 1) * UW], 0, 512)], 4)
            turns["p"]()
            splits(1)
            act.wait_ge(ple_in, 1)
            nc.scalar.activation(tok(D), tok(D), ACT.Sigmoid).then_inc(ple_sig, 1)
            for tt in range(TT):
                act.wait_ge(ple_prod, tt + 1)
                nc.scalar.activation(normed[:, tt, :], heads[:, tt, :], ACT.Square,
                                     accum_out=ssq[:, at.col:at.col + 1]).then_inc(ssq_ready, 1)
                at.col += 1

        @block.vector
        def _(dve):
            at = At()
            links = [0]
            v_ = nc.vector

            def mark(ins):
                links[0] += 1
                ins.then_inc(dve_link, 1)
                return links[0]

            def link(ins):
                dve.wait_ge(dve_link, mark(ins))

            def turn_copy(dests):
                r = at.r
                if r % 2 == 1:
                    dve.wait_ge(turn_done, r + 1)
                    for dst, (c0, c1) in dests:
                        src = turn_bank(r)[0:dst.shape[0], c0:c1]
                        if len(dst.shape) == 3:
                            src = src.rearrange("p (c s) -> p c s", s=P)
                        ins = v_.tensor_copy(dst, src)
                    ins.then_inc(turn_out[1], 1)
                at.r += 1

            def turn_split(hi, lo, m):
                at.th += 1
                dve.wait_ge(turn_hi, at.th)
                v_.tensor_tensor(lo, turn_bank(at.r)[:, 0:m * P].rearrange("p (c s) -> p c s", s=P), hi.bitcast(F32),
                                 ALU.subtract).then_inc(turn_out[at.r % 2], 1)
                at.r += 1

            late = []

            def turn_scaled(dests, v, hi, lo):
                r = at.r
                if r % 2 == 1:
                    dve.wait_ge(turn_done, r + 1)
                    for dst, (c0, c1), scale, bias in dests:
                        src = turn_bank(r)[0:dst.shape[0], c0:c1]
                        if scale is None:
                            ins = v_.tensor_copy(dst, src)
                        elif bias is None:
                            ins = v_.tensor_scalar(dst, src, scale, None, ALU.mult)
                        else:
                            ins = v_.tensor_scalar(dst, src, scale, bias, ALU.mult, ALU.add)
                    ins.then_inc(turn_out[1], 1)
                late.append((v, hi, lo))
                at.r += 1
                if len(late) == 2:
                    for x, hi_, lo_ in late:
                        at.th += 1
                        dve.wait_ge(turn_hi, at.th)
                        v_.tensor_tensor(lo_, x, hi_.bitcast(F32), ALU.subtract).then_inc(scaled_out, 1)
                    late.clear()

            def split(i, ub, h):
                if isinstance(i, int) and 4 * i + ub >= N_UNITS:
                    return
                n, first = unit_half(i, ub, h)
                dve.wait_ge(split_hi, i * (2 * SLOTS) + 2 * ub + h + 1)
                v_.tensor_tensor(w_lo[ub % 2][:, h, 0:n], ring[ub % SLOTS][:, first:first + n], w_hi[ub % 2][:, h, 0:n].bitcast(F32),
                                 ALU.subtract).then_inc(split_lo, 1)

            def splits(n, keep=0):
                for k in range(n):
                    if k < n - keep:
                        for h in range(2):
                            split(0, at.u + AHEAD, h)
                    at.u += 1

            def kept():
                for h in range(2):
                    split(0, at.u - 1 + AHEAD, h)

            def step_copy(dest_of, n):
                u0, v0 = at.u, at.v
                for i, j in unit_groups(dve, u0, n):
                    split(i, u0 + j + AHEAD, 0)
                    if (v0 + j) % 2 == 1:
                        dve.wait_ge(halves_used, i * (2 * SLOTS) + 2 * (u0 + j + 1))
                        for dst, c0, c1 in dest_of(i * SLOTS + j):
                            src = step_bank(v0 + j)[:, c0:c1]
                            if len(dst.shape) == 3:
                                src = src.rearrange("p (a b) -> p a b", a=dst.shape[1])
                            ins = v_.tensor_copy(dst, src)
                        ins.then_inc(step_out[1], 1)
                    split(i, u0 + j + AHEAD, 1)
                at.u += n
                at.v += n

            def rotate(rows, cos, sin, dests):
                k = at.rot
                n, half = rows.shape[1], rows.shape[3]
                c = rot_c_view(k, n, half)
                s = rot_s_view(k, n, half)
                if k >= 2:
                    dve.wait_ge(rot_out, k - 1)
                link(v_.tensor_tensor(c, rows, bcast(cos, n, half), ALU.mult))
                dve.wait_ge(rot_sin, k + 1)
                ins = None
                for (a, b), outs in dests:
                    for e, op in ((0, ALU.subtract), (1, ALU.add)):
                        x, y = c[:, a:b, e, :], s[:, a:b, 1 - e, :]
                        o = outs[e]
                        if len(o.shape) == 4:
                            x = x.unsqueeze(2).to_broadcast([P, b - a, o.shape[2], half])
                            y = y.unsqueeze(2).to_broadcast([P, b - a, o.shape[2], half])
                        ins = v_.tensor_tensor(o, x, y, op)
                ins.then_inc(rot_out, 1)
                at.rot += 1

            def attend(a):
                n0 = at.n

                def soft(i):
                    n = n0 + i
                    st = stat[n % 2]
                    segs = a.segs(i)
                    ns = len(segs)
                    dve.wait_ge(scores_done, n + 1)
                    if n >= 2:
                        dve.wait_ge(exp_done, n - 1)
                    if a.mask:
                        src = a.bufs(n)[0][:, 0:segs[-1][1]]
                        link(v_.scalar_tensor_tensor(out=src, in0=a.s_bank(i), scalar=a.scale, in1=a.mask(i),
                                                     op0=ALU.mult, op1=ALU.add))
                    else:
                        src = a.s_bank(i)
                    for t, (c0, c1) in enumerate(segs):
                        ins = v_.reduce_max(st[:, t:t + 1], src[:, c0:c1], AX.X)
                        if t < ns - 1:
                            pass
                    link(ins)
                    if a.sink:
                        ins = v_.tensor_scalar(st[:, 2:2 + ns], st[:, 0:ns], a.sink(i), -1.0, ALU.max, ALU.mult)
                    else:
                        ins = v_.tensor_scalar(st[:, 2:2 + ns], st[:, 0:ns], -1.0 if a.mask else -a.scale, None, ALU.mult)
                    ins.then_inc(soft_done, 1)

                def denominators(i):
                    n = n0 + i
                    st = stat[n % 2]
                    ns = len(a.segs(i))
                    dve.wait_ge(exp_done, n + 1)
                    den = st[:, 4:4 + ns]
                    if a.sink:
                        den = st[:, 8:8 + ns]
                        link(v_.tensor_tensor(den, st[:, 4:4 + ns], st[:, 6:6 + ns], ALU.add))
                    link(v_.reciprocal(st[:, 10:10 + ns], den))

                def heads_out(i):
                    n = n0 + i
                    st = stat[n % 2]
                    dst = a.dest(i)
                    t, wd = dst.shape[1], dst.shape[2]
                    dve.wait_ge(pv_done, n + 1)
                    v_.tensor_tensor(dst, a.o_bank(i)[:, 0:t * wd].rearrange("p (t c) -> p t c", t=t),
                                     st[:, 10:10 + t].unsqueeze(2).to_broadcast([P, t, wd]), ALU.mult).then_inc(head_out, 1)

                for i in range(a.count):
                    soft(i)
                    if i >= 2:
                        heads_out(i - 2)
                    if i >= 1:
                        denominators(i - 1)
                if a.count >= 2:
                    heads_out(a.count - 2)
                denominators(a.count - 1)
                heads_out(a.count - 1)
                at.n += a.count

            def wait_acc(tt):
                if tt == 0:
                    at.acc += 1
                    dve.wait_ge(acc_first, at.acc)
                else:
                    dve.wait_ge(halves_used, 2 * at.u)

            def layer_norm():
                n = at.nrm
                for tt in range(TT):
                    wait_acc(tt)
                    if n == 0:
                        dve.wait_ge(x_in, 16)
                        dve.wait_ge(turn_done, 10)
                    else:
                        dve.wait_ge(resid_ready, TT * (n - 1) + tt + 1)
                    ks = []
                    for half in range(2):
                        h = slice(half * 512, (half + 1) * 512)
                        ks.append(mark(v_.scalar_tensor_tensor(out=resid[:, tt, h], in0=resid[:, tt, h], scalar=ALPHA,
                                                               in1=acc_bank(tt, half), op0=ALU.mult, op1=ALU.add)))
                    for half in range(2):
                        dve.wait_ge(dve_link, ks[half])
                        k = mark(v_.bn_stats(bn[:, tt, half, :], resid[:, tt, half * 512:(half + 1) * 512]))
                    dve.wait_ge(dve_link, k)
                    link(v_.bn_aggr(bn_mv[:, tt, :], bn[:, tt, :, :].rearrange("p a b -> p (a b)")))
                    v_.tensor_scalar(var[:, at.col + tt:at.col + tt + 1], bn_mv[:, tt, 1:2], LN_EPS, None, ALU.add).then_inc(var_ready, 1)
                for tt in range(TT):
                    at.msq += 1
                    dve.wait_ge(rstd_ready, at.msq)
                    k = at.col + tt
                    v_.tensor_scalar(normed[:, tt, :], resid[:, tt, :], bn_mv[:, tt, 0:1], rstd[:, k:k + 1],
                                     ALU.subtract, ALU.mult).then_inc(normed_ready, 1)
                kept()
                at.col += TT
                at.nrm += 1

            def mean_square(width, n=1):
                at.sq += 1
                dve.wait_ge(ssq_ready, at.sq)
                v_.tensor_scalar(var[:, at.col:at.col + n], ssq[:, at.col:at.col + n], 1.0 / width, RMS_EPS,
                                 ALU.mult, ALU.add).then_inc(var_ready, 1)
                at.msq += 1
                at.col += n

            turns = for_turns(at, turn_copy, turn_split, turn_scaled)
            for u in range(AHEAD):
                for h in range(2):
                    split(0, u, h)
            turns["setup"]()
            step_copy(lambda q: [(mem_kt[:, 2 * q:2 * q + 2, :], 0, 512)], 4)
            step_copy(lambda q: [(mem_v[:, :, q * UW:(q + 1) * UW], 0, 512)], 4)
            dve.wait_ge(tables_in, 16 * 6)
            link(v_.tensor_copy(pos_f[:, :], pos_i[:, :]))
            for tt in range(TT):
                k = mark(v_.tensor_scalar(angles[:, 0, tt, :], freq[:, :], pos_f[:, tt:tt + 1], None, ALU.mult))
            dve.wait_ge(dve_link, k)
            link(v_.tensor_scalar(angles[:, 1, :, :], angles[:, 0, :, :], 1.0 / TWO_PI, ROUND, ALU.mult, ALU.add))
            link(v_.tensor_scalar(angles[:, 1, :, :], angles[:, 1, :, :], -ROUND, None, ALU.add))
            for c in (PI_1, PI_2, PI_3):
                link(v_.scalar_tensor_tensor(out=angles[:, 0, :, :], in0=angles[:, 1, :, :], scalar=-c, in1=angles[:, 0, :, :],
                                             op0=ALU.mult, op1=ALU.add))
            v_.tensor_scalar(angles[:, 0, :, :], angles[:, 0, :, :], 3.1415925, -3.1415925, ALU.min, ALU.max).then_inc(angle_ready, 1)

            for layer in range(DEPTH):
                kind = layer % 3
                if kind == 0:
                    qkv = tok(1536)
                    step_copy(lambda q: [(qkv[:, :, q * UW:(q + 1) * UW], 0, 512)], 6)
                    wait_steps(dve, at.v)
                    for tt in range(TT):
                        rows = in_rows(qkv[:, tt, 0:A_HEADS * A_HD], A_HEADS, A_HD // 2)
                        rotate(rows, rope_t[:, tt, 0, :], rope_t[:, tt, 1, :], [((0, A_HEADS), [rows[:, :, e, :] for e in range(2)])])
                        rows = in_rows(qkv[:, tt, A_HEADS * A_HD:], A_KV, A_HD // 2)
                        rotate(rows, rope_t[:, tt, 0, :], rope_t[:, tt, 1, :],
                               [((0, A_KV), [k_dup[:, tt, :, :, e * 32:(e + 1) * 32] for e in range(2)])])
                    turns["swa"]()
                    attend(swa(layer // 3))
                    turns["heads"]()
                    splits(4, keep=1)
                elif kind == 1:
                    gel, u, rg, ig, a_, b_ = lru_parts
                    lam = params[:, COL["b_lambda"]:COL["b_lambda"] + DC]
                    sp0, sp1, sp2, sp3, sp4, sp5 = (softplus[:, i, :] for i in range(6))
                    link(v_.tensor_scalar(sp0, lam, -1.0, None, ALU.mult))
                    link(v_.tensor_tensor(sp1, sp0, lam, ALU.min))
                    v_.tensor_scalar(sp5, sp0, 0.0, None, ALU.max).then_inc(lru_dve, 1)
                    for q in range(8):
                        split(0, at.u + AHEAD, 0)
                        if q < 4:
                            split(0, at.u + AHEAD, 1)
                        else:
                            dve.wait_ge(lru_act, q - 3)
                            bk = step_bank(at.v)
                            for sh in range(1, LRU_TAPS):
                                for c in range(2):
                                    ch = 2 * (q - 4) + c
                                    ins = v_.scalar_tensor_tensor(out=u[:, ch, sh:S], in0=bk[:, c * S:(c + 1) * S - sh],
                                                                  scalar=col("b_conv_w", (3 - sh) * DC + ch), in1=u[:, ch, sh:S],
                                                                  op0=ALU.mult, op1=ALU.add)
                                    if sh < LRU_TAPS - 1:
                                        k = mark(ins)
                                if sh < LRU_TAPS - 1:
                                    dve.wait_ge(dve_link, k)
                            ins.then_inc(step_out[at.v % 2], 1)
                            split(0, at.u + AHEAD, 1)
                        at.u += 1
                        at.v += 1
                    dve.wait_ge(lru_uhi, 1)
                    v_.tensor_tensor(xt[1][:, :, :], u[:, :, :], xt[0][:, :, :].bitcast(F32), ALU.subtract).then_inc(lru_ulo, 1)
                    dve.wait_ge(lru_pool_exp, 1)
                    link(v_.tensor_scalar(sp0, sp2, 2.0, None, ALU.add))
                    link(v_.reciprocal(sp3, sp0))
                    link(v_.tensor_tensor(sp0, sp2, sp3, ALU.mult))
                    link(v_.tensor_tensor(sp1, sp0, sp0, ALU.mult))
                    link(v_.tensor_scalar(sp3, sp1, 1.0 / 17, 1.0 / 15, ALU.mult, ALU.add))
                    for k in range(13, 0, -2):
                        link(v_.tensor_tensor(sp3, sp3, sp1, ALU.mult))
                        link(v_.tensor_scalar(sp3, sp3, 1.0 / k, None, ALU.add))
                    link(v_.tensor_tensor(sp3, sp3, sp0, ALU.mult))
                    link(v_.scalar_tensor_tensor(out=sp5, in0=sp3, scalar=2.0, in1=sp5, op0=ALU.mult, op1=ALU.add))
                    v_.tensor_scalar(sp5, sp5, -LRU_C, None, ALU.mult).then_inc(lru_dve, 1)
                    splits(2)
                    at.v += 2 * LRU_BLOCKS
                    dve.wait_ge(lru_act, 5)
                    wait_steps(dve, at.v)
                    link(v_.tensor_tensor(ig[:, :, :], ig[:, :, :], u[:, :, :], ALU.mult))
                    link(v_.tensor_tensor(u[:, :, :], a_[:, :, :], a_[:, :, :], ALU.mult))
                    link(v_.tensor_scalar(u[:, :, :], u[:, :, :], -1.0, -1.0, ALU.mult, ALU.add))
                    v_.tensor_tensor(b_[:, :, :], b_[:, :, :], u[:, :, :], ALU.mult).then_inc(lru_dve, 1)
                    dve.wait_ge(lru_act, 6)
                    link(v_.tensor_tensor(b_[:, :, :], rg[:, :, :], ig[:, :, :], ALU.mult))
                    for ch in range(DC):
                        v_.tensor_tensor_scan(u[:, ch, :], a_[:, ch, :], b_[:, ch, :], 0.0, ALU.mult, ALU.add).then_inc(lru_dve, 1)
                    splits(4, keep=1)
                else:
                    low = tok(C_DOWN)
                    step_copy(lambda q: [(low[:, :, q * UW:(q + 1) * UW], 0, 512)], 2)
                    step_copy(lambda q: [(low[:, :, 2 * UW:C_DOWN], 0, 2 * (C_DOWN - 2 * UW))], 1)
                    wait_steps(dve, at.v)
                    for tt in range(TT):
                        rows = low[:, tt, C_QR + C_KVR:C_DOWN].rearrange("p (h e d) -> p h e d", e=2, d=C_ROPE // 2)
                        rotate(rows, rope_t[:, tt, 0, :], rope_t[:, tt, 1, :], [((0, 1), [rows[:, :, e, :] for e in range(2)])])
                    at.sq += 1
                    dve.wait_ge(ssq_ready, at.sq)
                    for t, width in enumerate((C_QR, C_KVR)):
                        ins = v_.tensor_scalar(var[:, at.col + t:at.col + 4:2], ssq[:, at.col + t:at.col + 4:2], 1.0 / width, RMS_EPS,
                                               ALU.mult, ALU.add)
                    ins.then_inc(var_ready, 1)
                    at.msq += 1
                    dve.wait_ge(rstd_ready, at.msq)
                    for tt in range(TT):
                        for t, (c0, c1) in enumerate(((0, C_QR), (C_QR, C_QR + C_KVR))):
                            k = at.col + 2 * tt + t
                            ins = v_.tensor_scalar(low[:, tt, c0:c1], low[:, tt, c0:c1], rstd[:, k:k + 1], None, ALU.mult)
                    ins.then_inc(mla_scaled, 1)
                    at.col += 4
                    turns["mla_low"]()
                    step_copy(lambda q: [(qt[:, q, :], 0, S), (mla_qr()[:, :, q, :], S, S + 2 * C_ROPE)], 8)
                    wait_steps(dve, at.v)
                    for tt in range(TT):
                        rows = mla_qr()[:, tt, :, :].rearrange("p h (e d) -> p h e d", e=2)
                        rotate(rows, rope_t[:, tt, 0, :], rope_t[:, tt, 1, :], [((0, C_HEADS), [rows[:, :, e, :] for e in range(2)])])
                    step_copy(lambda q: [(kt[:, q, :], 0, S), (mla_v()[:, :, q * P:(q + 1) * P], S, 2 * S)], 8)
                    turns["mla_q"]()
                    attend(mla())
                    turns["heads"]()
                    splits(4, keep=1)
                layer_norm()
                turns["norm"](lambda c, n=3 * layer: (col("ln_g", n * DC + c), col("ln_b", n * DC + c)))
                step_copy(lambda q: [(qt[:, 2 * q:2 * q + 2, :], 0, 512)], 4)
                attend(cross())
                turns["heads"]()
                splits(4, keep=1)
                layer_norm()
                turns["norm"](lambda c, n=3 * layer + 1: (col("ln_g", n * DC + c), col("ln_b", n * DC + c)))
                def glu_unit(i, ub, vb, qb, role):
                    par = qb % 2
                    split(i, ub + AHEAD, 0)
                    done = i * SLOTS + (layer * FFC + 2 * qb + role + 1)
                    dve.wait_ge(conv_start, done)
                    bk = step_bank(vb)
                    for sh in (1, 2):
                        for c in range(2):
                            ch = i * 4 + (2 * qb + c + role * FFC)
                            dst = cwork[par][role][:, c, sh:S]
                            if sh == 2 and c == 0:
                                dve.wait_ge(conv_tap, done)
                            ins = v_.scalar_tensor_tensor(out=dst, in0=bk[:, c * S:(c + 1) * S - sh],
                                                          scalar=params[:, bass.ds(ch + (COL["f_conv_w"] + (layer * 3 + 2 - sh) * 2 * FFC), 1)],
                                                          in1=dst, op0=ALU.mult, op1=ALU.add)
                        ins.then_inc(conv_tap if sh == 1 else step_out[vb % 2], 1)
                    split(i, ub + AHEAD, 1)

                u0, v0 = at.u, at.v
                for i, j in unit_groups(dve, u0, 2 * GLU_LAG, peel=1):
                    glu_unit(i, u0 + j, v0 + j, j // 2, j % 2)
                at.u += 2 * GLU_LAG
                at.v += 2 * GLU_LAG
                for what, q in glu_order:
                    if what == "up":
                        for role in range(2):
                            glu_unit(0, at.u, at.v, q, role)
                            at.u += 1
                            at.v += 1
                    else:
                        splits(1, keep=1 if q == N_GLU - 1 else 0)
                layer_norm()
                if layer < DEPTH - 1:
                    turns["norm"](lambda c, n=3 * layer + 2: (col("ln_g", n * DC + c), col("ln_b", n * DC + c)))

            def pre_norm():
                for tt in range(TT):
                    mean_square(D)
                for tt in range(TT):
                    k = at.col - TT + tt
                    dve.wait_ge(rstd_ready, at.msq - TT + tt + 1)
                    v_.tensor_scalar(normed[:, tt, :], resid[:, tt, :], rstd[:, k:k + 1], None, ALU.mult).then_inc(normed_ready, 1)

            def post_norm(gain, src_of):
                for tt in range(TT):
                    mean_square(D)
                for tt in range(TT):
                    k = at.col - TT + tt
                    dve.wait_ge(rstd_ready, at.msq - TT + tt + 1)
                    link(v_.scalar_tensor_tensor(out=normed[:, tt, :], in0=src_of(tt), scalar=rstd[:, k:k + 1], in1=gain,
                                                 op0=ALU.mult, op1=ALU.mult))
                    v_.tensor_tensor(resid[:, tt, :], resid[:, tt, :], normed[:, tt, :], ALU.add).then_inc(resid_ready, 1)
                if at.u < N_UNITS:
                    kept()

            pre_norm()
            turns["norm"](lambda c: (col("g_pre_mix_2", c), None))
            dve.wait_ge(trig_ready, 1)
            link(v_.tensor_tensor(angles[:, 2, :, :], angles[:, 2, :, :], angles[:, 2, :, :], ALU.mult))
            v_.tensor_scalar(angles[:, 2, :, :], angles[:, 2, :, :], -2.0, 1.0, ALU.mult, ALU.add).then_inc(trig_ready, 1)
            dve.wait_ge(trig_ready, 2)
            ret = tok(2048)
            ret_v = tok_at(4096, 2048)
            step_copy(lambda q: [(ret[:, :, q * UW:(q + 1) * UW], 0, 512)], 8)
            step_copy(lambda q: [(ret_v[:, :, q * UW:(q + 1) * UW], 0, 512)], 8)
            wait_steps(dve, at.v)
            half = R_QK // 2
            for pq in range(2):
                for tt in range(TT):
                    for hh in range(0, R_HEADS, 2):
                        c = pq * 1024 + hh * R_QK
                        rows = ret[:, tt, c:c + 2 * R_QK].rearrange("p (h e d) -> p h e d", e=2, d=half)
                        rotate(rows, angles[:, 2, tt, 0:half], angles[:, 1, tt, 0:half], [((0, 2), [rows[:, :, e, :] for e in range(2)])])
            turns["ret_qk"]()
            step_copy(lambda q: [(ret[:, :, q * UW:(q + 1) * UW], 0, 512)], 8)
            dve.wait_ge(tables2_in, 32)
            for h in range(R_HEADS):
                def decayed(h):
                    dve.wait_ge(ret_scores, h + 1)
                    if h >= 2:
                        dve.wait_ge(ret_pv, TT * (h - 1))
                    v_.tensor_tensor(ret_pt[h % 2][:, 0:3 * P], bank[:, STEP + h % 2, 0:3 * P], decay[:, h, :], ALU.mult).then_inc(ret_decayed, 1)
                if h == 0:
                    decayed(0)
                if h + 1 < R_HEADS:
                    decayed(h + 1)
                for tt in range(TT):
                    mean_square(R_V)
                if h == 0:
                    dve.wait_ge(gate_sig, 1)
                for tt in range(TT):
                    k = at.col - TT + tt
                    dve.wait_ge(rstd_ready, at.msq - TT + tt + 1)
                    g = ret[:, tt, h * R_V:(h + 1) * R_V]
                    v_.scalar_tensor_tensor(out=g, in0=bank[:, ACC + 2 * (h % 2) + tt, :], scalar=rstd[:, k:k + 1], in1=g,
                                            op0=ALU.mult, op1=ALU.mult).then_inc(ret_norm, 1)
            turns["ret_out"]()
            splits(8)
            for tt in range(TT):
                wait_acc(tt)
                v_.tensor_copy(mem_v[:, tt, :], acc_tile(tt)).then_inc(branch_out, 1)
            dil = tok(2 * D_W)
            dil_v = tok_at(2 * TT * D_W, D_W)
            step_copy(lambda q: [(dil[:, :, bass.ds(q * UW, UW)], 0, 512)], 12)
            step_copy(lambda q: [(dil_v[:, :, q * UW:(q + 1) * UW], 0, 512)], 6)
            wait_steps(dve, at.v)
            rh = D_ROT // 2
            for pq in range(2):
                for tt in range(TT):
                    rows = dil[:, tt, pq * D_W:(pq + 1) * D_W].rearrange("p (h d) -> p h d", d=D_HD)[:, :, 0:D_ROT].rearrange("p h (e d) -> p h e d", e=2)
                    rotate(rows, angles[:, 2, tt, half:NF], angles[:, 1, tt, half:NF], [((0, D_W // D_HD), [rows[:, :, e, :] for e in range(2)])])
            turns["dil_qk"]()
            gates = tok(2 * D)
            step_copy(lambda q: [(gates[:, :, q * UW:(q + 1) * UW], 0, 512)], 8)
            wait_steps(dve, at.v)
            gb = 3 * DEPTH
            dve.wait_ge(gains_in, 32 * (gb + 1))
            for tt in range(TT):
                g = gates[:, tt, :]
                ins = v_.tensor_tensor(g, g, gains[:, :, :].rearrange("p a n -> p (a n)"), ALU.add)
            ins.then_inc(gate_in, 1)
            attend(dilated())
            turns["dil_out"]()
            splits(2)
            dve.wait_ge(gate_sig, 2)
            for tt in range(TT):
                wait_acc(tt)
                link(v_.tensor_tensor(mem_v[:, tt, :], mem_v[:, tt, :], gates[:, tt, 0:D], ALU.mult))
                link(v_.tensor_tensor(heads[:, tt, :], acc_tile(tt), gates[:, tt, D:2 * D], ALU.mult))
                v_.tensor_tensor(heads[:, tt, :], heads[:, tt, :], mem_v[:, tt, :], ALU.add).then_inc(mix_ready, 1)
            turns["heads"]()
            splits(4, keep=1)
            gp = gb + 1
            dve.wait_ge(gains_in, 32 * (gp + 1))
            at.acc += 1
            post_norm(gains[:, 0, :], acc_tile)
            pre_norm()
            turns["norm"](lambda c: (col("g_pre_mlp_2", c), None))

            def relu_unit(q):
                split(0, at.u + AHEAD, 0)
                src = cwork[0][q % 2][:, :, :]
                dve.wait_ge(step_out[at.v % 2], at.v // 2 + 1)
                if q >= 2:
                    dve.wait_ge(relu_sq, q - 1)
                v_.tensor_tensor(pwork[q % 2][:, :, :], src, src, ALU.mult).then_inc(relu_prod, 1)
                split(0, at.u + AHEAD, 1)
                at.u += 1
                at.v += 1

            for q in range(RELU_LAG):
                relu_unit(q)
            for what, q in relu_order:
                if what == "up":
                    relu_unit(q)
                else:
                    splits(1, keep=1 if q == N_RELU - 1 else 0)
            at.acc += 1
            post_norm(gains[:, 1, :], acc_tile)
            pre_norm()
            turns["norm"](lambda c: (col("g_pre_ple_2", c), None))
            step_copy(lambda q: [(tok(D)[:, :, q * UW:(q + 1) * UW], 0, 512)], 4)
            turns["p"]()
            wait_steps(dve, at.v)
            ge = gb + 2
            dve.wait_ge(gains_in, 32 * (ge + 1))
            for tt in range(TT):
                ins = v_.tensor_tensor(tok(D)[:, tt, :], tok(D)[:, tt, :], gains[:, 0, :], ALU.add)
            ins.then_inc(ple_in, 1)
            splits(1)
            dve.wait_ge(ple_sig, 1)
            for tt in range(TT):
                wait_acc(tt)
                v_.tensor_tensor(heads[:, tt, :], acc_tile(tt), tok(D)[:, tt, :], ALU.mult).then_inc(ple_prod, 1)
            post_norm(gains[:, 1, :], lambda tt: heads[:, tt, :])

        @block.gpsimd
        def _(pool):
            at = At()
            links = [0]
            g_ = nc.gpsimd

            def link(ins):
                links[0] += 1
                ins.then_inc(pool_link, 1)
                pool.wait_ge(pool_link, links[0])

            def powers(n=1):
                pool.wait_ge(var_ready, at.msq + 1)
                g_.tensor_tensor(rstd[:, at.col:at.col + n], var[:, at.col:at.col + n], minus_half[:, 0:n], ALU.pow).then_inc(rstd_ready, 1)
                at.msq += 1
                at.col += n

            def layer_norm():
                n = at.nrm
                for tt in range(TT):
                    powers()
                pool.wait_ge(gains_in, 32 * (n + 1))
                ga = gains
                for tt in range(TT):
                    pool.wait_ge(normed_ready, TT * n + tt + 1)
                    link(g_.tensor_tensor(resid[:, tt, :], normed[:, tt, :], ga[:, 0, :], ALU.mult))
                    g_.tensor_tensor(resid[:, tt, :], resid[:, tt, :], ga[:, 1, :], ALU.add).then_inc(resid_ready, 1)
                pool.wait_ge(resid_ready, TT * (n + 1))
                pool.sem_inc(gains_used, 1)
                at.nrm += 1

            def rotate(rows, sin):
                k = at.rot
                n, half = rows.shape[1], rows.shape[3]
                if k >= 2:
                    pool.wait_ge(rot_out, k - 1)
                g_.tensor_tensor(rot_s_view(k, n, half), rows, bcast(sin, n, half), ALU.mult).then_inc(rot_sin, 1)
                at.rot += 1

            link(g_.memset(minus_half[:, :], -0.5))
            at.v += 8
            pool.wait_ge(tables_in, 16 * 6)
            for layer in range(DEPTH):
                kind = layer % 3
                if kind == 0:
                    at.v += 6
                    wait_steps(pool, at.v)
                    for tt in range(TT):
                        qkv = tok(1536)
                        rotate(in_rows(qkv[:, tt, 0:A_HEADS * A_HD], A_HEADS, A_HD // 2), rope_t[:, tt, 1, :])
                        rotate(in_rows(qkv[:, tt, A_HEADS * A_HD:], A_KV, A_HD // 2), rope_t[:, tt, 1, :])
                elif kind == 1:
                    pool.wait_ge(lru_dve, 1)
                    link(g_.memset(softplus[:, 4, :], float(np.e)))
                    g_.tensor_tensor(softplus[:, 2, :], softplus[:, 4, :], softplus[:, 1, :], ALU.pow).then_inc(lru_pool_exp, 1)
                    at.v += 8 + 2 * LRU_BLOCKS
                    gel, u, rg, ig, a_, b_ = lru_parts
                    for ch in range(DC):
                        pool.wait_ge(lru_dve, LRU_SP + 2 + ch)
                        g_.tensor_tensor(ig[:, ch, :], u[:, ch, :], gel[:, ch, :], ALU.mult).then_inc(lru_pool, 1)
                        if ch % 2:
                            pool.wait_ge(lru_hi, ch // 2 + 1)
                            g_.tensor_tensor(ht[1][:, ch - 1:ch + 1, :], ig[:, ch - 1:ch + 1, :], ht[0][:, ch - 1:ch + 1, :].bitcast(F32),
                                             ALU.subtract).then_inc(lru_lo, 1)
                else:
                    at.v += 3
                    wait_steps(pool, at.v)
                    low = tok(C_DOWN)
                    for tt in range(TT):
                        rotate(low[:, tt, C_QR + C_KVR:C_DOWN].rearrange("p (h e d) -> p h e d", e=2, d=C_ROPE // 2), rope_t[:, tt, 1, :])
                    powers(4)
                    at.v += 8
                    wait_steps(pool, at.v)
                    for tt in range(TT):
                        rotate(mla_qr()[:, tt, :, :].rearrange("p h (e d) -> p h e d", e=2), rope_t[:, tt, 1, :])
                    at.v += 8
                layer_norm()
                at.v += 4
                layer_norm()
                def glu_product(i, vb, qb):
                    par = qb % 2
                    pool.wait_ge(glu_gate, i * 2 + (layer * N_GLU + qb + 1))
                    pool.wait_ge(step_out[vb % 2], i * 2 + vb // 2 + 1)
                    if not (isinstance(i, int) and 2 * i + qb < 2 and layer == 0):
                        pool.wait_ge(glu_out, i * 2 + (layer * N_GLU + qb - 1))
                    g_.tensor_tensor(pwork[par][:, :, :], swork[par][:, :, :], cwork[par][1][:, :, :], ALU.mult).then_inc(glu_prod, 1)
                    if not (isinstance(i, int) and 2 * i + qb == 0):
                        glu_low(i, qb - 1)

                def glu_low(i, qb):
                    pool.wait_ge(glu_hi, i * 2 + (layer * N_GLU + qb + 1))
                    if isinstance(i, int):
                        c = (4 * i + 2 * qb) % HC
                        hi, lo = (x[:, c:c + 2, :] for x in ht)
                    else:
                        hi, lo = (x[:, bass.ds(i * 4 + 2 * qb, 2), :] for x in ht)
                    g_.tensor_tensor(lo, pwork[qb % 2][:, :, :], hi.bitcast(F32), ALU.subtract).then_inc(glu_out, 1)

                v0 = at.v
                for i, j in unit_groups(pool, SLOTS, 2 * GLU_LAG, peel=1):
                    if j % 2 == 1:
                        glu_product(i, v0 + j, j // 2)
                for q in range(GLU_LAG, N_GLU):
                    glu_product(0, v0 + 2 * q + 1, q)
                glu_low(0, N_GLU - 1)
                at.v += FFC
                layer_norm()
            for tt in range(TT):
                powers()
            pool.wait_ge(trig_ready, 2)
            at.v += 16
            wait_steps(pool, at.v)
            ret = tok(2048)
            half = R_QK // 2
            for pq in range(2):
                for tt in range(TT):
                    for hh in range(0, R_HEADS, 2):
                        c = pq * 1024 + hh * R_QK
                        rotate(ret[:, tt, c:c + 2 * R_QK].rearrange("p (h e d) -> p h e d", e=2, d=half), angles[:, 1, tt, 0:half])
            for h in range(R_HEADS):
                for tt in range(TT):
                    powers()
            at.v += 8 + 18
            wait_steps(pool, at.v)
            dil = tok(2 * D_W)
            for pq in range(2):
                for tt in range(TT):
                    rows = dil[:, tt, pq * D_W:(pq + 1) * D_W].rearrange("p (h d) -> p h d", d=D_HD)[:, :, 0:D_ROT].rearrange("p h (e d) -> p h e d", e=2)
                    rotate(rows, angles[:, 1, tt, half:NF])
            pool.wait_ge(gate_in, 1)
            pool.sem_inc(gains_used, 1)
            for k in range(5):
                for tt in range(TT):
                    powers()
                if k == 1:
                    for q in range(N_RELU):
                        pool.wait_ge(relu_hi, q + 1)
                        hi, lo = (x[:, 2 * q % HC:2 * q % HC + 2, :] for x in ht)
                        g_.tensor_tensor(lo, pwork[q % 2][:, :, :], hi.bitcast(F32), ALU.subtract).then_inc(relu_sq, 1)
                if k == 2:
                    pool.wait_ge(resid_ready, TT * (3 * DEPTH + 2))
                    pool.sem_inc(gains_used, 1)


def kernel(**inputs):
    import concourse.bacc as bacc
    from concourse.bass_utils import run_bass_kernel_spmd as run

    nc = bacc.Bacc("TRN2", target_bir_lowering=False, num_devices=1, dynamic_dma_scratch_size=1024)
    arrays, args = {}, {}
    for name, value in {**inputs, **shape_constants()}.items():
        a = np.ascontiguousarray(value)
        a = a.reshape(LAYOUT[name]) if name in LAYOUT else a
        arrays[f"in_{name}"] = a
        args[name] = nc.dram_tensor(f"in_{name}", a.shape, mybir.dt.from_np(a.dtype), kind="ExternalInput").ap()
    out = nc.dram_tensor("out", (S, D), F32, kind="ExternalOutput").ap()
    build(nc, args, out)
    r = run(nc, [arrays], core_ids=[0])
    return r.results[0]["out"].reshape(1, S, D)
```

```python
from contextlib import ExitStack

import numpy as np

import concourse.bass as bass
from concourse import mybir

F32 = mybir.dt.float32
F32R = mybir.dt.float32r
I32 = mybir.dt.int32
ALU = mybir.AluOpType
ACT = mybir.ActivationFunctionType
AX = mybir.AxisListType

P = 128
S = 256
D = 1024
DEPTH = 4
TT = S // P
DC = D // P
SLOTS = 4
AHEAD = 2
HC = 16
UW = 256
NEG = -1e30
LN_EPS = 1e-5
RMS_EPS = 1e-6
ALPHA = (2.0 * DEPTH) ** 0.25

A_HEADS, A_KV, A_HD = 16, 4, 64
LRU_BLOCKS, LRU_TAPS, LRU_C = 4, 4, 8.0
C_HEADS, C_NOPE, C_ROPE, C_QR, C_KVR = 8, 128, 64, 384, 256
C_DOWN = C_QR + C_KVR + C_ROPE
X_HEADS, X_HD = 4, 256
FF, FFC, F_TAPS = 2816, 22, 3
FF2 = 4096
R_HEADS, R_QK, R_V = 4, 256, 512
D_SLOTS, D_GROUPS, D_HD, D_ROT = 8, ((128, 1), (512, 4), (2048, 16)), 64, 16
D_W = D_SLOTS * len(D_GROUPS) * D_HD
R_COLS = 2 * R_HEADS * R_QK + 2 * R_HEADS * R_V
D_COLS = 3 * D_W + 2 * D
NF = R_QK // 2 + D_ROT // 2
TWO_PI = 2 * np.pi
PI_1 = 6.28125
PI_2 = 2029 / 2.0**20
PI_3 = TWO_PI - PI_1 - PI_2
ROUND = 12582912.0
LRU_SP = 2

PARAM_ROWS = [
    ("ln_g", 96), ("ln_b", 96), ("f_conv_w", 528), ("f_conv_b", 176), ("b_conv_w", 32), ("b_conv_b", 8),
    ("b_b_rgate", 8), ("b_b_igate", 8), ("b_lambda", 8), ("c_q_norm", 3), ("c_kv_norm", 2),
    ("g_pre_mix_2", 8), ("g_pre_mlp_2", 8), ("g_pre_ple_2", 8),
]
COL = {}
_at = 0
for _name, _rows in PARAM_ROWS:
    COL[_name] = _at
    _at += _rows
PARAMS = _at

ACC, STEP, TURN = 0, 4, 6


def shape_constants():
    f = np.float32
    inv = f(1.0) / (f(10000.0) ** (np.arange(0, A_HD, 2, dtype=f) / f(A_HD)))
    ang = np.arange(S, dtype=f)[:, None] * inv[None, :]
    rope = np.stack([np.cos(ang), np.sin(ang)], 1).astype(f)
    q = np.arange(P)[:, None]
    k = np.arange(P)[None, :]
    causal = np.where(q >= k, 0.0, NEG)
    window = np.where(k > q, 0.0, NEG)
    mask_a = np.concatenate([causal, window, causal], 1)
    mask_c = np.concatenate([causal, np.zeros((P, P)), causal], 1)
    parts = []
    for tt in range(TT):
        for span, dil in D_GROUPS:
            dist = q + tt * P - np.arange((tt + 1) * P)[None, :]
            parts.append(np.where((dist >= 0) & (dist % dil == 0) & (dist <= span), 0.0, NEG))
    mask_d = np.concatenate(parts, 1)
    log_gamma = np.log1p(-(2.0 ** (-5.0 - np.arange(R_HEADS))))
    diff = np.arange(S)[None, :] - np.arange(P)[:, None]
    dec = np.where(diff[None] >= 0, np.exp(np.maximum(diff, 0)[None] * log_gamma[:, None, None]), 0.0) * R_QK**-0.5
    dec = np.concatenate([dec, dec[:, :, :P]], 2).transpose(1, 0, 2)
    fr = f(1.0) / (f(10000.0) ** np.linspace(0.0, 1.0, R_QK // 2, dtype=f))
    fd = f(500000.0) ** (-np.arange(0, D_ROT, 2, dtype=f) / f(D_ROT))
    return {
        "k_ident": np.eye(P, dtype=f), "k_rope": rope, "k_mask_a": mask_a.astype(f), "k_mask_c": mask_c.astype(f),
        "k_mask_d": mask_d.astype(f), "k_decay": np.ascontiguousarray(dec.astype(f)),
        "k_freq": np.concatenate([fr, fd]).astype(f)[None, :],
    }


LAYOUT = {
    "x": (S, D), "mem": (S, D), "p_2": (S, 256), "positions_2": (S,), "w_in_2": (D, R_COLS + D_COLS), "b_gate_2": (2, D),
    "w_ret_out_2": (R_HEADS * R_V, D), "w_dil_out_2": (D_SLOTS * D_HD, D), "w_o_2": (D, D), "g_pre_mix_2": (D,),
    "g_post_mix_2": (D,), "g_pre_mlp_2": (D,), "g_post_mlp_2": (D,), "w_up_2": (D, FF2), "w_down_2": (FF2, D),
    "g_pre_ple_2": (D,), "w_ple_gate_2": (D, D), "b_ple_gate_2": (D,), "w_ple_in_2": (256, D), "g_post_ple_2": (D,),
}


def build(nc, w, out):
    param_views = {}
    for name, rows in PARAM_ROWS:
        v = w[name]
        axes = "abcd"[:len(v.shape) - 1]
        names = " ".join(axes)
        param_views[name] = v.rearrange(f"{names} (c f) -> ({names} c) f", f=P)
    n_row_loads = 0
    _r = 0
    for name, rows in PARAM_ROWS:
        n_row_loads += (_r + rows - 1) // P - _r // P + 1
        _r += rows
    with ExitStack() as ctx:
        sb = lambda name, shape, dt=F32: ctx.enter_context(nc.sbuf_tensor(name, shape, dt))
        sem = lambda name: ctx.enter_context(nc.semaphore(name))

        ring_at = (nc.sbuf_base + 31) // 32 * 32
        sb("ring_region", [P, SLOTS * 2048 + 8])
        w_hi = [sb(f"w_hi{i}", [P, 2048], F32R) for i in range(SLOTS)]
        resid = sb("resid", [P, TT, D])
        work = sb("work", [P, 9216])
        heads = sb("heads", [P, TT, D])
        qt = sb("qt", [P, DC, S])
        kt = sb("kt", [P, DC, S])
        mem_kt = sb("mem_kt", [P, DC, S])
        mem_v = sb("mem_v", [P, TT, D])
        gains = sb("gains", [P, 2, D])
        params = sb("params", [P, PARAMS])
        ident = sb("ident", [P, P])
        rope_t = sb("rope_t", [P, TT, 2, A_HD // 2])
        mask_a = sb("mask_a", [P, 3 * P])
        mask_c = sb("mask_c", [P, 3 * P])
        sinks = sb("sinks", [P, 2 * A_HEADS])
        stat = [sb(f"stat{i}", [P, 12]) for i in range(2)]
        var = sb("var", [P, 96])
        rstd = sb("rstd", [P, 96])
        ssq = sb("ssq", [P, 96])
        bn = sb("bn", [P, TT, 2, 6])
        bn_mv = sb("bn_mv", [P, TT, 2])
        minus_half = sb("minus_half", [P, 4])
        softplus = sb("softplus", [P, 6, DC])
        angles = sb("angles", [P, 3, TT, NF])
        pos_i = sb("pos_i", [P, TT], I32)
        pos_f = sb("pos_f", [P, TT])
        freq = sb("freq", [P, NF])
        x_at = (nc.sbuf_base + 31) // 32 * 32
        h_at = x_at + 2 * DC * S * 4
        sb("parts_region", [P, 2 * (DC + HC) * S + 8])
        at_byte = lambda name, shape, dt, byte: nc.alloc_sbuf_tensor_at(name, shape, dt, offset=byte)
        ring = [at_byte(f"ring{i}", [P, 2048], F32, ring_at + i * 2048 * 4) for i in range(SLOTS)]
        w_lo = [at_byte(f"w_lo{i}", [P, 2048], F32R, ring_at + i * 2048 * 4) for i in range(SLOTS)]
        xt = [at_byte(f"xt_{n}", [P, DC, S], F32R, x_at + i * DC * S * 4) for i, n in enumerate(("hi", "lo"))]
        ht = [at_byte(f"ht_{n}", [P, HC, S], F32R, h_at + i * HC * S * 4) for i, n in enumerate(("hi", "lo"))]
        xt_plain = at_byte("xt_plain", [P, 2 * DC * S], F32, x_at)
        ht_plain = at_byte("ht_plain", [P, 2 * HC * S], F32, h_at)
        bank = ctx.enter_context(nc.psum_tensor("bank", [P, 8, 512], F32))

        tok_at = lambda first, cols: work[:, first:first + TT * cols].rearrange("p (t c) -> p t c", t=TT)
        tok = lambda cols: tok_at(0, cols)
        part = lambda i: work[:, i * 2048:(i + 1) * 2048].rearrange("p (c s) -> p c s", s=S)
        normed = tok_at(7168, D)
        heads_feat = heads[:, :, :].rearrange("p t f -> p (t f)").rearrange("p (c s) -> p c s", s=S)
        flat_heads = heads[:, :, :].rearrange("p t f -> p (t f)")
        stage_rows = work[:, 0:1024].rearrange("p (a f) -> p a f", f=P)
        k_dup = work[:, 4096:4096 + TT * A_KV * P].rearrange("p (t h e d) -> p t h e d", t=TT, h=A_KV, e=2)
        mla_qr = lambda: work[:, 2048:2048 + TT * C_HEADS * C_ROPE].rearrange("p (t h d) -> p t h d", t=TT, h=C_HEADS)
        mla_v = lambda: tok_at(4096, D)
        latent_q = [[qt[:, 2 * q:2 * q + 2, :], mla_qr()[:, :, 2 * q:2 * q + 2, :]] for q in range(4)]
        latent_kv = [[kt[:, 4 * q:4 * q + 2, :], kt[:, 4 * q + 2:4 * q + 4, :]] +
                     [mla_v()[:, t, q * 512:(q + 1) * 512] for t in range(TT)] for q in range(2)]
        q_rope_t = ht_plain[0:C_ROPE, 2048:4096].rearrange("p (h s) -> p h s", s=S)
        k_rope_t = ht_plain[0:C_ROPE, 5632:5632 + S]
        dil_qk = ht_plain[:, 0:2 * D_W // P * S].rearrange("p (c s) -> p c s", s=S)
        masked = [xt_plain[:, i * 512:(i + 1) * 512] for i in range(2)]
        probs = [xt_plain[:, 1024 + i * 512:1536 + i * 512] for i in range(2)]
        probs_t = [xt_plain[:, 2048 + i * 512:2560 + i * 512] for i in range(2)]
        ret_pt = [flat_heads[:, i * 512:(i + 1) * 512] for i in range(2)]
        ret_junk = [flat_heads[:, 1024 + i * 512:1536 + i * 512] for i in range(2)]

        def in_rows(flat, n, half):
            return flat[:, 0:n * 2 * half].rearrange("p (h e d) -> p h e d", e=2, d=half)

        rot_c_view = lambda k, n, half: in_rows(heads[:, k % 2, :], n, half)
        rot_s_view = lambda k, n, half: in_rows(ht_plain[:, 6144 + k % 2 * 1024:7168 + k % 2 * 1024], n, half)

        def bcast(table, n, half):
            return table.unsqueeze(1).unsqueeze(1).to_broadcast([P, n, 2, half])

        def flat2(x):
            return x[:, :, :].rearrange("p c s -> p (c s)")

        wide_bufs = [[x[:, i * 768:(i + 1) * 768] for i in range(2)] for x in (flat2(qt), flat2(kt), xt_plain)]
        pair_view = lambda first: work[:, first:first + 512].rearrange("p (c s) -> p c s", s=S)
        cwork = [[pair_view((2 * i + j) * 512) for j in range(2)] for i in range(2)]
        swork = [pair_view(2048 + i * 512) for i in range(2)]
        pwork = [pair_view(3072 + i * 512) for i in range(2)]
        mask_d = flat2(mem_kt)[:, 0:9 * P]
        decay = flat2(mem_v)[:, 0:R_HEADS * 3 * P].rearrange("p (h c) -> p h c", h=R_HEADS)

        w_full = [sem(f"w_full{i}") for i in range(SLOTS)]
        halves_used = sem("halves_used")
        split_hi, split_lo = sem("split_hi"), [sem(f"split_lo{i}") for i in range(SLOTS)]
        acc_ready, latent_step = sem("acc_ready"), sem("latent_step")
        ln_turned, ln_hi, ln_lo = sem("ln_turned"), sem("ln_hi"), sem("ln_lo")
        turn_hi, scaled_out = sem("turn_hi"), sem("scaled_out")
        glu_hi, glu_prod = sem("glu_hi"), sem("glu_prod")
        relu_prod, relu_hi = sem("relu_prod"), sem("relu_hi")
        lru_uhi, lru_ulo, lru_hi, lru_lo = (sem(n) for n in ("lru_uhi", "lru_ulo", "lru_hi", "lru_lo"))
        gate_step = sem("gate_step")
        step_out = [sem("step_out0"), sem("step_out1")]
        turn_done = sem("turn_done")
        turn_out = [sem("turn_out0"), sem("turn_out1")]
        ident_in, x_in, mem_in, rows_in, tables_in = (sem(n) for n in ("ident_in", "x_in", "mem_in", "rows_in", "tables_in"))
        tables2_in, p_in, out_written = sem("tables2_in"), sem("p_in"), sem("out_written")
        gains_in = sem("gains_in")
        gains_used = sem("gains_used")
        half_set = sem("half_set")
        var_ready, rstd_ready, ssq_ready = sem("var_ready"), sem("rstd_ready"), sem("ssq_ready")
        normed_ready, resid_ready = sem("normed_ready"), sem("resid_ready")
        dve_link, act_link, pool_link = sem("dve_link"), sem("act_link"), sem("pool_link")
        scores_done, soft_done, exp_done, pt_done, pt_out, pv_done, head_out = (
            sem(n) for n in ("scores_done", "soft_done", "exp_done", "pt_done", "pt_out", "pv_done", "head_out"))
        conv_start, conv_tap, glu_gate, glu_out = (sem(n) for n in ("conv_start", "conv_tap", "glu_gate", "glu_out"))
        rot_cos, rot_sin, rot_out = sem("rot_cos"), sem("rot_sin"), sem("rot_out")
        lru_act, lru_dve, lru_pool, lru_pool_exp = (sem(n) for n in ("lru_act", "lru_dve", "lru_pool", "lru_pool_exp"))
        mla_sq, mla_scaled = sem("mla_sq"), sem("mla_scaled")
        ret_scores, ret_decayed, ret_pv, ret_norm = (sem(n) for n in ("ret_scores", "ret_decayed", "ret_pv", "ret_norm"))
        relu_out, relu_sq = sem("relu_out"), sem("relu_sq")
        angle_ready, trig_ready = sem("angle_ready"), sem("trig_ready")
        branch_out, gate_in, gate_sig, mix_ready = (sem(n) for n in ("branch_out", "gate_in", "gate_sig", "mix_ready"))
        ple_in, ple_sig, ple_prod = sem("ple_in"), sem("ple_sig"), sem("ple_prod")
        block = ctx.enter_context(nc.Block())

        lru_parts = (qt[:, :, :], kt[:, :, :], part(0), part(1), part(2), heads_feat)
        p_tok = tok_at(4096, 256)

        class At:

            def __init__(self):
                self.u = self.v = self.r = self.n = self.rot = self.msq = self.col = self.sq = self.nrm = self.acc = self.th = self.sc = self.ln = self.lat = 0

        FULL = (1024, 1024)
        mixer_units = [[FULL] * 10, [FULL] * 14, [FULL] * 2 + [(4 * 192,) * 2] + [(384, 768)] * 4 + [FULL] * 6]
        unit_sizes = [FULL] * 8
        behind_norm = []
        for layer in range(DEPTH):
            for units in (mixer_units[layer % 3], [FULL] * 8, [FULL] * (FFC + FFC // 2)):
                unit_sizes += units
                behind_norm.append(len(unit_sizes))
        unit_sizes += [FULL] * (24 + 8 + 26 + 2 + 4 + 16 + 16 + 4 + 1)
        N_UNITS = len(unit_sizes)

        pool_units = {u + 1 for u in behind_norm}

        def half_of(x, i, ub, h):
            sizes = unit_sizes[4 * i + ub] if isinstance(i, int) else FULL
            return x[ub % SLOTS][:, h * sizes[0]:h * sizes[0] + sizes[h]]

        def lows(i, ub, h):
            return i * 2 + 2 * (ub // SLOTS) + h + 1

        def low_part(eng, vec, i, ub, h):
            if isinstance(i, int) and 4 * i + ub >= N_UNITS:
                return
            eng.wait_ge(split_hi, i * (2 * SLOTS) + 2 * ub + h + 1)
            raw, hi, lo = (half_of(x, i, ub, h) for x in (ring, w_hi, w_lo))
            vec.tensor_tensor(lo, raw, hi.bitcast(F32), ALU.subtract).then_inc(split_lo[ub % SLOTS], 1)

        def unit_groups(eng, u0, n, peel=0, loops=3):
            full = n // SLOTS
            start = full if (u0 < SLOTS or full - peel < loops) else peel
            for i in range(start):
                for j in range(SLOTS):
                    yield i, j
            if start < full:
                with eng.Fori(start, full) as i:
                    for j in range(SLOTS):
                        yield i, j
            for j in range(n - SLOTS * full):
                yield full, j

        GLU_LAG, RELU_LAG = HC // 2, HC // 2
        N_GLU, N_RELU = FFC // 2, FF2 // UW

        def interleave(n, lag):
            order = []
            for q in range(n):
                order.append(("down", q))
                if q + lag < n:
                    order.append(("up", q + lag))
            return order

        glu_order, relu_order = interleave(N_GLU, GLU_LAG), interleave(N_RELU, RELU_LAG)

        def slot_of(u0, j):
            return (u0 + j) % SLOTS

        def fills(u0, i, j):
            return i * 16 + 16 * ((u0 + j) // SLOTS + 1)

        def pairs_before(v0, i, j):
            return i * 2 + (v0 + j) // 2

        def wait_step(eng, v):
            eng.wait_ge(step_out[v % 2], v // 2 + 1)

        def wait_turn(eng, r):
            eng.wait_ge(turn_out[r % 2], r // 2 + 1)

        def wait_turns(eng, r_end):
            wait_turn(eng, r_end - 1)
            wait_turn(eng, r_end - 2)

        def wait_steps(eng, v_end):
            wait_step(eng, v_end - 1)
            wait_step(eng, v_end - 2)

        def step_bank(v):
            return bank[:, STEP + v % 2, :]

        def turn_bank(r):
            return bank[:, TURN + r % 2, :]

        def ln_bank(tt, h):
            return bank[:, STEP + 2 * tt + h, :]

        def acc_bank(tt, half):
            return bank[:, ACC + 2 * tt + half, :]

        def acc_tile(tt):
            return bank[:, ACC + 2 * tt:ACC + 2 * tt + 2, :].rearrange("p a b -> p (a b)")

        def for_turns(at, copy, split, scaled):

            def wide(how, dst, chunks, tts=range(TT), base=0):
                for tt in tts:
                    for c in range(0, chunks, 4):
                        m = min(4, chunks - c)
                        at_c = (slice(None), slice(base + c, base + c + m), slice(tt * P, (tt + 1) * P))
                        if how is copy:
                            copy([(dst[at_c], (0, m * P))])
                        else:
                            split(dst[0][at_c], dst[1][at_c], m)

            def setup():
                copy([(params[:, 0:4 * P], (0, 4 * P))])
                copy([(params[:, 4 * P:PARAMS], (0, PARAMS - 4 * P))])
                wide(split, xt, DC)

            def swa_turns():
                for tt in range(TT):
                    wide(copy, qt, DC, [tt])
                    wide(copy, kt, A_KV, [tt])

            def norm(gain):
                for tt in range(TT):
                    for c in range(0, DC, 4):
                        t = slice(tt * P, (tt + 1) * P)
                        scaled([(heads_feat[:, c + k, t], (k * P, (k + 1) * P), *gain(c + k)) for k in range(4)],
                               heads_feat[:, c:c + 4, t], xt[0][:, c:c + 4, t], xt[1][:, c:c + 4, t])

            def mla_low():
                for tt in range(TT):
                    t = slice(tt * P, (tt + 1) * P)
                    scaled([(heads_feat[:, c, t], (c * P, (c + 1) * P), col("c_q_norm", c) if c < 3 else col("c_kv_norm", 0), None)
                            for c in range(4)], heads_feat[:, 0:4, t], ht[0][:, 0:4, t], ht[1][:, 0:4, t])
                    scaled([(k_rope_t[:, t], (P, 2 * P), None, None), (heads_feat[:, 4, t], (0, P), col("c_kv_norm", 1), None)],
                           heads_feat[:, 4, t], ht[0][:, 4, t], ht[1][:, 4, t])

            def mla_q():
                for tt in range(TT):
                    for h in range(0, C_HEADS, 4):
                        copy([(q_rope_t[:, h:h + 4, tt * P:(tt + 1) * P], (0, 4 * P))])

            def ret_qk():
                for dst in (qt, kt):
                    wide(copy, dst, DC)

            def dil_turns():
                for pq in range(2):
                    wide(copy, dil_qk, D_W // P, base=pq * (D_W // P))

            def p_turn():
                for tt in range(TT):
                    split(ht[0][:, 0:2, tt * P:(tt + 1) * P], ht[1][:, 0:2, tt * P:(tt + 1) * P], 2)

            return {"mem": lambda: wide(split, ht, DC), "setup": setup, "swa": swa_turns, "heads": lambda: wide(split, ht, DC), "norm": norm, "mla_low": mla_low,
                    "mla_q": mla_q, "ret_qk": ret_qk, "ret_out": lambda: wide(split, ht, 2 * DC), "dil_qk": dil_turns,
                    "dil_out": lambda: wide(split, ht, 4), "p": p_turn}

        col = lambda name, i: params[:, COL[name] + i:COL[name] + i + 1]

        class Attention:
            def __init__(self, count, segs, scale, mask, sink, scores, pv, dest, wide=False):
                self.count, self.segs, self.scale, self.mask, self.sink = count, segs, scale, mask, sink
                self.scores, self.pv, self.dest, self.wide = scores, pv, dest, wide

            def bufs(self, n):
                return [x[n % 2] for x in (wide_bufs if self.wide else (masked, probs, probs_t))]

            def s_bank(self, i):
                n = self.segs(i)[-1][1]
                if self.wide:
                    return bank[:, ACC + 2 * (i % 2):ACC + 2 * (i % 2) + 2, :].rearrange("p a b -> p (a b)")[:, 0:n]
                return bank[:, ACC + i % 2, 0:n]

            def t_bank(self, i):
                n = self.segs(i)[-1][1]
                if self.wide:
                    return bank[:, STEP:STEP + 2, :].rearrange("p a b -> p (a b)")[:, 0:n]
                return bank[:, ACC + 2 + i % 2, 0:n]

            def o_bank(self, i):
                return bank[:, (TURN if self.wide else STEP) + i % 2, :]

        causal_segs = lambda i: [(0, P), (P, 3 * P)]

        def swa(layer):
            qkv = tok(1536)

            def scores(h):
                o, kv = h % 2 * A_HD, h // (A_HEADS // A_KV)
                return [(c0, c1, [(qt[o:o + A_HD, h // 2, tt * P:(tt + 1) * P], kt[o:o + A_HD, kv, 0:c1 - c0])])
                        for tt, (c0, c1) in enumerate(causal_segs(h))]

            def pv(h):
                at = (A_HEADS + A_KV + h // (A_HEADS // A_KV)) * A_HD
                v = [qkv[:, kb, at:at + A_HD] for kb in range(TT)]
                return [(0, A_HD, [(0, v[0])]), (A_HD, 2 * A_HD, [(1, v[0]), (2, v[1])])]

            return Attention(A_HEADS, causal_segs, A_HD**-0.5, lambda i: mask_a[:, :],
                             lambda i: sinks[:, layer * A_HEADS + i:layer * A_HEADS + i + 1], scores, pv,
                             lambda i: heads[:, :, i * A_HD:(i + 1) * A_HD])

        def mla():
            v_tok = mla_v()

            def scores(h):
                return [(c0, c1, [(qt[:, h, tt * P:(tt + 1) * P], kt[:, h, 0:c1 - c0]),
                                  (q_rope_t[:, h, tt * P:(tt + 1) * P], k_rope_t[:, 0:c1 - c0])])
                        for tt, (c0, c1) in enumerate(causal_segs(h))]

            def pv(h):
                v = [v_tok[:, kb, h * P:(h + 1) * P] for kb in range(TT)]
                return [(0, P, [(0, v[0])]), (P, 2 * P, [(1, v[0]), (2, v[1])])]

            return Attention(C_HEADS, causal_segs, (C_NOPE + C_ROPE) ** -0.5, lambda i: mask_c[:, :], None, scores, pv,
                             lambda i: heads[:, :, i * P:(i + 1) * P])

        def cross():
            segs = lambda i: [(0, S), (S, 2 * S)]

            def scores(h):
                return [(c0, c1, [(qt[:, 2 * h + c, tt * P:(tt + 1) * P], mem_kt[:, 2 * h + c, :]) for c in range(2)])
                        for tt, (c0, c1) in enumerate(segs(h))]

            def pv(h):
                v = [mem_v[:, kb, h * X_HD:(h + 1) * X_HD] for kb in range(TT)]
                return [(0, X_HD, [(0, v[0]), (1, v[1])]), (X_HD, 2 * X_HD, [(2, v[0]), (3, v[1])])]

            return Attention(X_HEADS, segs, X_HD**-0.5, None, None, scores, pv,
                             lambda i: heads[:, :, i * X_HD:(i + 1) * X_HD])

        def dilated():
            v_tok = tok_at(2 * TT * D_W, D_W)
            n_g = len(D_GROUPS)
            width = lambda i: (i % TT + 1) * P

            def scores(i):
                s, tt, kw = i // TT, i % TT, width(i)
                mms = []
                for g in range(n_g):
                    head = g * D_SLOTS + s
                    o = head % 2 * D_HD
                    mms.append((g * kw, (g + 1) * kw, [(dil_qk[o:o + D_HD, head // 2, tt * P:(tt + 1) * P],
                                                        dil_qk[o:o + D_HD, D_W // P + head // 2, 0:kw])]))
                return mms

            def pv(i):
                s, tt = i // TT, i % TT
                terms = []
                for g in range(n_g):
                    at = (g * D_SLOTS + s) * D_HD
                    terms += [(g * (tt + 1) + kb, v_tok[:, kb, at:at + D_HD]) for kb in range(tt + 1)]
                return [(0, D_HD, terms)]

            return Attention(D_SLOTS * TT, lambda i: [(0, n_g * width(i))], D_HD**-0.5,
                             lambda i: mask_d[:, 0:n_g * P] if i % TT == 0 else mask_d[:, n_g * P:9 * P], None, scores, pv,
                             lambda i: heads[:, i % TT:i % TT + 1, i // TT * D_HD:(i // TT + 1) * D_HD], wide=True)

        @block.sync
        def _(sp):
            at = At()

            def load(n, src, dst=lambda slot: ring[slot][:, :].rearrange("p (k c) -> p k c", k=DC)):
                u0 = at.u
                for i, j in unit_groups(sp, u0, n):
                    if isinstance(i, int) and u0 + 4 * i + j < SLOTS:
                        pass
                    else:
                        sp.wait_ge(halves_used, i * (2 * SLOTS) + 2 * (u0 + j - SLOTS + 1))
                    slot = slot_of(u0, j)
                    sp.dma_start(dst(slot), src(i * SLOTS + j)).then_inc(w_full[slot], 16)
                at.u += n

            def cols(mat, first=0, width=UW, kc=DC):
                view = mat.rearrange("(k p) n -> p k n", p=P)
                return lambda q: view[:, :, bass.ds(q * width + first, width)]

            def packed(kc, width):
                return lambda slot: ring[slot][:, 0:kc * width].rearrange("p (k c) -> p k c", k=kc)

            def rows(mat):
                view = mat.rearrange("(u k p) n -> p u k n", p=P, k=2)
                return lambda q: view[:, bass.ds(q, 1), :, :].rearrange("p a k n -> p (a k) n")

            def load_gains(first, second):
                g = at.nrm
                if g >= 1:
                    sp.wait_ge(gains_used, g)
                for h, row in enumerate((first, second)):
                    sp.dma_start(gains[:, h, :], row.rearrange("(a n) -> a n", a=1).to_broadcast([P, D])).then_inc(gains_in, 16)
                at.nrm += 1

            def square(mat, n_units):
                load(n_units, rows(mat), packed(2, D))

            def load_ln(n):
                load_gains(w["ln_g"][n // 3, n % 3, :], w["ln_b"][n // 3, n % 3, :])

            sp.dma_start(heads[:, :, :], w["mem"].rearrange("(t p) n -> p t n", p=P)).then_inc(mem_in, 16)
            sp.dma_start(ident[:, :], w["k_ident"]).then_inc(ident_in, 16)
            load(4, cols(w["mem_w_kv"]))
            r = 0
            for name, n_rows in PARAM_ROWS:
                v = param_views[name]
                done = 0
                while done < n_rows:
                    k = min(n_rows - done, P - r % P)
                    sp.dma_start(stage_rows[r % P:r % P + k, r // P, :], v[done:done + k, :]).then_inc(rows_in, 16)
                    r += k
                    done += k
            sp.dma_start(resid[:, :, :], w["x"].rearrange("(t p) n -> p t n", p=P)).then_inc(x_in, 16)
            sp.dma_start(rope_t[:, :, :, :], w["k_rope"].rearrange("(t p) e d -> p t e d", p=P)).then_inc(tables_in, 16)
            sp.dma_start(mask_a[:, :], w["k_mask_a"]).then_inc(tables_in, 16)
            sp.dma_start(mask_c[:, :], w["k_mask_c"]).then_inc(tables_in, 16)
            sp.dma_start(sinks[:, :], w["a_sinks"].rearrange("a h -> (a h)").rearrange("(o n) -> o n", o=1).to_broadcast([P, 2 * A_HEADS])).then_inc(tables_in, 16)
            sp.dma_start(freq[:, :], w["k_freq"].to_broadcast([P, NF])).then_inc(tables_in, 16)
            with nc.allow_non_contiguous_dma(reason="256 positions"):
                sp.dma_start(pos_i[:, :], w["positions_2"].rearrange("(t p) -> p t", p=P)).then_inc(tables_in, 16)
            load(4, cols(w["mem_w_kv"], 4 * UW))
            for layer in range(DEPTH):
                kind, j = layer % 3, layer // 3
                if kind == 0:
                    load(6, cols(w["a_w_qkv"][j]))
                    load_ln(3 * layer)
                    square(w["a_w_o"][j], 4)
                elif kind == 1:
                    load(8, cols(w["b_w_in"][j]))
                    for name in ("b_w_igate", "b_w_rgate"):
                        v = w[name][j].rearrange("h (k p) n -> p (h k) n", p=P)
                        load(1, lambda q, v=v: v)
                    load_ln(3 * layer)
                    square(w["b_w_o"][j], 4)
                else:
                    load(2, cols(w["c_w_down"][j]))
                    load(1, cols(w["c_w_down"][j], 2 * UW, C_DOWN - 2 * UW), packed(DC, C_DOWN - 2 * UW))
                    load(4, cols(w["c_w_uq"][j], 0, 2 * (C_NOPE + C_ROPE)), packed(3, 2 * (C_NOPE + C_ROPE)))
                    load(2, cols(w["c_w_ukv"][j], 0, 4 * UW), packed(2, 4 * UW))
                    load_ln(3 * layer)
                    square(w["c_w_o"][j], 4)
                load(4, cols(w["x_w_q"][layer]))
                load_ln(3 * layer + 1)
                square(w["x_w_o"][layer], 4)
                up = w["f_w_up"][layer].rearrange("(k p) (h q n) -> p k h q n", p=P, h=2, n=UW)
                down = w["f_w_down"][layer].rearrange("(u k p) n -> p u k n", p=P, k=2)

                def load_up(i, ub, q, role):
                    slot = ub % SLOTS
                    sp.wait_ge(halves_used, i * (2 * SLOTS) + 2 * (ub - SLOTS + 1))
                    src = up[:, :, role, bass.ds(q, 1), :].rearrange("p k a n -> p k (a n)")
                    sp.dma_start(ring[slot][:, :].rearrange("p (k c) -> p k c", k=DC), src).then_inc(w_full[slot], 16)

                u0 = at.u
                for i, j in unit_groups(sp, u0, 2 * GLU_LAG):
                    load_up(i, u0 + j, i * 2 + j // 2, j % 2)
                at.u += 2 * GLU_LAG
                load_ln(3 * layer + 2)
                for what, q in glu_order:
                    if what == "up":
                        for role in range(2):
                            load_up(0, at.u, q, role)
                            at.u += 1
                    else:
                        slot = at.u % SLOTS
                        sp.wait_ge(halves_used, 2 * (at.u - SLOTS + 1))
                        sp.dma_start(packed(2, D)(slot), down[:, q, :, :]).then_inc(w_full[slot], 16)
                        at.u += 1
            load(24, cols(w["w_in_2"]))
            square(w["w_ret_out_2"], 8)
            load_gains(w["b_gate_2"][0, :], w["b_gate_2"][1, :])
            load(26, cols(w["w_in_2"], R_COLS))
            square(w["w_dil_out_2"], 2)
            square(w["w_o_2"], 4)
            load_gains(w["g_post_mix_2"], w["g_post_mlp_2"])
            load(RELU_LAG, cols(w["w_up_2"]))
            up, down = cols(w["w_up_2"]), rows(w["w_down_2"])
            for what, q in relu_order:
                slot = at.u % SLOTS
                sp.wait_ge(halves_used, 2 * (at.u - SLOTS + 1))
                if what == "up":
                    sp.dma_start(ring[slot][:, :].rearrange("p (k c) -> p k c", k=DC), up(q)).then_inc(w_full[slot], 16)
                else:
                    sp.dma_start(packed(2, D)(slot), down(q)).then_inc(w_full[slot], 16)
                at.u += 1
            load(4, cols(w["w_ple_gate_2"]))
            load_gains(w["b_ple_gate_2"], w["g_post_ple_2"])
            square(w["w_ple_in_2"], 1)
            sp.wait_ge(resid_ready, 12 * DEPTH + TT * 3)
            sp.dma_start(out.rearrange("(t p) n -> p t n", p=P), resid[:, :, :]).then_inc(out_written, 16)
            sp.wait_ge(out_written, 16)

        @block.tensor
        def _(pe):
            at = At()

            def turn(blocks):
                r = at.r
                if r >= 2:
                    pe.wait_ge(turn_out[r % 2], r // 2)
                for j, x in enumerate(blocks):
                    n, m = x.shape[0], x.shape[1]
                    mm = nc.tensor.transpose(turn_bank(r)[0:m, j * P:j * P + n], x, ident[0:n, 0:n])
                mm.then_inc(turn_done, 1)
                at.r += 1

            def turn_wide(src, tt, chunks):
                for c in range(0, chunks, 4):
                    turn([src[:, tt, k * P:(k + 1) * P] for k in range(c, min(c + 4, chunks))])

            def turn_all(src, chunks):
                for tt in range(TT):
                    turn_wide(src, tt, chunks)

            def half_k(kc):
                return [range(0, kc // 2), range(kc // 2, kc)]

            def parts_of(ub, h, kc, width):
                ks = half_k(kc)[h]
                return [x[ub % SLOTS][:, ks[0] * width:(ks[-1] + 1) * width].rearrange("p (k c) -> p k c", k=len(ks))
                        for x in (w_hi, w_lo)]

            def three(out, x, w_, first, last, x_moves=False):
                for t, (a, b) in enumerate(((0, 0), (0, 1), (1, 0))):
                    l, r = (w_[b], x[a]) if x_moves else (x[a], w_[b])
                    mm = nc.tensor.matmul(out, l, r, start=first and t == 0, stop=last and t == 2, skip_group_check=True)
                return mm

            def unit(i, ub, vb, x, kind, kc, width, ready=None):
                if not (isinstance(i, int) and 4 * i + vb < 2):
                    pe.wait_ge(step_out[vb % 2], i * 2 + vb // 2)
                bk = step_bank(vb)
                split_at = {"tok": 0, "feat": width, "both": P}[kind]
                tok_n = width - split_at
                first = True
                for h, ks in enumerate(half_k(kc)):
                    pe.wait_ge(split_lo[ub % SLOTS], lows(i, ub, h))
                    if ready and isinstance(i, int) and 4 * i + ub == at.u:
                        ready(h)
                    wt = parts_of(ub, h, kc, width)
                    for c in range(0, split_at, P):
                        for k in ks:
                            mm = three(bk[:, c * 2:c * 2 + S], [y[:, k, :] for y in x], [y[:, k - ks[0], c:c + P] for y in wt],
                                       first, k == kc - 1, x_moves=True)
                            first = False
                    if tok_n:
                        for tt in range(TT):
                            b0 = 2 * split_at + tt * tok_n
                            for k in ks:
                                mm = three(bk[:, b0:b0 + tok_n], [y[:, k, tt * P:(tt + 1) * P] for y in x],
                                           [y[:, k - ks[0], split_at:width] for y in wt], first, k == kc - 1)
                                first = False
                    mm.then_inc(halves_used, 1)

            def project(n, x, kind, kc=DC, width=UW, ready=None):
                u0, v0 = at.u, at.v
                for i, j in unit_groups(pe, u0, n, peel=1 if ready else 0):
                    unit(i, u0 + j, v0 + j, x, kind, kc, width, ready)
                at.u += n
                at.v += n

            def latent_up(n, x, kc, heads_, width):
                rest = heads_ * (width - C_NOPE)
                for _ in range(n):
                    for h in range(2):
                        pe.wait_ge(split_lo[at.u % SLOTS], lows(0, at.u, h))
                    wt = [y[at.u % SLOTS][:, 0:kc * heads_ * width].rearrange("p (k h c) -> p k h c", k=kc, h=heads_) for y in (w_hi, w_lo)]
                    steps = [[(c % 2 * S, c) for c in (c0, c0 + 1)] for c0 in range(0, heads_, 2)]
                    per = 512 // rest
                    steps += [[(t % per * rest, (t,)) for t in range(t0, min(t0 + per, TT))] for t0 in range(0, TT, per)]
                    for outs in steps:
                        pe.wait_ge(step_out[at.v % 2], at.v // 2)
                        bk, first = step_bank(at.v), True
                        for b0, what in outs:
                            for k in range(kc):
                                if isinstance(what, int):
                                    mm = three(bk[:, b0:b0 + S], [y[:, k, :] for y in x], [y[:, k, what, 0:C_NOPE] for y in wt],
                                               first, k == kc - 1, x_moves=True)
                                else:
                                    t = what[0]
                                    mm = three(bk[:, b0:b0 + rest].rearrange("p (h d) -> p h d", h=heads_),
                                               [y[:, k, t * P:(t + 1) * P] for y in x], [y[:, k, :, C_NOPE:width] for y in wt],
                                               first, k == kc - 1)
                                first = False
                        mm.then_inc(latent_step, 1)
                        at.v += 1
                    at.u += 1
                    at.lat += len(steps)
                    pe.wait_ge(latent_step, at.lat)
                    pe.sem_inc(halves_used, 2)

            def acc_products(ub, h, tt, half, x, chunk, first, last):
                return three(acc_bank(tt, half), [y[:, chunk + h, tt * P:(tt + 1) * P] for y in x],
                             [y[ub % SLOTS][:, h * D + half * 512:h * D + (half + 1) * 512] for y in (w_hi, w_lo)],
                             first, last)

            def gather_unit(x, chunk, first):
                for h in range(2):
                    pe.wait_ge(split_lo[at.u % SLOTS], lows(0, at.u, h))
                    for tt in range(TT):
                        for half in range(2):
                            mm = acc_products(at.u, h, tt, half, x, chunk, first and h == 0, False)
                    mm.then_inc(halves_used, 1)
                at.u += 1

            def gather_last(x, chunks, first=False):
                n = len(chunks)
                for k in range(n):
                    pe.wait_ge(split_lo[(at.u + k) % SLOTS], lows(0, at.u + k, 1))
                for tt in range(TT):
                    for half in range(2):
                        for k, chunk in enumerate(chunks):
                            for h in range(2):
                                mm = acc_products(at.u + k, h, tt, half, x, chunk, first and k == 0 and h == 0, k == n - 1 and h == 1)
                        mm.then_inc(acc_ready, 1)
                at.u += n
                pe.wait_ge(acc_ready, 4 * (at.acc + 1))
                pe.sem_inc(halves_used, 2 * n)
                at.acc += 1

            def gather(n, x, ready=None):
                for q in range(n - 2):
                    if ready:
                        ready(q)
                    gather_unit(x, 2 * q, q == 0)
                if ready:
                    ready(n - 1)
                last = range(max(0, n - 2), n)
                gather_last(x, [2 * q for q in last], first=n <= 2)

            def attend(a):
                n0 = at.n

                def scores(i):
                    n = n0 + i
                    if n >= 2:
                        pe.wait_ge(soft_done if a.mask else exp_done, n - 1)
                    for c0, c1, terms in a.scores(i):
                        for t, (l, r) in enumerate(terms):
                            mm = nc.tensor.matmul(a.s_bank(i)[:, c0:c1], l, r, start=t == 0, stop=t == len(terms) - 1)
                    mm.then_inc(scores_done, 1)

                def turn_probs(i):
                    n = n0 + i
                    pe.wait_ge(exp_done, n + 1)
                    if n >= 1 and a.wide:
                        pe.wait_ge(pt_out, n)
                    elif n >= 2:
                        pe.wait_ge(pt_out, n - 1)
                    for c in range(0, a.segs(i)[-1][1], P):
                        mm = nc.tensor.transpose(a.t_bank(i)[:, c:c + P], a.bufs(n)[1][:, c:c + P], ident[:, :])
                    mm.then_inc(pt_done, 1)

                def values(i):
                    n = n0 + i
                    pe.wait_ge(pt_out, n + 1)
                    if n >= 2:
                        pe.wait_ge(head_out, n - 1)
                    for c0, c1, terms in a.pv(i):
                        for t, (b, r) in enumerate(terms):
                            mm = nc.tensor.matmul(a.o_bank(i)[:, c0:c1], a.bufs(n)[2][:, b * P:(b + 1) * P], r,
                                                  start=t == 0, stop=t == len(terms) - 1)
                    mm.then_inc(pv_done, 1)

                scores(0)
                for i in range(a.count):
                    if i + 1 < a.count:
                        scores(i + 1)
                    turn_probs(i)
                    if i >= 1:
                        values(i - 1)
                values(a.count - 1)
                at.n += a.count

            def norm_turns():
                for tt in range(TT):
                    pe.wait_ge(normed_ready, at.nrm + tt + 1)
                    turn_wide(normed, tt, DC)
                at.nrm += TT
                at.sc += 4
                pe.wait_ge(scaled_out, at.sc)

            def layer_norm_turns():
                wait_steps(pe, at.v)
                wait_turns(pe, at.r)
                for tt in range(TT):
                    for h in range(2):
                        at.ln += 1
                        pe.wait_ge(resid_ready, at.ln)
                        for k in range(4):
                            c = 4 * h + k
                            mm = nc.tensor.transpose(ln_bank(tt, h)[:, k * P:(k + 1) * P], resid[:, tt, c * P:(c + 1) * P], ident[:, :])
                        mm.then_inc(ln_turned, 1)
                done = at.ln
                return lambda h: pe.wait_ge(ln_lo, done - 1 + h)

            def output(n_units, source_ready=True):
                pe.wait_ge(head_out, at.n)
                turn_all(heads, DC)
                wait_turns(pe, at.r)
                gather(n_units, ht)

            pe.wait_ge(ident_in, 16)
            pe.wait_ge(mem_in, 16)
            turn_all(heads, DC)
            wait_turns(pe, at.r)
            project(4, ht, "feat")
            project(4, ht, "tok")
            pe.wait_ge(rows_in, 16 * n_row_loads)
            turn([stage_rows[:, c, :] for c in range(4)])
            turn([stage_rows[0:min(P, PARAMS - c * P), c, :] for c in range(4, 8)])
            pe.wait_ge(x_in, 16)
            turn_all(resid, DC)

            ready = None
            for layer in range(DEPTH):
                kind = layer % 3
                if kind == 0:
                    if layer == 0:
                        wait_turns(pe, at.r)
                    project(6, xt, "tok", ready=ready)
                    for tt in range(TT):
                        pe.wait_ge(rot_out, at.rot + 2 * tt + 2)
                        turn_wide(tok(1536), tt, DC)
                        turn([k_dup[:, tt, h, :, :].rearrange("p e d -> p (e d)") for h in range(A_KV)])
                    at.rot += 2 * TT
                    wait_turns(pe, at.r)
                    wait_steps(pe, at.v)
                    attend(swa(layer // 3))
                    output(4)
                elif kind == 1:
                    project(8, xt, "feat", ready=ready)
                    for gate in range(2):
                        for h in range(LRU_BLOCKS):
                            v, half = at.v, h // 2
                            pe.wait_ge(split_lo[at.u % SLOTS], lows(0, at.u, half))
                            pe.wait_ge(step_out[v % 2], v // 2)
                            pe.wait_ge(lru_ulo, h + 1)
                            wt = parts_of(at.u, half, DC, UW)
                            for c in range(2):
                                for k in range(2):
                                    mm = three(step_bank(v)[:, c * S:(c + 1) * S], [y[:, DC + 2 * h + k, :] for y in ht],
                                               [y[:, 2 * (h % 2) + k, c * P:(c + 1) * P] for y in wt], k == 0 and c == 0, k == 1, x_moves=True)
                            mm.then_inc(halves_used if h % 2 else gate_step, 1)
                            at.v += 1
                        at.u += 1
                    gather(4, ht, ready=lambda q: pe.wait_ge(lru_lo, q + 1))
                else:
                    project(2, xt, "tok", ready=ready)
                    project(1, xt, "tok", width=C_DOWN - 2 * UW)
                    pe.wait_ge(rot_out, at.rot + TT)
                    at.rot += TT
                    pe.wait_ge(mla_scaled, 1)
                    low = tok(C_DOWN)
                    for tt in range(TT):
                        turn([low[:, tt, c * P:(c + 1) * P] for c in range(4)])
                        turn([low[:, tt, 4 * P:5 * P], low[:, tt, 5 * P:5 * P + C_ROPE]])
                    at.sc += 4
                    pe.wait_ge(scaled_out, at.sc)
                    latent_up(4, ht, 3, 2, C_NOPE + C_ROPE)
                    latent_up(2, [y[:, 3:5, :] for y in ht], 2, 4, 2 * C_NOPE)
                    for tt in range(TT):
                        pe.wait_ge(rot_out, at.rot + tt + 1)
                        q_rope = mla_qr()
                        for h in range(0, C_HEADS, 4):
                            turn([q_rope[:, tt, h + m, :] for m in range(4)])
                    at.rot += TT
                    wait_turns(pe, at.r)
                    wait_steps(pe, at.v)
                    attend(mla())
                    output(4)
                ready = layer_norm_turns()
                project(4, xt, "feat", ready=ready)
                wait_steps(pe, at.v)
                attend(cross())
                output(4)
                ready = layer_norm_turns()
                project(2 * GLU_LAG, xt, "feat", ready=ready)
                for what, q in glu_order:
                    if what == "up":
                        project(2, xt, "feat")
                    elif q < N_GLU - 2:
                        pe.wait_ge(glu_out, layer * N_GLU + q + 1)
                        gather_unit(ht, 2 * q % HC, q == 0)
                pe.wait_ge(glu_out, (layer + 1) * N_GLU)
                gather_last(ht, [2 * q % HC for q in (N_GLU - 2, N_GLU - 1)])
                if layer < DEPTH - 1:
                    ready = layer_norm_turns()

            norm_turns()
            project(16, xt, "tok")
            ret = tok(2048)
            ret_v = tok_at(4096, 2048)
            for part_q in range(2):
                for tt in range(TT):
                    pe.wait_ge(rot_out, at.rot + 2)
                    at.rot += 2
                    turn_wide(ret[:, :, part_q * 1024:(part_q + 1) * 1024], tt, DC)
            wait_turns(pe, at.r)
            project(8, xt, "tok")

            def ret_score(h):
                if h >= 2:
                    pe.wait_ge(ret_decayed, h - 1)
                for c0, c1, kb, q0 in ((0, S, 0, 0), (S, S + P, 1, P)):
                    for k in range(2):
                        mm = nc.tensor.matmul(bank[:, STEP + h % 2, c0:c1], kt[:, 2 * h + k, kb * P:(kb + 1) * P],
                                              qt[:, 2 * h + k, q0:S], start=k == 0, stop=k == 1)
                mm.then_inc(ret_scores, 1)

            wait_steps(pe, at.v)
            ret_score(0)
            for h in range(R_HEADS):
                if h + 1 < R_HEADS:
                    ret_score(h + 1)
                pe.wait_ge(ret_decayed, h + 1)
                if h >= 2:
                    pe.wait_ge(ret_norm, TT * (h - 1))
                for tt in range(TT):
                    for kb in range(tt + 1):
                        b = tt + kb
                        mm = nc.tensor.matmul(bank[:, ACC + 2 * (h % 2) + tt, :], ret_pt[h % 2][:, b * P:(b + 1) * P],
                                              ret_v[:, kb, h * R_V:(h + 1) * R_V], start=kb == 0, stop=kb == tt)
                    mm.then_inc(ret_pv, 1)
            pe.wait_ge(ret_norm, TT * R_HEADS)
            for tt in range(TT):
                turn_wide(ret, tt, 16)
            wait_turns(pe, at.r)
            gather(8, ht)
            project(18, xt, "tok")
            dil = tok(2 * D_W)
            for part_q in range(2):
                for tt in range(TT):
                    pe.wait_ge(rot_out, at.rot + 1)
                    at.rot += 1
                    turn_wide(dil[:, :, part_q * D_W:(part_q + 1) * D_W], tt, D_W // P)
            wait_turns(pe, at.r)
            project(8, xt, "tok")
            wait_steps(pe, at.v)
            pe.wait_ge(branch_out, TT)
            attend(dilated())
            pe.wait_ge(head_out, at.n)
            turn_all(heads, 4)
            wait_turns(pe, at.r)
            gather(2, ht)
            for tt in range(TT):
                pe.wait_ge(mix_ready, tt + 1)
                turn_wide(heads, tt, DC)
            wait_turns(pe, at.r)
            gather(4, ht)
            norm_turns()
            project(RELU_LAG, xt, "feat")
            for what, q in relu_order:
                if what == "up":
                    project(1, xt, "feat")
                elif q < N_RELU - 2:
                    pe.wait_ge(relu_sq, q + 1)
                    gather_unit(ht, 2 * q % HC, q == 0)
            pe.wait_ge(relu_sq, N_RELU)
            gather_last(ht, [2 * q % HC for q in (N_RELU - 2, N_RELU - 1)])
            norm_turns()
            project(4, xt, "tok")
            pe.wait_ge(p_in, 16)
            for tt in range(TT):
                turn([p_tok[:, tt, c * P:(c + 1) * P] for c in range(2)])
            wait_turns(pe, at.r)
            gather(1, ht)

        @block.scalar
        def _(act):
            at = At()
            links = [0]

            def link(ins):
                links[0] += 1
                ins.then_inc(act_link, 1)
                act.wait_ge(act_link, links[0])

            def turn_copy(dests):
                r = at.r
                if r % 2 == 0:
                    act.wait_ge(turn_done, r + 1)
                    for dst, (c0, c1) in dests:
                        src = turn_bank(r)[0:dst.shape[0], c0:c1]
                        if len(dst.shape) == 3:
                            src = src.rearrange("p (c s) -> p c s", s=P)
                        ins = nc.scalar.copy(dst, src)
                    ins.then_inc(turn_out[0], 1)
                at.r += 1

            def turn_split(hi, lo, m):
                act.wait_ge(turn_done, at.r + 1)
                nc.scalar.copy(hi, turn_bank(at.r)[:, 0:m * P].rearrange("p (c s) -> p c s", s=P)).then_inc(turn_hi, 1)
                at.r += 1
                at.th += 1

            late = []

            def turn_scaled(dests, v, hi, lo):
                r = at.r
                if r % 2 == 0:
                    act.wait_ge(turn_done, r + 1)
                    for dst, (c0, c1), scale, bias in dests:
                        ins = nc.scalar.activation(dst, turn_bank(r)[0:dst.shape[0], c0:c1], ACT.Copy if bias is None else ACT.Identity,
                                                   **({} if scale is None else {"scale": scale}), **({} if bias is None else {"bias": bias}))
                    ins.then_inc(turn_out[0], 1)
                late.append((r, v, hi))
                at.r += 1
                if len(late) == 2:
                    for r_, v_, hi_ in late:
                        wait_turn(act, r_)
                        nc.scalar.copy(hi_, v_).then_inc(turn_hi, 1)
                        at.th += 1
                    late.clear()

            def split(i, ub, h):
                if isinstance(i, int) and 4 * i + ub >= N_UNITS:
                    return
                if h == 0:
                    act.wait_ge(w_full[ub % SLOTS], i * 16 + 16 * (ub // SLOTS + 1))
                nc.scalar.copy(half_of(w_hi, i, ub, h), half_of(ring, i, ub, h)).then_inc(split_hi, 1)

            def splits(n):
                for _ in range(n):
                    for h in range(2):
                        split(0, at.u + AHEAD, h)
                    at.u += 1

            def step_copy(dest_of, n):
                u0, v0 = at.u, at.v
                for i, j in unit_groups(act, u0, n):
                    split(i, u0 + j + AHEAD, 0)
                    if (v0 + j) % 2 == 0:
                        act.wait_ge(halves_used, i * (2 * SLOTS) + 2 * (u0 + j + 1))
                        for dst, c0, c1 in dest_of(i * SLOTS + j):
                            src = step_bank(v0 + j)[:, c0:c1]
                            if len(dst.shape) == 3:
                                src = src.rearrange("p (a b) -> p a b", a=dst.shape[1])
                            ins = nc.scalar.copy(dst, src)
                        ins.then_inc(step_out[0], 1)
                    split(i, u0 + j + AHEAD, 1)
                at.u += n
                at.v += n

            def latent_copy(dests_of, n, per):
                for q in range(n):
                    for k, dst in enumerate(dests_of(q)):
                        if k < 2:
                            split(0, at.u + AHEAD, k)
                        at.lat += 1
                        if at.v % 2 == 0:
                            act.wait_ge(latent_step, at.lat)
                            src = step_bank(at.v)
                            if len(dst.shape) == 3:
                                src = src.rearrange("p (a b) -> p a b", a=dst.shape[1])
                            elif len(dst.shape) == 4:
                                src = src[:, 0:2 * dst.shape[1] * C_ROPE].rearrange("p (t h d) -> p t h d", t=TT, h=2)
                            nc.scalar.copy(dst, src).then_inc(step_out[0], 1)
                        at.v += 1
                    at.u += 1

            def attend(a):
                n0 = at.n

                def exps(i):
                    n = n0 + i
                    act.wait_ge(soft_done, n + 1)
                    if n >= 2:
                        act.wait_ge(pt_done, n - 1)
                    st = stat[n % 2]
                    segs = a.segs(i)
                    if a.sink:
                        nc.scalar.activation(st[:, 6:8], st[:, 2:4], ACT.Exp, bias=a.sink(i))
                    for t, (c0, c1) in enumerate(segs):
                        src = a.bufs(n)[0][:, c0:c1] if a.mask else a.s_bank(i)[:, c0:c1]
                        ins = nc.scalar.activation(a.bufs(n)[1][:, c0:c1], src, ACT.Exp, bias=st[:, 2 + t:3 + t],
                                                   scale=1.0 if a.mask else a.scale, accum_out=st[:, 4 + t:5 + t])
                    ins.then_inc(exp_done, 1)

                def copy_t(i):
                    n = n0 + i
                    act.wait_ge(pt_done, n + 1)
                    if n >= 2:
                        act.wait_ge(pv_done, n - 1)
                    nc.scalar.copy(a.bufs(n)[2][:, 0:a.segs(i)[-1][1]], a.t_bank(i)).then_inc(pt_out, 1)

                for i in range(a.count):
                    exps(i)
                    if a.wide:
                        if i >= 1:
                            copy_t(i - 1)
                    elif i >= 1:
                        copy_t(i - 1)
                copy_t(a.count - 1)
                at.n += a.count

            def layer_norm_turns():
                for tt in range(TT):
                    for h in range(2):
                        at.ln += 1
                        act.wait_ge(ln_turned, at.ln)
                        nc.scalar.copy(xt[0][:, 4 * h:4 * h + 4, tt * P:(tt + 1) * P],
                                       ln_bank(tt, h).rearrange("p (c s) -> p c s", s=P)).then_inc(ln_hi, 1)

            turns = for_turns(at, turn_copy, turn_split, turn_scaled)
            for u in range(AHEAD):
                for h in range(2):
                    split(0, u, h)
            turns["mem"]()
            step_copy(lambda q: [(mem_kt[:, 2 * q:2 * q + 2, :], 0, 512)], 4)
            step_copy(lambda q: [(mem_v[:, :, q * UW:(q + 1) * UW], 0, 512)], 4)
            turns["setup"]()

            def glu_unit(i, ub, vb, qb, role, layer):
                par = qb % 2
                split(i, ub + AHEAD, 0)
                act.wait_ge(halves_used, i * (2 * SLOTS) + 2 * (ub + 1))
                first = isinstance(i, int) and layer == 0 and 2 * i + qb < 2
                if not first:
                    act.wait_ge(glu_prod, i * 2 + (layer * N_GLU + qb - 1))
                for c in range(2):
                    ch = i * 4 + (2 * qb + c + role * FFC)
                    ins = nc.scalar.activation(cwork[par][role][:, c, :], step_bank(vb)[:, c * S:(c + 1) * S], ACT.Identity,
                                               bias=params[:, bass.ds(ch + (COL["f_conv_b"] + layer * 2 * FFC), 1)],
                                               scale=params[:, bass.ds(ch + (COL["f_conv_w"] + (layer * 3 + 2) * 2 * FFC), 1)])
                ins.then_inc(conv_start, 1)
                split(i, ub + AHEAD, 1)
                if role == 1:
                    act.wait_ge(step_out[(vb - 1) % 2], i * 2 + (vb - 1) // 2 + 1)
                    nc.scalar.activation(swork[par][:, :, :], cwork[par][0][:, :, :], ACT.Silu).then_inc(glu_gate, 1)
                    if not (isinstance(i, int) and 2 * i + qb == 0):
                        glu_high(i, qb - 1, layer)

            def glu_high(i, qb, layer):
                act.wait_ge(glu_prod, i * 2 + (layer * N_GLU + qb + 1))
                if isinstance(i, int):
                    dst = ht[0][:, (4 * i + 2 * qb) % HC:(4 * i + 2 * qb) % HC + 2, :]
                else:
                    dst = ht[0][:, bass.ds(i * 4 + 2 * qb, 2), :]
                nc.scalar.copy(dst, pwork[qb % 2][:, :, :]).then_inc(glu_hi, 1)

            for layer in range(DEPTH):
                kind = layer % 3
                if kind == 0:
                    step_copy(lambda q: [(tok(1536)[:, :, q * UW:(q + 1) * UW], 0, 512)], 6)
                    turns["swa"]()
                    attend(swa(layer // 3))
                    turns["heads"]()
                    splits(4)
                elif kind == 1:
                    def conv_high(k, v):
                        wait_step(act, v)
                        nc.scalar.copy(ht[0][:, DC + 2 * k:DC + 2 * k + 2, :], lru_parts[1][:, 2 * k:2 * k + 2, :]).then_inc(lru_uhi, 1)

                    gel, u, rg, ig, a_, b_ = lru_parts
                    for q in range(8):
                        split(0, at.u + AHEAD, 0)
                        act.wait_ge(halves_used, 2 * (at.u + 1))
                        bk = step_bank(at.v)
                        if q < 4:
                            nc.scalar.activation(gel[:, 2 * q:2 * q + 2, :], bk.rearrange("p (c s) -> p c s", s=S),
                                                 ACT.Gelu_apprx_tanh).then_inc(step_out[at.v % 2], 1)
                        else:
                            for c in range(2):
                                ch = 2 * (q - 4) + c
                                ins = nc.scalar.activation(u[:, ch, :], bk[:, c * S:(c + 1) * S], ACT.Identity,
                                                           bias=col("b_conv_b", ch), scale=col("b_conv_w", 3 * DC + ch))
                            ins.then_inc(lru_act, 1)
                        split(0, at.u + AHEAD, 1)
                        if q > 4:
                            conv_high(q - 5, at.v - 1)
                        at.u += 1
                        at.v += 1
                    conv_high(3, at.v - 1)
                    for gate, (dst, bias) in enumerate(((ig, "b_b_igate"), (rg, "b_b_rgate"))):
                        for h in range(LRU_BLOCKS):
                            if h % 2 == 0:
                                act.wait_ge(gate_step, gate * 2 + h // 2 + 1)
                            else:
                                act.wait_ge(halves_used, 2 * at.u + h // 2 + 1)
                            for c in range(2):
                                ins = nc.scalar.activation(dst[:, 2 * h + c, :], step_bank(at.v)[:, c * S:(c + 1) * S],
                                                           ACT.Sigmoid, bias=col(bias, 2 * h + c))
                            ins.then_inc(step_out[at.v % 2], 1)
                            at.v += 1
                            if h % 2:
                                split(0, at.u + AHEAD, h // 2)
                        at.u += 1
                    wait_steps(act, at.v)
                    act.wait_ge(lru_dve, LRU_SP)
                    for g in range(4):
                        for ch in (2 * g, 2 * g + 1):
                            nc.scalar.activation(a_[:, ch, :], rg[:, ch, :], ACT.Exp, scale=softplus[:, 5, ch:ch + 1])
                        for ch in (2 * g, 2 * g + 1):
                            ins = nc.scalar.activation(b_[:, ch, :], rg[:, ch, :], ACT.Tanh, scale=softplus[:, 5, ch:ch + 1])
                        ins.then_inc(lru_act, 1)
                    for g in range(4):
                        act.wait_ge(lru_dve, LRU_SP + g + 1)
                        nc.scalar.activation(rg[:, 2 * g:2 * g + 2, :], b_[:, 2 * g:2 * g + 2, :], ACT.Sqrt).then_inc(lru_act, 1)
                    for g in range(4):
                        act.wait_ge(lru_pool, g + 1)
                        nc.scalar.copy(ht[0][:, 2 * g:2 * g + 2, :], ig[:, 2 * g:2 * g + 2, :]).then_inc(lru_hi, 1)
                    splits(4)
                else:
                    low = tok(C_DOWN)
                    step_copy(lambda q: [(low[:, :, q * UW:(q + 1) * UW], 0, 512)], 2)
                    step_copy(lambda q: [(low[:, :, 2 * UW:C_DOWN], 0, 2 * (C_DOWN - 2 * UW))], 1)
                    wait_steps(act, at.v)
                    for tt in range(TT):
                        for t, (c0, c1) in enumerate(((0, C_QR), (C_QR, C_QR + C_KVR))):
                            k = at.col + 2 * tt + t
                            ins = nc.scalar.activation((masked, probs)[tt][t][:, 0:c1 - c0], low[:, tt, c0:c1], ACT.Square,
                                                       accum_out=ssq[:, k:k + 1])
                    ins.then_inc(ssq_ready, 1)
                    at.col += 4
                    at.sq += 1
                    turns["mla_low"]()
                    latent_copy(lambda q: latent_q[q], 4, 2)
                    latent_copy(lambda q: latent_kv[q], 2, 4)
                    turns["mla_q"]()
                    attend(mla())
                    turns["heads"]()
                    splits(4)
                at.col += TT
                layer_norm_turns()
                step_copy(lambda q: [(qt[:, 2 * q:2 * q + 2, :], 0, 512)], 4)
                attend(cross())
                turns["heads"]()
                splits(4)
                at.col += TT
                layer_norm_turns()
                u0, v0 = at.u, at.v
                for i, j in unit_groups(act, u0, 2 * GLU_LAG, peel=1):
                    glu_unit(i, u0 + j, v0 + j, j // 2, j % 2, layer)
                at.u += 2 * GLU_LAG
                at.v += 2 * GLU_LAG
                for what, q in glu_order:
                    if what == "up":
                        for role in range(2):
                            glu_unit(0, at.u, at.v, q, role, layer)
                            at.u += 1
                            at.v += 1
                        if q == N_GLU - 1:
                            glu_high(0, q, layer)
                    else:
                        splits(1)
                at.col += TT
                if layer < DEPTH - 1:
                    layer_norm_turns()

            def squares(src_of, wait_of, n=TT):
                for tt in range(n):
                    wait_of(tt)
                    nc.scalar.activation(normed[:, tt, :], src_of(tt), ACT.Square,
                                         accum_out=ssq[:, at.col:at.col + 1]).then_inc(ssq_ready, 1)
                    at.col += 1
                    at.sq += 1

            act.wait_ge(head_out, at.n)
            act.dma_start(mask_d, w["k_mask_d"]).then_inc(tables2_in, 16)
            act.dma_start(decay, w["k_decay"]).then_inc(tables2_in, 16)
            act.wait_ge(resid_ready, 12 * DEPTH)
            squares(lambda tt: resid[:, tt, :], lambda tt: None)
            turns["norm"](lambda c: (col("g_pre_mix_2", c), None))
            act.wait_ge(angle_ready, 1)
            nc.scalar.activation(angles[:, 1, :, :], angles[:, 0, :, :], ACT.Sin)
            nc.scalar.activation(angles[:, 2, :, :], angles[:, 0, :, :], ACT.Sin, scale=0.5).then_inc(trig_ready, 1)
            ret = tok(2048)
            ret_v = tok_at(4096, 2048)
            step_copy(lambda q: [(ret[:, :, q * UW:(q + 1) * UW], 0, 512)], 8)
            step_copy(lambda q: [(ret_v[:, :, q * UW:(q + 1) * UW], 0, 512)], 8)
            turns["ret_qk"]()
            step_copy(lambda q: [(ret[:, :, q * UW:(q + 1) * UW], 0, 512)], 8)
            wait_steps(act, at.v)
            for tt in range(TT):
                ins = nc.scalar.activation(ret[:, tt, :], ret[:, tt, :], ACT.Silu)
            ins.then_inc(gate_sig, 1)
            for h in range(R_HEADS):
                for tt in range(TT):
                    if h:
                        act.wait_ge(ssq_ready, at.sq - 1)
                    act.wait_ge(ret_pv, TT * h + tt + 1)
                    nc.scalar.activation(ret_junk[tt], bank[:, ACC + 2 * (h % 2) + tt, :], ACT.Square,
                                         accum_out=ssq[:, at.col:at.col + 1]).then_inc(ssq_ready, 1)
                    at.col += 1
                    at.sq += 1
            turns["ret_out"]()
            splits(8)
            dil = tok(2 * D_W)
            dil_v = tok_at(2 * TT * D_W, D_W)
            step_copy(lambda q: [(dil[:, :, bass.ds(q * UW, UW)], 0, 512)], 12)
            step_copy(lambda q: [(dil_v[:, :, q * UW:(q + 1) * UW], 0, 512)], 6)
            turns["dil_qk"]()
            gates = tok(2 * D)
            step_copy(lambda q: [(gates[:, :, q * UW:(q + 1) * UW], 0, 512)], 8)
            attend(dilated())
            turns["dil_out"]()
            act.wait_ge(gate_in, 1)
            for tt in range(TT):
                ins = nc.scalar.activation(gates[:, tt, :], gates[:, tt, :], ACT.Sigmoid)
            ins.then_inc(gate_sig, 1)
            splits(2)
            turns["heads"]()
            splits(4)

            def post_squares():
                squares(acc_tile, lambda tt: act.wait_ge(acc_ready, 4 * at.acc + 2 * tt + 2))
                at.acc += 1

            def pre_squares(k):
                squares(lambda tt: resid[:, tt, :], lambda tt: act.wait_ge(resid_ready, 12 * DEPTH + TT * k + tt + 1))

            at.acc = 3 * DEPTH + 2
            post_squares()
            pre_squares(0)
            turns["norm"](lambda c: (col("g_pre_mlp_2", c), None))

            def relu_high(q):
                act.wait_ge(relu_prod, q + 1)
                nc.scalar.copy(ht[0][:, 2 * q % HC:2 * q % HC + 2, :], pwork[q % 2][:, :, :]).then_inc(relu_hi, 1)

            def relu_unit(q):
                split(0, at.u + AHEAD, 0)
                act.wait_ge(halves_used, 2 * (at.u + 1))
                if q >= 2:
                    act.wait_ge(relu_prod, q - 1)
                nc.scalar.activation(cwork[0][q % 2][:, :, :], step_bank(at.v).rearrange("p (c s) -> p c s", s=S),
                                     ACT.Relu).then_inc(step_out[at.v % 2], 1)
                split(0, at.u + AHEAD, 1)
                if q:
                    relu_high(q - 1)
                at.u += 1
                at.v += 1

            for q in range(RELU_LAG):
                relu_unit(q)
            for what, q in relu_order:
                if what == "up":
                    relu_unit(q)
                    if q == N_RELU - 1:
                        relu_high(q)
                else:
                    splits(1)
            post_squares()
            pre_squares(1)
            act.dma_start(p_tok, w["p_2"].rearrange("(t p) n -> p t n", p=P)).then_inc(p_in, 16)
            turns["norm"](lambda c: (col("g_pre_ple_2", c), None))
            step_copy(lambda q: [(tok(D)[:, :, q * UW:(q + 1) * UW], 0, 512)], 4)
            turns["p"]()
            splits(1)
            act.wait_ge(ple_in, 1)
            nc.scalar.activation(tok(D), tok(D), ACT.Sigmoid).then_inc(ple_sig, 1)
            for tt in range(TT):
                act.wait_ge(ple_prod, tt + 1)
                nc.scalar.activation(normed[:, tt, :], heads[:, tt, :], ACT.Square,
                                     accum_out=ssq[:, at.col:at.col + 1]).then_inc(ssq_ready, 1)
                at.col += 1

        @block.vector
        def _(dve):
            at = At()
            links = [0]
            v_ = nc.vector

            def mark(ins):
                links[0] += 1
                ins.then_inc(dve_link, 1)
                return links[0]

            def link(ins):
                dve.wait_ge(dve_link, mark(ins))

            def turn_copy(dests):
                r = at.r
                if r % 2 == 1:
                    dve.wait_ge(turn_done, r + 1)
                    for dst, (c0, c1) in dests:
                        src = turn_bank(r)[0:dst.shape[0], c0:c1]
                        if len(dst.shape) == 3:
                            src = src.rearrange("p (c s) -> p c s", s=P)
                        ins = v_.tensor_copy(dst, src)
                    ins.then_inc(turn_out[1], 1)
                at.r += 1

            def turn_split(hi, lo, m):
                at.th += 1
                dve.wait_ge(turn_hi, at.th)
                v_.tensor_tensor(lo, turn_bank(at.r)[:, 0:m * P].rearrange("p (c s) -> p c s", s=P), hi.bitcast(F32),
                                 ALU.subtract).then_inc(turn_out[at.r % 2], 1)
                at.r += 1

            late = []

            def turn_scaled(dests, v, hi, lo):
                r = at.r
                if r % 2 == 1:
                    dve.wait_ge(turn_done, r + 1)
                    for dst, (c0, c1), scale, bias in dests:
                        src = turn_bank(r)[0:dst.shape[0], c0:c1]
                        if scale is None:
                            ins = v_.tensor_copy(dst, src)
                        elif bias is None:
                            ins = v_.tensor_scalar(dst, src, scale, None, ALU.mult)
                        else:
                            ins = v_.tensor_scalar(dst, src, scale, bias, ALU.mult, ALU.add)
                    ins.then_inc(turn_out[1], 1)
                late.append((v, hi, lo))
                at.r += 1
                if len(late) == 2:
                    for x, hi_, lo_ in late:
                        at.th += 1
                        dve.wait_ge(turn_hi, at.th)
                        v_.tensor_tensor(lo_, x, hi_.bitcast(F32), ALU.subtract).then_inc(scaled_out, 1)
                    late.clear()

            def split(i, ub, h):
                if not (isinstance(i, int) and 4 * i + ub in pool_units):
                    low_part(dve, v_, i, ub, h)

            def splits(n):
                for _ in range(n):
                    for h in range(2):
                        split(0, at.u + AHEAD, h)
                    at.u += 1

            def step_copy(dest_of, n):
                u0, v0 = at.u, at.v
                for i, j in unit_groups(dve, u0, n):
                    split(i, u0 + j + AHEAD, 0)
                    if (v0 + j) % 2 == 1:
                        dve.wait_ge(halves_used, i * (2 * SLOTS) + 2 * (u0 + j + 1))
                        for dst, c0, c1 in dest_of(i * SLOTS + j):
                            src = step_bank(v0 + j)[:, c0:c1]
                            if len(dst.shape) == 3:
                                src = src.rearrange("p (a b) -> p a b", a=dst.shape[1])
                            ins = v_.tensor_copy(dst, src)
                        ins.then_inc(step_out[1], 1)
                    split(i, u0 + j + AHEAD, 1)
                at.u += n
                at.v += n

            def rotate(rows, cos, sin, dests):
                k = at.rot
                n, half = rows.shape[1], rows.shape[3]
                c = rot_c_view(k, n, half)
                s = rot_s_view(k, n, half)
                if k >= 2:
                    dve.wait_ge(rot_out, k - 1)
                link(v_.tensor_tensor(c, rows, bcast(cos, n, half), ALU.mult))
                dve.wait_ge(rot_sin, k + 1)
                ins = None
                for (a, b), outs in dests:
                    for e, op in ((0, ALU.subtract), (1, ALU.add)):
                        x, y = c[:, a:b, e, :], s[:, a:b, 1 - e, :]
                        o = outs[e]
                        if len(o.shape) == 4:
                            x = x.unsqueeze(2).to_broadcast([P, b - a, o.shape[2], half])
                            y = y.unsqueeze(2).to_broadcast([P, b - a, o.shape[2], half])
                        ins = v_.tensor_tensor(o, x, y, op)
                ins.then_inc(rot_out, 1)
                at.rot += 1

            def latent_copy(dests_of, n, per):
                for q in range(n):
                    for k, dst in enumerate(dests_of(q)):
                        if k < 2:
                            split(0, at.u + AHEAD, k)
                        at.lat += 1
                        if at.v % 2 == 1:
                            dve.wait_ge(latent_step, at.lat)
                            src = step_bank(at.v)
                            if len(dst.shape) == 3:
                                src = src.rearrange("p (a b) -> p a b", a=dst.shape[1])
                            elif len(dst.shape) == 4:
                                src = src[:, 0:2 * dst.shape[1] * C_ROPE].rearrange("p (t h d) -> p t h d", t=TT, h=2)
                            v_.tensor_copy(dst, src).then_inc(step_out[1], 1)
                        at.v += 1
                    at.u += 1

            def attend(a):
                n0 = at.n

                def soft(i):
                    n = n0 + i
                    st = stat[n % 2]
                    segs = a.segs(i)
                    ns = len(segs)
                    dve.wait_ge(scores_done, n + 1)
                    if n >= 2:
                        dve.wait_ge(exp_done, n - 1)
                    if a.mask:
                        src = a.bufs(n)[0][:, 0:segs[-1][1]]
                        link(v_.scalar_tensor_tensor(out=src, in0=a.s_bank(i), scalar=a.scale, in1=a.mask(i),
                                                     op0=ALU.mult, op1=ALU.add))
                    else:
                        src = a.s_bank(i)
                    for t, (c0, c1) in enumerate(segs):
                        ins = v_.reduce_max(st[:, t:t + 1], src[:, c0:c1], AX.X)
                        if t < ns - 1:
                            pass
                    link(ins)
                    if a.sink:
                        ins = v_.tensor_scalar(st[:, 2:2 + ns], st[:, 0:ns], a.sink(i), -1.0, ALU.max, ALU.mult)
                    else:
                        ins = v_.tensor_scalar(st[:, 2:2 + ns], st[:, 0:ns], -1.0 if a.mask else -a.scale, None, ALU.mult)
                    ins.then_inc(soft_done, 1)

                def denominators(i):
                    n = n0 + i
                    st = stat[n % 2]
                    ns = len(a.segs(i))
                    dve.wait_ge(exp_done, n + 1)
                    den = st[:, 4:4 + ns]
                    if a.sink:
                        den = st[:, 8:8 + ns]
                        link(v_.tensor_tensor(den, st[:, 4:4 + ns], st[:, 6:6 + ns], ALU.add))
                    link(v_.reciprocal(st[:, 10:10 + ns], den))

                def heads_out(i):
                    n = n0 + i
                    st = stat[n % 2]
                    dst = a.dest(i)
                    t, wd = dst.shape[1], dst.shape[2]
                    dve.wait_ge(pv_done, n + 1)
                    v_.tensor_tensor(dst, a.o_bank(i)[:, 0:t * wd].rearrange("p (t c) -> p t c", t=t),
                                     st[:, 10:10 + t].unsqueeze(2).to_broadcast([P, t, wd]), ALU.mult).then_inc(head_out, 1)

                for i in range(a.count):
                    soft(i)
                    if i >= 2:
                        heads_out(i - 2)
                    if i >= 1:
                        denominators(i - 1)
                if a.count >= 2:
                    heads_out(a.count - 2)
                denominators(a.count - 1)
                heads_out(a.count - 1)
                at.n += a.count

            def wait_acc(tt, half=1):
                dve.wait_ge(acc_ready, 4 * at.acc + 2 * tt + half + 1)
                if tt == TT - 1 and half == 1:
                    at.acc += 1

            def layer_norm(turned=True):
                n = at.nrm
                dve.wait_ge(gains_in, 32 * (n + 1))
                for tt in range(TT):
                    for half in range(2):
                        h = slice(half * 512, (half + 1) * 512)
                        wait_acc(tt, half)
                        if n == 0:
                            dve.wait_ge(x_in, 16)
                            dve.wait_ge(turn_done, 10)
                        elif tt == 0 and half == 0:
                            dve.wait_ge(ln_turned, 4 * n)
                            dve.wait_ge(resid_ready, 4 * n)
                        link(v_.scalar_tensor_tensor(out=resid[:, tt, h], in0=resid[:, tt, h], scalar=ALPHA,
                                                     in1=acc_bank(tt, half), op0=ALU.mult, op1=ALU.add))
                        link(v_.bn_stats(bn[:, tt, half, :], resid[:, tt, h]))
                    link(v_.bn_aggr(bn_mv[:, tt, :], bn[:, tt, :, :].rearrange("p a b -> p (a b)")))
                    v_.tensor_scalar(var[:, at.col:at.col + 1], bn_mv[:, tt, 1:2], LN_EPS, None, ALU.add).then_inc(var_ready, 1)
                    link(v_.scalar_tensor_tensor(out=resid[:, tt, :], in0=resid[:, tt, :], scalar=bn_mv[:, tt, 0:1], in1=gains[:, 0, :],
                                                 op0=ALU.subtract, op1=ALU.mult))
                    at.msq += 1
                    dve.wait_ge(rstd_ready, at.msq)
                    for half in range(2):
                        h = slice(half * 512, (half + 1) * 512)
                        v_.scalar_tensor_tensor(out=resid[:, tt, h], in0=resid[:, tt, h], scalar=rstd[:, at.col:at.col + 1],
                                                in1=gains[:, 1, h], op0=ALU.mult, op1=ALU.add).then_inc(resid_ready, 1)
                    at.col += 1
                at.nrm += 1
                if turned:
                    for tt in range(TT):
                        for h in range(2):
                            at.ln += 1
                            dve.wait_ge(ln_hi, at.ln)
                            c = (slice(None), slice(4 * h, 4 * h + 4), slice(tt * P, (tt + 1) * P))
                            v_.tensor_tensor(xt[1][c], ln_bank(tt, h).rearrange("p (c s) -> p c s", s=P), xt[0][c].bitcast(F32),
                                             ALU.subtract).then_inc(ln_lo, 1)

            def mean_square(width, n=1):
                at.sq += 1
                dve.wait_ge(ssq_ready, at.sq)
                v_.tensor_scalar(var[:, at.col:at.col + n], ssq[:, at.col:at.col + n], 1.0 / width, RMS_EPS,
                                 ALU.mult, ALU.add).then_inc(var_ready, 1)
                at.msq += 1
                at.col += n

            turns = for_turns(at, turn_copy, turn_split, turn_scaled)
            for u in range(AHEAD):
                for h in range(2):
                    split(0, u, h)
            turns["mem"]()
            step_copy(lambda q: [(mem_kt[:, 2 * q:2 * q + 2, :], 0, 512)], 4)
            step_copy(lambda q: [(mem_v[:, :, q * UW:(q + 1) * UW], 0, 512)], 4)
            turns["setup"]()
            dve.wait_ge(tables_in, 16 * 6)
            link(v_.tensor_copy(pos_f[:, :], pos_i[:, :]))
            for tt in range(TT):
                k = mark(v_.tensor_scalar(angles[:, 0, tt, :], freq[:, :], pos_f[:, tt:tt + 1], None, ALU.mult))
            dve.wait_ge(dve_link, k)
            link(v_.tensor_scalar(angles[:, 1, :, :], angles[:, 0, :, :], 1.0 / TWO_PI, ROUND, ALU.mult, ALU.add))
            link(v_.tensor_scalar(angles[:, 1, :, :], angles[:, 1, :, :], -ROUND, None, ALU.add))
            for c in (PI_1, PI_2, PI_3):
                link(v_.scalar_tensor_tensor(out=angles[:, 0, :, :], in0=angles[:, 1, :, :], scalar=-c, in1=angles[:, 0, :, :],
                                             op0=ALU.mult, op1=ALU.add))
            v_.tensor_scalar(angles[:, 0, :, :], angles[:, 0, :, :], 3.1415925, -3.1415925, ALU.min, ALU.max).then_inc(angle_ready, 1)

            for layer in range(DEPTH):
                kind = layer % 3
                if kind == 0:
                    qkv = tok(1536)
                    step_copy(lambda q: [(qkv[:, :, q * UW:(q + 1) * UW], 0, 512)], 6)
                    wait_steps(dve, at.v)
                    for tt in range(TT):
                        rows = in_rows(qkv[:, tt, 0:A_HEADS * A_HD], A_HEADS, A_HD // 2)
                        rotate(rows, rope_t[:, tt, 0, :], rope_t[:, tt, 1, :], [((0, A_HEADS), [rows[:, :, e, :] for e in range(2)])])
                        rows = in_rows(qkv[:, tt, A_HEADS * A_HD:], A_KV, A_HD // 2)
                        rotate(rows, rope_t[:, tt, 0, :], rope_t[:, tt, 1, :],
                               [((0, A_KV), [k_dup[:, tt, :, :, e * 32:(e + 1) * 32] for e in range(2)])])
                    turns["swa"]()
                    attend(swa(layer // 3))
                    turns["heads"]()
                    splits(4)
                elif kind == 1:
                    gel, u, rg, ig, a_, b_ = lru_parts
                    lam = params[:, COL["b_lambda"]:COL["b_lambda"] + DC]
                    sp0, sp1, sp2, sp3, sp4, sp5 = (softplus[:, i, :] for i in range(6))
                    link(v_.tensor_scalar(sp0, lam, -1.0, None, ALU.mult))
                    link(v_.tensor_tensor(sp1, sp0, lam, ALU.min))
                    v_.tensor_scalar(sp5, sp0, 0.0, None, ALU.max).then_inc(lru_dve, 1)
                    def conv_low(k):
                        dve.wait_ge(lru_uhi, k + 1)
                        c = slice(DC + 2 * k, DC + 2 * k + 2)
                        v_.tensor_tensor(ht[1][:, c, :], u[:, 2 * k:2 * k + 2, :], ht[0][:, c, :].bitcast(F32),
                                         ALU.subtract).then_inc(lru_ulo, 1)

                    def softplus_chain():
                        dve.wait_ge(lru_pool_exp, 1)
                        link(v_.tensor_scalar(sp0, sp2, 2.0, None, ALU.add))
                        link(v_.reciprocal(sp3, sp0))
                        link(v_.tensor_tensor(sp0, sp2, sp3, ALU.mult))
                        link(v_.tensor_tensor(sp1, sp0, sp0, ALU.mult))
                        link(v_.tensor_scalar(sp3, sp1, 1.0 / 17, 1.0 / 15, ALU.mult, ALU.add))
                        for k in range(13, 0, -2):
                            link(v_.tensor_tensor(sp3, sp3, sp1, ALU.mult))
                            link(v_.tensor_scalar(sp3, sp3, 1.0 / k, None, ALU.add))
                        link(v_.tensor_tensor(sp3, sp3, sp0, ALU.mult))
                        link(v_.scalar_tensor_tensor(out=sp5, in0=sp3, scalar=2.0, in1=sp5, op0=ALU.mult, op1=ALU.add))
                        v_.tensor_scalar(sp5, sp5, -LRU_C, None, ALU.mult).then_inc(lru_dve, 1)

                    for q in range(8):
                        if q == 2:
                            softplus_chain()
                        split(0, at.u + AHEAD, 0)
                        if q < 4:
                            split(0, at.u + AHEAD, 1)
                        else:
                            dve.wait_ge(lru_act, q - 3)
                            bk = step_bank(at.v)
                            for sh in range(1, LRU_TAPS):
                                for c in range(2):
                                    ch = 2 * (q - 4) + c
                                    ins = v_.scalar_tensor_tensor(out=u[:, ch, sh:S], in0=bk[:, c * S:(c + 1) * S - sh],
                                                                  scalar=col("b_conv_w", (3 - sh) * DC + ch), in1=u[:, ch, sh:S],
                                                                  op0=ALU.mult, op1=ALU.add)
                                    if sh < LRU_TAPS - 1:
                                        k = mark(ins)
                                if sh < LRU_TAPS - 1:
                                    dve.wait_ge(dve_link, k)
                            ins.then_inc(step_out[at.v % 2], 1)
                            split(0, at.u + AHEAD, 1)
                            if q > 4:
                                conv_low(q - 5)
                        at.u += 1
                        at.v += 1
                    conv_low(3)
                    splits(1)
                    wait_steps(dve, at.v + LRU_BLOCKS)
                    link(v_.tensor_tensor(ig[:, :, :], ig[:, :, :], u[:, :, :], ALU.mult))
                    splits(1)
                    at.v += 2 * LRU_BLOCKS
                    for g in range(4):
                        c = slice(2 * g, 2 * g + 2)
                        dve.wait_ge(lru_act, 4 + g + 1)
                        link(v_.tensor_tensor(u[:, c, :], a_[:, c, :], a_[:, c, :], ALU.mult))
                        link(v_.tensor_scalar(u[:, c, :], u[:, c, :], -1.0, -1.0, ALU.mult, ALU.add))
                        v_.tensor_tensor(b_[:, c, :], b_[:, c, :], u[:, c, :], ALU.mult).then_inc(lru_dve, 1)

                    def gated_low(g):
                        dve.wait_ge(lru_hi, g + 1)
                        c = slice(2 * g, 2 * g + 2)
                        v_.tensor_tensor(ht[1][:, c, :], ig[:, c, :], ht[0][:, c, :].bitcast(F32), ALU.subtract).then_inc(lru_lo, 1)

                    for g in range(4):
                        c = slice(2 * g, 2 * g + 2)
                        dve.wait_ge(lru_act, 8 + g + 1)
                        link(v_.tensor_tensor(b_[:, c, :], rg[:, c, :], ig[:, c, :], ALU.mult))
                        for ch in (2 * g, 2 * g + 1):
                            v_.tensor_tensor_scan(u[:, ch, :], a_[:, ch, :], b_[:, ch, :], 0.0, ALU.mult, ALU.add).then_inc(lru_dve, 1)
                        if g >= 1:
                            gated_low(g - 1)
                    gated_low(3)
                    splits(4)
                else:
                    low = tok(C_DOWN)
                    step_copy(lambda q: [(low[:, :, q * UW:(q + 1) * UW], 0, 512)], 2)
                    step_copy(lambda q: [(low[:, :, 2 * UW:C_DOWN], 0, 2 * (C_DOWN - 2 * UW))], 1)
                    wait_steps(dve, at.v)
                    for tt in range(TT):
                        rows = low[:, tt, C_QR + C_KVR:C_DOWN].rearrange("p (h e d) -> p h e d", e=2, d=C_ROPE // 2)
                        rotate(rows, rope_t[:, tt, 0, :], rope_t[:, tt, 1, :], [((0, 1), [rows[:, :, e, :] for e in range(2)])])
                    at.sq += 1
                    dve.wait_ge(ssq_ready, at.sq)
                    for t, width in enumerate((C_QR, C_KVR)):
                        ins = v_.tensor_scalar(var[:, at.col + t:at.col + 4:2], ssq[:, at.col + t:at.col + 4:2], 1.0 / width, RMS_EPS,
                                               ALU.mult, ALU.add)
                    ins.then_inc(var_ready, 1)
                    at.msq += 1
                    dve.wait_ge(rstd_ready, at.msq)
                    for tt in range(TT):
                        for t, (c0, c1) in enumerate(((0, C_QR), (C_QR, C_QR + C_KVR))):
                            k = at.col + 2 * tt + t
                            ins = v_.tensor_scalar(low[:, tt, c0:c1], low[:, tt, c0:c1], rstd[:, k:k + 1], None, ALU.mult)
                    ins.then_inc(mla_scaled, 1)
                    at.col += 4
                    turns["mla_low"]()
                    latent_copy(lambda q: latent_q[q], 4, 2)
                    wait_steps(dve, at.v)
                    for tt in range(TT):
                        rows = mla_qr()[:, tt, :, :].rearrange("p h (e d) -> p h e d", e=2)
                        rotate(rows, rope_t[:, tt, 0, :], rope_t[:, tt, 1, :], [((0, C_HEADS), [rows[:, :, e, :] for e in range(2)])])
                    latent_copy(lambda q: latent_kv[q], 2, 4)
                    turns["mla_q"]()
                    attend(mla())
                    turns["heads"]()
                    splits(4)
                layer_norm()
                step_copy(lambda q: [(qt[:, 2 * q:2 * q + 2, :], 0, 512)], 4)
                attend(cross())
                turns["heads"]()
                splits(4)
                layer_norm()
                def glu_unit(i, ub, vb, qb, role):
                    par = qb % 2
                    split(i, ub + AHEAD, 0)
                    done = i * SLOTS + (layer * FFC + 2 * qb + role + 1)
                    dve.wait_ge(conv_start, done)
                    bk = step_bank(vb)
                    for sh in (1, 2):
                        for c in range(2):
                            ch = i * 4 + (2 * qb + c + role * FFC)
                            dst = cwork[par][role][:, c, sh:S]
                            if sh == 2 and c == 0:
                                dve.wait_ge(conv_tap, done)
                            ins = v_.scalar_tensor_tensor(out=dst, in0=bk[:, c * S:(c + 1) * S - sh],
                                                          scalar=params[:, bass.ds(ch + (COL["f_conv_w"] + (layer * 3 + 2 - sh) * 2 * FFC), 1)],
                                                          in1=dst, op0=ALU.mult, op1=ALU.add)
                        ins.then_inc(conv_tap if sh == 1 else step_out[vb % 2], 1)
                    split(i, ub + AHEAD, 1)

                u0, v0 = at.u, at.v
                for i, j in unit_groups(dve, u0, 2 * GLU_LAG, peel=1):
                    glu_unit(i, u0 + j, v0 + j, j // 2, j % 2)
                at.u += 2 * GLU_LAG
                at.v += 2 * GLU_LAG
                for what, q in glu_order:
                    if what == "up":
                        for role in range(2):
                            glu_unit(0, at.u, at.v, q, role)
                            at.u += 1
                            at.v += 1
                    else:
                        splits(1)
                layer_norm(turned=layer < DEPTH - 1)

            def pre_norm():
                for tt in range(TT):
                    mean_square(D)
                for tt in range(TT):
                    k = at.col - TT + tt
                    dve.wait_ge(rstd_ready, at.msq - TT + tt + 1)
                    v_.tensor_scalar(normed[:, tt, :], resid[:, tt, :], rstd[:, k:k + 1], None, ALU.mult).then_inc(normed_ready, 1)

            def post_norm(gain, src_of, acc=False):
                for tt in range(TT):
                    mean_square(D)
                for tt in range(TT):
                    k = at.col - TT + tt
                    dve.wait_ge(rstd_ready, at.msq - TT + tt + 1)
                    if acc:
                        wait_acc(tt)
                    link(v_.scalar_tensor_tensor(out=normed[:, tt, :], in0=src_of(tt), scalar=rstd[:, k:k + 1], in1=gain,
                                                 op0=ALU.mult, op1=ALU.mult))
                    v_.tensor_tensor(resid[:, tt, :], resid[:, tt, :], normed[:, tt, :], ALU.add).then_inc(resid_ready, 1)

            pre_norm()
            turns["norm"](lambda c: (col("g_pre_mix_2", c), None))
            dve.wait_ge(trig_ready, 1)
            link(v_.tensor_tensor(angles[:, 2, :, :], angles[:, 2, :, :], angles[:, 2, :, :], ALU.mult))
            v_.tensor_scalar(angles[:, 2, :, :], angles[:, 2, :, :], -2.0, 1.0, ALU.mult, ALU.add).then_inc(trig_ready, 1)
            dve.wait_ge(trig_ready, 2)
            ret = tok(2048)
            ret_v = tok_at(4096, 2048)
            step_copy(lambda q: [(ret[:, :, q * UW:(q + 1) * UW], 0, 512)], 8)
            step_copy(lambda q: [(ret_v[:, :, q * UW:(q + 1) * UW], 0, 512)], 8)
            wait_steps(dve, at.v)
            half = R_QK // 2
            for pq in range(2):
                for tt in range(TT):
                    for hh in range(0, R_HEADS, 2):
                        c = pq * 1024 + hh * R_QK
                        rows = ret[:, tt, c:c + 2 * R_QK].rearrange("p (h e d) -> p h e d", e=2, d=half)
                        rotate(rows, angles[:, 2, tt, 0:half], angles[:, 1, tt, 0:half], [((0, 2), [rows[:, :, e, :] for e in range(2)])])
            turns["ret_qk"]()
            step_copy(lambda q: [(ret[:, :, q * UW:(q + 1) * UW], 0, 512)], 8)
            dve.wait_ge(tables2_in, 32)
            for h in range(R_HEADS):
                def decayed(h):
                    dve.wait_ge(ret_scores, h + 1)
                    if h >= 2:
                        dve.wait_ge(ret_pv, TT * (h - 1))
                    v_.tensor_tensor(ret_pt[h % 2][:, 0:3 * P], bank[:, STEP + h % 2, 0:3 * P], decay[:, h, :], ALU.mult).then_inc(ret_decayed, 1)
                if h == 0:
                    decayed(0)
                if h + 1 < R_HEADS:
                    decayed(h + 1)
                for tt in range(TT):
                    mean_square(R_V)
                if h == 0:
                    dve.wait_ge(gate_sig, 1)
                for tt in range(TT):
                    k = at.col - TT + tt
                    dve.wait_ge(rstd_ready, at.msq - TT + tt + 1)
                    g = ret[:, tt, h * R_V:(h + 1) * R_V]
                    v_.scalar_tensor_tensor(out=g, in0=bank[:, ACC + 2 * (h % 2) + tt, :], scalar=rstd[:, k:k + 1], in1=g,
                                            op0=ALU.mult, op1=ALU.mult).then_inc(ret_norm, 1)
            turns["ret_out"]()
            splits(8)
            for tt in range(TT):
                wait_acc(tt)
                v_.tensor_copy(mem_v[:, tt, :], acc_tile(tt)).then_inc(branch_out, 1)
            dil = tok(2 * D_W)
            dil_v = tok_at(2 * TT * D_W, D_W)
            step_copy(lambda q: [(dil[:, :, bass.ds(q * UW, UW)], 0, 512)], 12)
            step_copy(lambda q: [(dil_v[:, :, q * UW:(q + 1) * UW], 0, 512)], 6)
            wait_steps(dve, at.v)
            rh = D_ROT // 2
            for pq in range(2):
                for tt in range(TT):
                    rows = dil[:, tt, pq * D_W:(pq + 1) * D_W].rearrange("p (h d) -> p h d", d=D_HD)[:, :, 0:D_ROT].rearrange("p h (e d) -> p h e d", e=2)
                    rotate(rows, angles[:, 2, tt, half:NF], angles[:, 1, tt, half:NF], [((0, D_W // D_HD), [rows[:, :, e, :] for e in range(2)])])
            turns["dil_qk"]()
            gates = tok(2 * D)
            step_copy(lambda q: [(gates[:, :, q * UW:(q + 1) * UW], 0, 512)], 8)
            wait_steps(dve, at.v)
            gb = 3 * DEPTH
            dve.wait_ge(gains_in, 32 * (gb + 1))
            for tt in range(TT):
                g = gates[:, tt, :]
                ins = v_.tensor_tensor(g, g, gains[:, :, :].rearrange("p a n -> p (a n)"), ALU.add)
            ins.then_inc(gate_in, 1)
            attend(dilated())
            turns["dil_out"]()
            splits(2)
            dve.wait_ge(gate_sig, 2)
            for tt in range(TT):
                wait_acc(tt)
                link(v_.tensor_tensor(mem_v[:, tt, :], mem_v[:, tt, :], gates[:, tt, 0:D], ALU.mult))
                link(v_.tensor_tensor(heads[:, tt, :], acc_tile(tt), gates[:, tt, D:2 * D], ALU.mult))
                v_.tensor_tensor(heads[:, tt, :], heads[:, tt, :], mem_v[:, tt, :], ALU.add).then_inc(mix_ready, 1)
            turns["heads"]()
            splits(4)
            gp = gb + 1
            dve.wait_ge(gains_in, 32 * (gp + 1))
            post_norm(gains[:, 0, :], acc_tile, True)
            pre_norm()
            turns["norm"](lambda c: (col("g_pre_mlp_2", c), None))

            def relu_unit(q):
                split(0, at.u + AHEAD, 0)
                src = cwork[0][q % 2][:, :, :]
                dve.wait_ge(step_out[at.v % 2], at.v // 2 + 1)
                if q >= 2:
                    dve.wait_ge(relu_sq, q - 1)
                v_.tensor_tensor(pwork[q % 2][:, :, :], src, src, ALU.mult).then_inc(relu_prod, 1)
                split(0, at.u + AHEAD, 1)
                at.u += 1
                at.v += 1

            for q in range(RELU_LAG):
                relu_unit(q)
            for what, q in relu_order:
                if what == "up":
                    relu_unit(q)
                else:
                    splits(1)
            post_norm(gains[:, 1, :], acc_tile, True)
            pre_norm()
            turns["norm"](lambda c: (col("g_pre_ple_2", c), None))
            step_copy(lambda q: [(tok(D)[:, :, q * UW:(q + 1) * UW], 0, 512)], 4)
            turns["p"]()
            wait_steps(dve, at.v)
            ge = gb + 2
            dve.wait_ge(gains_in, 32 * (ge + 1))
            for tt in range(TT):
                ins = v_.tensor_tensor(tok(D)[:, tt, :], tok(D)[:, tt, :], gains[:, 0, :], ALU.add)
            ins.then_inc(ple_in, 1)
            splits(1)
            dve.wait_ge(ple_sig, 1)
            for tt in range(TT):
                wait_acc(tt)
                v_.tensor_tensor(heads[:, tt, :], acc_tile(tt), tok(D)[:, tt, :], ALU.mult).then_inc(ple_prod, 1)
            post_norm(gains[:, 1, :], lambda tt: heads[:, tt, :])

        @block.gpsimd
        def _(pool):
            at = At()
            links = [0]
            g_ = nc.gpsimd

            def link(ins):
                links[0] += 1
                ins.then_inc(pool_link, 1)
                pool.wait_ge(pool_link, links[0])

            def powers(n=1):
                pool.wait_ge(var_ready, at.msq + 1)
                g_.tensor_tensor(rstd[:, at.col:at.col + n], var[:, at.col:at.col + n], minus_half[:, 0:n], ALU.pow).then_inc(rstd_ready, 1)
                at.msq += 1
                at.col += n

            def layer_norm():
                for tt in range(TT):
                    powers()
                    if tt == 0:
                        for h in range(2):
                            low_part(pool, g_, 0, behind_norm[at.nrm] + 1, h)
                pool.wait_ge(resid_ready, 4 * (at.nrm + 1))
                pool.sem_inc(gains_used, 1)
                at.nrm += 1

            def rotate(rows, sin):
                k = at.rot
                n, half = rows.shape[1], rows.shape[3]
                if k >= 2:
                    pool.wait_ge(rot_out, k - 1)
                g_.tensor_tensor(rot_s_view(k, n, half), rows, bcast(sin, n, half), ALU.mult).then_inc(rot_sin, 1)
                at.rot += 1

            link(g_.memset(minus_half[:, :], -0.5))
            at.v += 8
            pool.wait_ge(tables_in, 16 * 6)
            for layer in range(DEPTH):
                kind = layer % 3
                if kind == 0:
                    at.v += 6
                    wait_steps(pool, at.v)
                    for tt in range(TT):
                        qkv = tok(1536)
                        rotate(in_rows(qkv[:, tt, 0:A_HEADS * A_HD], A_HEADS, A_HD // 2), rope_t[:, tt, 1, :])
                        rotate(in_rows(qkv[:, tt, A_HEADS * A_HD:], A_KV, A_HD // 2), rope_t[:, tt, 1, :])
                elif kind == 1:
                    pool.wait_ge(lru_dve, 1)
                    link(g_.memset(softplus[:, 4, :], float(np.e)))
                    g_.tensor_tensor(softplus[:, 2, :], softplus[:, 4, :], softplus[:, 1, :], ALU.pow).then_inc(lru_pool_exp, 1)
                    at.v += 8 + 2 * LRU_BLOCKS
                    gel, u, rg, ig, a_, b_ = lru_parts
                    for g in range(4):
                        pool.wait_ge(lru_dve, LRU_SP + 4 + 2 * g + 2)
                        c = slice(2 * g, 2 * g + 2)
                        g_.tensor_tensor(ig[:, c, :], u[:, c, :], gel[:, c, :], ALU.mult).then_inc(lru_pool, 1)
                else:
                    at.v += 3
                    wait_steps(pool, at.v)
                    low = tok(C_DOWN)
                    for tt in range(TT):
                        rotate(low[:, tt, C_QR + C_KVR:C_DOWN].rearrange("p (h e d) -> p h e d", e=2, d=C_ROPE // 2), rope_t[:, tt, 1, :])
                    powers(4)
                    at.v += 8
                    wait_steps(pool, at.v)
                    for tt in range(TT):
                        rotate(mla_qr()[:, tt, :, :].rearrange("p h (e d) -> p h e d", e=2), rope_t[:, tt, 1, :])
                    at.v += 8
                layer_norm()
                at.v += 4
                layer_norm()
                def glu_product(i, vb, qb):
                    par = qb % 2
                    pool.wait_ge(glu_gate, i * 2 + (layer * N_GLU + qb + 1))
                    pool.wait_ge(step_out[vb % 2], i * 2 + vb // 2 + 1)
                    if not (isinstance(i, int) and 2 * i + qb < 2 and layer == 0):
                        pool.wait_ge(glu_out, i * 2 + (layer * N_GLU + qb - 1))
                    g_.tensor_tensor(pwork[par][:, :, :], swork[par][:, :, :], cwork[par][1][:, :, :], ALU.mult).then_inc(glu_prod, 1)
                    if not (isinstance(i, int) and 2 * i + qb == 0):
                        glu_low(i, qb - 1)

                def glu_low(i, qb):
                    pool.wait_ge(glu_hi, i * 2 + (layer * N_GLU + qb + 1))
                    if isinstance(i, int):
                        c = (4 * i + 2 * qb) % HC
                        hi, lo = (x[:, c:c + 2, :] for x in ht)
                    else:
                        hi, lo = (x[:, bass.ds(i * 4 + 2 * qb, 2), :] for x in ht)
                    g_.tensor_tensor(lo, pwork[qb % 2][:, :, :], hi.bitcast(F32), ALU.subtract).then_inc(glu_out, 1)

                v0 = at.v
                for i, j in unit_groups(pool, SLOTS, 2 * GLU_LAG, peel=1):
                    if j % 2 == 1:
                        glu_product(i, v0 + j, j // 2)
                for q in range(GLU_LAG, N_GLU):
                    glu_product(0, v0 + 2 * q + 1, q)
                glu_low(0, N_GLU - 1)
                at.v += FFC
                layer_norm()
            for tt in range(TT):
                powers()
            pool.wait_ge(trig_ready, 2)
            at.v += 16
            wait_steps(pool, at.v)
            ret = tok(2048)
            half = R_QK // 2
            for pq in range(2):
                for tt in range(TT):
                    for hh in range(0, R_HEADS, 2):
                        c = pq * 1024 + hh * R_QK
                        rotate(ret[:, tt, c:c + 2 * R_QK].rearrange("p (h e d) -> p h e d", e=2, d=half), angles[:, 1, tt, 0:half])
            for h in range(R_HEADS):
                for tt in range(TT):
                    powers()
            at.v += 8 + 18
            wait_steps(pool, at.v)
            dil = tok(2 * D_W)
            for pq in range(2):
                for tt in range(TT):
                    rows = dil[:, tt, pq * D_W:(pq + 1) * D_W].rearrange("p (h d) -> p h d", d=D_HD)[:, :, 0:D_ROT].rearrange("p h (e d) -> p h e d", e=2)
                    rotate(rows, angles[:, 1, tt, half:NF])
            pool.wait_ge(gate_in, 1)
            pool.sem_inc(gains_used, 1)
            for k in range(5):
                for tt in range(TT):
                    powers()
                if k == 1:
                    for q in range(N_RELU):
                        pool.wait_ge(relu_hi, q + 1)
                        hi, lo = (x[:, 2 * q % HC:2 * q % HC + 2, :] for x in ht)
                        g_.tensor_tensor(lo, pwork[q % 2][:, :, :], hi.bitcast(F32), ALU.subtract).then_inc(relu_sq, 1)
                if k == 2:
                    pool.wait_ge(resid_ready, 12 * DEPTH + TT * 2)
                    pool.sem_inc(gains_used, 1)


def kernel(**inputs):
    import concourse.bacc as bacc
    from concourse.bass_utils import run_bass_kernel_spmd as run

    nc = bacc.Bacc("TRN2", target_bir_lowering=False, num_devices=1, dynamic_dma_scratch_size=1024)
    arrays, args = {}, {}
    for name, value in {**inputs, **shape_constants()}.items():
        a = np.ascontiguousarray(value)
        a = a.reshape(LAYOUT[name]) if name in LAYOUT else a
        arrays[f"in_{name}"] = a
        args[name] = nc.dram_tensor(f"in_{name}", a.shape, mybir.dt.from_np(a.dtype), kind="ExternalInput").ap()
    out = nc.dram_tensor("out", (S, D), F32, kind="ExternalOutput").ap()
    build(nc, args, out)
    r = run(nc, [arrays], core_ids=[0])
    return r.results[0]["out"].reshape(1, S, D)
```
